# Optimizing a Trainium2 kernel written in Bass

```python
import math
import jax, jax.numpy as jnp
from jax import lax
import numpy as np

D_MODEL = 1024
BATCH = 1
SEQ = 256
DEPTH = 2

NSA_HEADS = 8
NSA_KV_GROUPS = 2
NSA_HPG = NSA_HEADS // NSA_KV_GROUPS
NSA_HEAD_DIM = 64
CMP_LEN = 32
CMP_STRIDE = 16
SLC_BLOCK = 64
N_SELECT = 16
WINDOW = 512
Q_BLOCK = 128
FORCE_SCORE = 1.0e4
RET_HEADS = 8
RET_QK_DIM = 64
RET_V_DIM = 128
RET_CHUNK = 128
ROPE_BASE = 10000.0
REL_BUCKETS = 32
REL_MAX_EXACT = 16
REL_MAX_DIST = 2048
N_EXPERTS = 16
N_GROUPS = 4
EXPERTS_PER_GROUP = N_EXPERTS // N_GROUPS
TOP_K = 2
D_EXPERT = 512
MOE_BLOCK = 128
DN_ALPHA = (2 * DEPTH) ** 0.25
DN_BETA = (8 * DEPTH) ** -0.25
LN_EPS = 1e-5
GN_EPS = 1e-5
NEG_INF = -1e30

W_NSA_Q = NSA_HEADS * NSA_HEAD_DIM
W_NSA_KV = NSA_KV_GROUPS * NSA_HEAD_DIM
W_NSA_GATE = NSA_HEADS * 3
W_RET_QK = RET_HEADS * RET_QK_DIM
W_RET_V = RET_HEADS * RET_V_DIM
IN_WIDTHS = (W_NSA_Q, W_NSA_KV, W_NSA_KV, W_NSA_KV, W_NSA_KV, W_NSA_KV, W_NSA_KV, W_NSA_GATE,
             W_RET_QK, W_RET_QK, W_RET_V, W_RET_V, D_MODEL, D_MODEL)
D_IN = sum(IN_WIDTHS)

kernel_name = 'nsa_retention_gated_moe_deepnorm'

def layer_norm(x, g, b):
    xf = x.astype(jnp.float32)
    mu = jnp.mean(xf, axis=-1, keepdims=True)
    var = jnp.mean(jnp.square(xf - mu), axis=-1, keepdims=True)
    return ((xf - mu) * lax.rsqrt(var + LN_EPS) * g + b).astype(x.dtype)

def t5_bucket(rel):
    n = jnp.maximum(rel, 0)
    nf = jnp.maximum(n, 1).astype(jnp.float32)
    large = REL_MAX_EXACT + (jnp.log(nf / REL_MAX_EXACT) / math.log(REL_MAX_DIST / REL_MAX_EXACT)
                             * (REL_BUCKETS - REL_MAX_EXACT)).astype(jnp.int32)
    large = jnp.minimum(large, REL_BUCKETS - 1)
    return jnp.where(n < REL_MAX_EXACT, n, large)

def masked_softmax(s, mask):
    s = jnp.where(mask, s, NEG_INF)
    s = s - jnp.max(s, axis=-1, keepdims=True)
    p = jnp.exp(s) * mask
    return p / jnp.maximum(jnp.sum(p, axis=-1, keepdims=True), 1e-30)

def nsa_compress(kv, pos, w1, w2):
    b, s, g, d = kv.shape
    nc = (s - CMP_LEN) // CMP_STRIDE + 1
    idx = (jnp.arange(nc) * CMP_STRIDE)[:, None] + jnp.arange(CMP_LEN)[None, :]
    blocks = kv[:, idx] + pos[None, None, :, None, :]
    flat = blocks.transpose(0, 3, 1, 2, 4).reshape(b, g, nc, CMP_LEN * d)
    return jax.nn.gelu(flat @ w1) @ w2

def nsa_attention(q, k_cmp, v_cmp, k_slc, v_slc, k_win, v_win, gate_logits,
                  cmp_pos, cmp_w1, cmp_w2, rel_bias):
    b, s, h, d = q.shape
    g, r = NSA_KV_GROUPS, NSA_HPG
    scale = d ** -0.5
    qg = q.reshape(b, s, g, r, d).transpose(0, 2, 3, 1, 4)
    gates = jax.nn.sigmoid(gate_logits.astype(jnp.float32)).reshape(b, s, g, r, 3).transpose(0, 2, 3, 1, 4)
    kc = nsa_compress(k_cmp, cmp_pos[0], cmp_w1[0], cmp_w2[0])
    vc = nsa_compress(v_cmp, cmp_pos[1], cmp_w1[1], cmp_w2[1])
    nc = kc.shape[2]
    c_start = jnp.arange(nc) * CMP_STRIDE
    cmp_end = c_start + CMP_LEN - 1
    ns = s // SLC_BLOCK
    n_sel = min(N_SELECT, ns)
    ks_blk = k_slc.transpose(0, 2, 1, 3).reshape(b, g, ns, SLC_BLOCK, d)
    vs_blk = v_slc.transpose(0, 2, 1, 3).reshape(b, g, ns, SLC_BLOCK, d)
    s_start = jnp.arange(ns) * SLC_BLOCK
    cover = jnp.maximum(jnp.minimum(c_start[:, None] + CMP_LEN, s_start[None, :] + SLC_BLOCK)
                        - jnp.maximum(c_start[:, None], s_start[None, :]), 0).astype(jnp.float32) / CMP_LEN
    kw = jnp.pad(k_win.transpose(0, 2, 1, 3), ((0, 0), (0, 0), (WINDOW, 0), (0, 0)))
    vw = jnp.pad(v_win.transpose(0, 2, 1, 3), ((0, 0), (0, 0), (WINDOW, 0), (0, 0)))
    bias_g = rel_bias.reshape(REL_BUCKETS, g, r)
    b_ix = jnp.arange(b)[:, None, None, None]
    g_ix = jnp.arange(g)[None, :, None, None]
    blk_ids = jnp.arange(ns)

    def head_bias(bucket):
        return rel_bias[bucket].transpose(2, 0, 1).reshape(g, r, *bucket.shape)

    def query_block(qi):
        q0 = qi * Q_BLOCK
        t = q0 + jnp.arange(Q_BLOCK)
        qb = lax.dynamic_slice_in_dim(qg, q0, Q_BLOCK, axis=3)
        gb = lax.dynamic_slice_in_dim(gates, q0, Q_BLOCK, axis=3)
        s_c = jnp.einsum('bgrqd,bgkd->bgrqk', qb, kc).astype(jnp.float32) * scale \
            + head_bias(t5_bucket(t[:, None] - cmp_end[None, :]))
        p_c = masked_softmax(s_c, cmp_end[None, :] <= t[:, None])
        o_c = jnp.einsum('bgrqk,bgkd->bgrqd', p_c.astype(vc.dtype), vc)
        imp = jnp.einsum('bgrqk,kj->bgqj', p_c, cover)
        cur = (t // SLC_BLOCK)[:, None]
        eligible = blk_ids[None, :] <= cur
        forced = (blk_ids[None, :] == 0) | (blk_ids[None, :] == cur) | (blk_ids[None, :] == cur - 1)
        score = jnp.where(eligible, imp + jnp.where(forced, FORCE_SCORE, 0.0), -1.0)
        top_s, sel = lax.top_k(score, n_sel)
        ks = ks_blk[b_ix, g_ix, sel].reshape(b, g, Q_BLOCK, n_sel * SLC_BLOCK, d)
        vs = vs_blk[b_ix, g_ix, sel].reshape(b, g, Q_BLOCK, n_sel * SLC_BLOCK, d)
        kpos = (sel[..., None] * SLC_BLOCK + jnp.arange(SLC_BLOCK)).reshape(b, g, Q_BLOCK, n_sel * SLC_BLOCK)
        valid = jnp.broadcast_to((top_s >= 0.0)[..., None], sel.shape + (SLC_BLOCK,)).reshape(kpos.shape)
        rel_s = t[None, None, :, None] - kpos
        mask_s = valid & (rel_s >= 0)
        bias_s = jnp.moveaxis(bias_g[t5_bucket(rel_s), g_ix], -1, 2)
        s_s = jnp.einsum('bgrqd,bgqkd->bgrqk', qb, ks).astype(jnp.float32) * scale + bias_s
        p_s = masked_softmax(s_s, mask_s[:, :, None])
        o_s = jnp.einsum('bgrqk,bgqkd->bgrqd', p_s.astype(vs.dtype), vs)
        kwb = lax.dynamic_slice_in_dim(kw, q0, Q_BLOCK + WINDOW, axis=2)
        vwb = lax.dynamic_slice_in_dim(vw, q0, Q_BLOCK + WINDOW, axis=2)
        kpos_w = q0 - WINDOW + jnp.arange(Q_BLOCK + WINDOW)
        rel_w = t[:, None] - kpos_w[None, :]
        mask_w = (kpos_w[None, :] >= 0) & (rel_w >= 0) & (rel_w < WINDOW)
        s_w = jnp.einsum('bgrqd,bgkd->bgrqk', qb, kwb).astype(jnp.float32) * scale + head_bias(t5_bucket(rel_w))
        p_w = masked_softmax(s_w, mask_w)
        o_w = jnp.einsum('bgrqk,bgkd->bgrqd', p_w.astype(vwb.dtype), vwb)
        o = gb[..., 0:1] * o_c + gb[..., 1:2] * o_s + gb[..., 2:3] * o_w
        return o.astype(q.dtype).transpose(0, 3, 1, 2, 4).reshape(b, Q_BLOCK, h * d)

    out = lax.map(query_block, jnp.arange(s // Q_BLOCK))
    return out.transpose(1, 0, 2, 3).reshape(b, s, h * d)

def rotary(x):
    s, dk = x.shape[1], x.shape[-1]
    half = dk // 2
    inv = ROPE_BASE ** (-jnp.arange(half, dtype=jnp.float32) * 2.0 / dk)
    ang = jnp.arange(s, dtype=jnp.float32)[:, None] * inv[None, :]
    cos = jnp.cos(ang)[None, :, None, :]
    sin = jnp.sin(ang)[None, :, None, :]
    x1, x2 = x[..., :half], x[..., half:]
    return jnp.concatenate([x1 * cos - x2 * sin, x1 * sin + x2 * cos], axis=-1)

def retention(q, k, v, gate):
    b, s, h, dk = q.shape
    dv = v.shape[-1]
    c = RET_CHUNK
    n = s // c

    def chunks(a):
        return a.reshape(b, n, c, h, -1).transpose(0, 3, 1, 2, 4)

    qc = chunks(rotary(q.astype(jnp.float32)))
    kc = chunks(rotary(k.astype(jnp.float32)) * dk ** -0.5)
    vc = chunks(v.astype(jnp.float32))
    lg = jnp.log(1.0 - 2.0 ** (-5.0 - jnp.arange(h, dtype=jnp.float32)))
    i = jnp.arange(c, dtype=jnp.float32)
    diff = i[:, None] - i[None, :]
    dmat = jnp.where(diff >= 0, jnp.exp(jnp.maximum(diff, 0.0)[None] * lg[:, None, None]), 0.0)
    intra = jnp.einsum('bhncj,bhnje->bhnce',
                       jnp.einsum('bhncd,bhnjd->bhncj', qc, kc) * dmat[None, :, None], vc)
    k_dec = kc * jnp.exp((c - 1.0 - i)[None, :] * lg[:, None])[None, :, None, :, None]
    kv = jnp.einsum('bhncd,bhnce->bhnde', k_dec, vc)
    chunk_decay = jnp.exp(c * lg)[None, :, None, None]

    def step(state, kv_n):
        return chunk_decay * state + kv_n, state

    _, s_prev = lax.scan(step, jnp.zeros((b, h, dk, dv), jnp.float32), jnp.moveaxis(kv, 2, 0))
    s_prev = jnp.moveaxis(s_prev, 0, 2)
    q_dec = qc * jnp.exp((i + 1.0)[None, :] * lg[:, None])[None, :, None, :, None]
    y = intra + jnp.einsum('bhncd,bhnde->bhnce', q_dec, s_prev)
    y = y.transpose(0, 2, 3, 1, 4).reshape(b, s, h, dv)
    mu = jnp.mean(y, axis=-1, keepdims=True)
    var = jnp.mean(jnp.square(y - mu), axis=-1, keepdims=True)
    y = ((y - mu) * lax.rsqrt(var + GN_EPS)).reshape(b, s, h * dv)
    return (jax.nn.silu(gate.astype(jnp.float32)) * y).astype(v.dtype)

def moe_ffn(h, w_router, router_bias, w_gate, w_up, w_down):
    b, s, d = h.shape
    t = b * s
    hf = h.reshape(t, d)
    probs = jax.nn.softmax((hf @ w_router).astype(jnp.float32), axis=-1)
    sel = (probs + router_bias.astype(jnp.float32)).reshape(t, N_GROUPS, EXPERTS_PER_GROUP)
    group_score = jnp.sum(lax.top_k(sel, TOP_K)[0], axis=-1)
    best = jnp.argmax(group_score, axis=-1)
    in_group = sel[jnp.arange(t), best]
    _, local = lax.top_k(in_group, TOP_K)
    eidx = best[:, None] * EXPERTS_PER_GROUP + local
    wts = jnp.take_along_axis(probs, eidx, axis=1)
    wts = wts / jnp.sum(wts, axis=-1, keepdims=True)
    tk = t * TOP_K
    flat_e = eidx.reshape(tk)
    flat_tok = jnp.arange(tk) // TOP_K
    flat_w = wts.reshape(tk)
    order = jnp.argsort(flat_e)
    se = flat_e[order]
    counts = jnp.bincount(flat_e, length=N_EXPERTS)
    padded = ((counts + MOE_BLOCK - 1) // MOE_BLOCK) * MOE_BLOCK
    pad_end = jnp.cumsum(padded)
    pad_start = pad_end - padded
    start = jnp.cumsum(counts) - counts
    dest = pad_start[se] + jnp.arange(tk) - start[se]
    n_blk = -(-(tk + N_EXPERTS * MOE_BLOCK) // MOE_BLOCK)
    rows = n_blk * MOE_BLOCK
    row_tok = jnp.zeros((rows,), jnp.int32).at[dest].set(flat_tok[order])
    row_w = jnp.zeros((rows,), jnp.float32).at[dest].set(flat_w[order])
    blk_e = jnp.minimum(jnp.searchsorted(pad_end, jnp.arange(n_blk) * MOE_BLOCK, side='right'), N_EXPERTS - 1)
    xs = hf[row_tok].reshape(n_blk, MOE_BLOCK, d)

    def expert_block(args):
        xb, e = args
        return (jax.nn.silu(xb @ w_gate[e]) * (xb @ w_up[e])) @ w_down[e]

    ys = lax.map(expert_block, (xs, blk_e)).reshape(rows, d)
    out = jax.ops.segment_sum(ys * row_w[:, None].astype(ys.dtype), row_tok, num_segments=t)
    return out.reshape(b, s, d)

def setup_inputs(seed: int = 0) -> dict:
    key = jax.random.key(seed)
    ks = jax.random.split(key, 18)

    def nrm(k, shape, scale):
        return jax.random.normal(k, shape, jnp.float32) * scale

    return {
        'x': nrm(ks[0], (BATCH, SEQ, D_MODEL), 1.0),
        'w_in': nrm(ks[1], (DEPTH, D_MODEL, D_IN), D_MODEL ** -0.5),
        'cmp_pos': nrm(ks[2], (DEPTH, 2, CMP_LEN, NSA_HEAD_DIM), 0.1),
        'cmp_w1': nrm(ks[3], (DEPTH, 2, CMP_LEN * NSA_HEAD_DIM, NSA_HEAD_DIM), (CMP_LEN * NSA_HEAD_DIM) ** -0.5),
        'cmp_w2': nrm(ks[4], (DEPTH, 2, NSA_HEAD_DIM, NSA_HEAD_DIM), NSA_HEAD_DIM ** -0.5),
        'w_br_a': nrm(ks[5], (DEPTH, W_NSA_Q, D_MODEL), W_NSA_Q ** -0.5),
        'w_br_b': nrm(ks[6], (DEPTH, W_RET_V, D_MODEL), W_RET_V ** -0.5),
        'w_o': nrm(ks[7], (DEPTH, D_MODEL, D_MODEL), D_MODEL ** -0.5 * DN_BETA),
        'ln1_g': 1.0 + nrm(ks[8], (DEPTH, D_MODEL), 0.02),
        'ln1_b': nrm(ks[9], (DEPTH, D_MODEL), 0.02),
        'w_router': nrm(ks[10], (D_MODEL, N_EXPERTS), D_MODEL ** -0.5),
        'router_bias': nrm(ks[11], (N_EXPERTS,), 0.01),
        'moe_w_gate': nrm(ks[12], (DEPTH, N_EXPERTS, D_MODEL, D_EXPERT), D_MODEL ** -0.5),
        'moe_w_up': nrm(ks[13], (DEPTH, N_EXPERTS, D_MODEL, D_EXPERT), D_MODEL ** -0.5),
        'moe_w_down': nrm(ks[14], (DEPTH, N_EXPERTS, D_EXPERT, D_MODEL), D_EXPERT ** -0.5 * DN_BETA),
        'ln2_g': 1.0 + nrm(ks[15], (DEPTH, D_MODEL), 0.02),
        'ln2_b': nrm(ks[16], (DEPTH, D_MODEL), 0.02),
        'rel_bias': nrm(ks[17], (REL_BUCKETS, NSA_HEADS), 0.2),
    }

def reference(x, w_in, cmp_pos, cmp_w1, cmp_w2, w_br_a, w_br_b, w_o, ln1_g, ln1_b,
              w_router, router_bias, moe_w_gate, moe_w_up, moe_w_down, ln2_g, ln2_b, rel_bias):
    b, s, _ = x.shape
    offsets = [int(o) for o in np.cumsum(IN_WIDTHS)[:-1]]
    for l in range(DEPTH):
        proj = x @ w_in[l]
        (q_a, k_c, v_c, k_s, v_s, k_w, v_w, g_a,
         q_r, k_r, v_r, g_r, m_a, m_b) = jnp.split(proj, offsets, axis=-1)
        y_a = nsa_attention(q_a.reshape(b, s, NSA_HEADS, NSA_HEAD_DIM),
                            k_c.reshape(b, s, NSA_KV_GROUPS, NSA_HEAD_DIM),
                            v_c.reshape(b, s, NSA_KV_GROUPS, NSA_HEAD_DIM),
                            k_s.reshape(b, s, NSA_KV_GROUPS, NSA_HEAD_DIM),
                            v_s.reshape(b, s, NSA_KV_GROUPS, NSA_HEAD_DIM),
                            k_w.reshape(b, s, NSA_KV_GROUPS, NSA_HEAD_DIM),
                            v_w.reshape(b, s, NSA_KV_GROUPS, NSA_HEAD_DIM),
                            g_a.reshape(b, s, NSA_HEADS, 3),
                            cmp_pos[l], cmp_w1[l], cmp_w2[l], rel_bias)
        y_b = retention(q_r.reshape(b, s, RET_HEADS, RET_QK_DIM),
                        k_r.reshape(b, s, RET_HEADS, RET_QK_DIM),
                        v_r.reshape(b, s, RET_HEADS, RET_V_DIM), g_r)
        merged = jax.nn.sigmoid(m_a) * (y_a @ w_br_a[l]) + jax.nn.sigmoid(m_b) * (y_b @ w_br_b[l])
        x = layer_norm(DN_ALPHA * x + merged @ w_o[l], ln1_g[l], ln1_b[l])
        x = layer_norm(DN_ALPHA * x + moe_ffn(x, w_router, router_bias, moe_w_gate[l], moe_w_up[l], moe_w_down[l]),
                       ln2_g[l], ln2_b[l])
    return x


_drawn_inputs = setup_inputs


def setup_inputs(seed=0):
    import zlib

    import numpy as np

    out = dict(_drawn_inputs(seed))
    spreads = {}
    factors = {'rel_bias': 3.436}
    for name, (base, spread) in spreads.items():
        noise = np.random.default_rng([zlib.crc32(name.encode()), seed]).standard_normal(out[name].shape)
        drawn = base * np.exp(spread * noise) if base else spread * noise
        out[name] = __import__('jax').numpy.asarray(drawn.astype(out[name].dtype))
    for name, factor in factors.items():
        out[name] = (out[name] * factor).astype(out[name].dtype)
    return out
```

```python
import concourse.bass as bass
from concourse import mybir
from contextlib import ExitStack

F32 = mybir.dt.float32
ALU = mybir.AluOpType
ACT = mybir.ActivationFunctionType
AX = mybir.AxisListType

P = 128
D = 1024
SEQ = 256
DEPTH = 2
NT = SEQ // P
KD = D // P
NH = 8
HD = 64
GROUPS = 2
HPG = NH // GROUPS
NSTRIDE, NLEN = 16, 32
NC = (SEQ - NLEN) // NSTRIDE + 1
CP = 16
L2 = NLEN // 2
NE = 16
EG = 4
FE = 512
NG3 = 3 * NH
ALPHA = float((2 * DEPTH) ** 0.25)
LN_EPS = 1e-5
MASKED = -1e30

SLOT = KD * 512
RING = 6
O_Q, O_KC, O_KW = 0, 512, 1024
O_QR, O_KR, O_VR, O_GR, O_MA, O_MB = 1304, 1816, 2328, 3352, 4376, 5400
ROW = 6424
CHUNKS = [("in", O_Q, 512), ("in", O_KC, 512), ("in", O_KW, 280), ("in", O_QR, 512), ("in", O_KR, 512),
          ("in", O_VR, 512), ("in", O_VR + 512, 512), ("in", O_GR, 512), ("in", O_GR + 512, 512),
          ("in", O_MA, 512), ("in", O_MA + 512, 512), ("br_a", 0, 1024),
          ("in", O_MB, 512), ("in", O_MB + 512, 512), ("br_b", 0, 512), ("br_b", 512, 512),
          ("o", 0, 512), ("o", 512, 512)]
NCH = len(CHUNKS)
USES = (NCH + 3 * NE) // RING

STEPS = [("xT", t, c) for t in range(NT) for c in range(2)]
STEPS += [("q", 0), ("q", 1), ("kcvc",), ("ksvs",), ("kwvw",), ("gate",), ("win",), ("S", 0), ("qr", 0), ("H",),
          ("KC",), ("VC",), ("CS",), ("rot", 0), ("qr", 1), ("CN",), ("CT",), ("N", 0)]
_side = [("kr", 0), ("kr", 1)] + [("vr", c, t) for c in range(2) for t in range(NT)] \
    + [("gr", c, t) for c in range(2) for t in range(NT)]
for _h in range(NH):
    STEPS += [("T", _h)] + ([("S", _h + 1)] if _h < NH - 1 else []) + [_side[_h]]
    if _h < 3:
        STEPS += [("rot", _h + 1)]
    STEPS += [("V", _h)] + ([("N", _h + 1)] if _h < NH - 1 else [])
STEPS += [_side[8], _side[9], ("ST", 0)]
_side = [("ma", i) for i in range(4)] + [("wa", i) for i in range(4)]
for _h in range(NH):
    STEPS += [_side[_h]] + ([("ST", _h + 1)] if _h < NH - 1 else []) + [("Y", _h)]
STEPS += [("GN",)] + [("mb", i) for i in range(4)]
STEPS += [("ybT", t, c) for t in range(NT) for c in range(2)]
STEPS += [("wb", i) for i in range(4)] + [("wo", c, t) for c in range(2) for t in range(NT)]
STEPS += [("LN1",)] + [("x1T", t, c) for t in range(NT) for c in range(2)] + [("R",)]

CHUNK_OF = {"q": 0, "kcvc": 1, "ksvs": 1, "kwvw": 2, "gate": 2, "qr": 3, "kr": 4}
PJ = [s for s in STEPS if s[0] in ("q", "kcvc", "ksvs", "kwvw", "gate", "qr", "kr", "vr", "gr", "ma", "mb", "H", "KC")]
TP, SC, PV = [], [], []
for _s in STEPS:
    if _s[0] in ("xT", "CT", "ybT", "x1T"):
        TP.append(_s)
    if _s[0] == "T":
        TP += [_s + (0,), _s + (1,)]
    if _s[0] in ("CS", "VC", "rot", "ST", "wa", "wb", "wo", "R"):
        SC.append(_s)
    if _s[0] == "S":
        SC += [_s + (0,), _s + (1,)]
    if _s[0] == "Y" or (_s[0] == "V" and _s[1] % 2):
        PV.append(_s)
PJ_AT = {s: i for i, s in enumerate(PJ)}
TP_AT = {s: i for i, s in enumerate(TP)}
SC_AT = {s: i for i, s in enumerate(SC)}
PV_AT = {s: i for i, s in enumerate(PV)}

C_ID, C_SWAP, C_COS, C_SIN, C_CADD, C_CMUL, C_BLK, C_EIDX, C_GIDX = 0, 128, 256, 512, 768, 800, 832, 840, 856
NCONST = 860
FWD, FWD0, REV = 528, 272, 384


class Signal:

    def __init__(self, sem, per_layer, credit=0):
        self.sem, self.per_layer, self.credit = sem, per_layer, credit

    def at(self, l, n):
        return l * self.per_layer + n + self.credit


def build(nc, t):
    with ExitStack() as ctx:
        def sb(name, *shape):
            return ctx.enter_context(nc.sbuf_tensor(name, [P, *shape], F32))

        def bank(name):
            return ctx.enter_context(nc.psum_tensor(name, [P, 512], F32))

        def sem(name, per_layer=0, credit=0):
            return Signal(ctx.enter_context(nc.semaphore(name)), per_layer, credit)

        ring = sb("ring", RING, SLOT)
        x = sb("x", NT, D)
        xT = sb("xT", KD, SEQ)
        merged = sb("merged", KD, SEQ)
        qz = merged
        ybT = sb("ybT", KD, SEQ)
        qrz = ybT
        lnw = sb("lnw", 2, D)
        krT = lnw[:, 0, :].rearrange("p (b s) -> p b s", s=SEQ)
        yaT = lnw[:, 1, :].rearrange("p (b s) -> p b s", s=SEQ)
        vr = sb("vr", NT, D)
        gateb = vr[:].rearrange("p t d -> p (t d)").rearrange("p (b s) -> p b s", s=SEQ)
        yb = sb("yb", NT, D)
        yraw = sb("yraw", NT, D)
        bias = sb("bias", NH, SEQ)
        decay = sb("decay", NH, SEQ)
        kTd = sb("kTd", GROUPS, 2, SEQ)
        vn = sb("vn", NT, 2, P)
        sbuf_s = sb("scores", 768)
        pT = sb("pT", 768)
        const = sb("const", NCONST)
        wrt = sb("wrt", KD, NE)
        bcmp = sb("bcmp", NT, NH, CP)
        scmp = sb("scmp", NT * NH, CP)
        pcT = sb("pcT", SEQ)
        vcz = sb("vcz", NH, HD)
        kcd = sb("kcd", GROUPS, CP)
        gk = sb("gk", GROUPS, NC)
        gv = sb("gv", GROUPS, HPG, CP)
        gates = sb("gates", NT, NG3)
        w2 = sb("w2", HD)
        pos = sb("pos", 2, L2)
        small = sb("small", 512)
        cmpw = vr[:].rearrange("p a d -> p (a d)").rearrange("p (v l m) -> p v l m", v=2, l=L2)
        yflat = yraw[:].rearrange("p t d -> p (t d)")
        kv2 = yflat[:, 0:1024].rearrange("p (v g s) -> p v g s", v=2, g=GROUPS)
        win = yflat[:, 1024:1024 + 2 * L2 * 30].rearrange("p (v l g c) -> p v l g c", v=2, l=L2, g=GROUPS)
        ybf = yb[:].rearrange("p t d -> p (t d)")
        rraw = ybf[:, 0:1024].rearrange("p (u b s) -> p u b s", u=2, b=2)
        rtmp = ybf[:, 1024:1536].rearrange("p (b s) -> p b s", b=2)
        rsum = ybf[:, 1536:2048].rearrange("p (b s) -> p b s", b=2)
        st = sbuf_s[:].rearrange("p (u n) -> p u n", u=2)
        hs = ybf[:, 0:1024].rearrange("p (t f) -> p t f", t=NT)
        hh = ybf[:, 1024:2048].rearrange("p (t f) -> p t f", t=NT)
        hT = yflat[:, 0:1024].rearrange("p (t f s) -> p t f s", t=NT, f=4)
        for name, rows_, o, n in (("s_rel", 32, 0, NH), ("s_rev", 32, 8, REV), ("s_fwd", 32, 400, FWD),
                                  ("s_neg", NH, 1000, REV), ("s_rows", NH, 1400, REV)):
            t[name] = ybf[0:rows_, o:o + n]
        t["s_rb"] = sb("router_bias_rows", NE)[:]
        ident = const[:, C_ID:C_ID + P]
        cosT = const[:, C_COS:C_COS + SEQ]
        sinT = const[:, C_SIN:C_SIN + SEQ]

        at = [0]

        def piece(n):
            at[0] += n
            return small[:, at[0] - n:at[0]]
        nmax, psum4, r4 = piece(4), piece(4), piece(4)
        cmax, csum, crec = piece(16), piece(16), piece(16)
        stats = piece(NT * NH * 6).rearrange("p (t h n) -> p t h n", t=NT, h=NH)
        mv = piece(NT * NH * 2).rearrange("p (t h n) -> p t h n", t=NT, h=NH)
        vare, sdev, rstd = piece(16), piece(16), piece(16)
        lstats = piece(24).rearrange("p (t c n) -> p t c n", t=NT, c=2)
        lmv = piece(4).rearrange("p (t n) -> p t n", t=NT)
        rt = sb("rt", 12, NT, NE)

        pj = [bank(f"pj{i}") for i in range(2)]
        tp = [bank(f"tp{i}") for i in range(2)]
        sc = [bank(f"sc{i}") for i in range(2)]
        pv = [bank(f"pv{i}") for i in range(2)]

        landed = [sem(f"landed{i}", 32 * USES) for i in range(RING)]
        consts_in, x_in = sem("consts_in"), sem("x_in")
        rows_out, bias_in, toep_in = sem("rows_out"), sem("bias_in"), sem("toep_in")
        setup_mm, setup_rows, setup_bc, zero_once = sem("setup_mm"), sem("setup_rows"), sem("setup_bc"), sem("zero_once")
        cw_in, lnw_in = sem("cw_in", 96), sem("lnw_in", 64)
        zeroed = sem("zeroed", 4)
        pj_ready, pj_done = sem("pj_ready", len(PJ)), sem("pj_done", len(PJ))
        tp_ready, tp_done = sem("tp_ready", len(TP)), sem("tp_done", len(TP))
        sc_ready, sc_done = sem("sc_ready", len(SC)), sem("sc_done", len(SC))
        pv_ready, pv_done = sem("pv_ready", len(PV)), sem("pv_done", len(PV))
        win_ready, soft_in, exp_done, p_ready = sem("win_ready", 1), sem("soft_in", 10), sem("exp_done", 10), sem("p_ready", 9)
        var_ready, sqrt_done, yb_ready, x_ready = sem("var_ready", 3), sem("sqrt_done", 3), sem("yb_ready", 1), sem("x_ready", 2)
        g_ready, u_ready, silu_done = sem("g_ready", 2 * NE), sem("u_ready", 2 * NE), sem("silu_done", 2 * NE, 2)
        h_ready, ht_ready, ht_done = sem("h_ready", 2 * NE, 2), sem("ht_ready", 2 * NE, 2), sem("ht_done", 2 * NE, 2)
        y_ready, y_done = sem("y_ready", 4 * NE, 4), sem("y_done", 4 * NE, 4)
        dve_step, sp_paced = sem("dve_step"), sem("sp_paced")
        out_done = sem("out_done")

        rows_dram = nc.dram_tensor("bias_rows", [NH, REV], F32)
        PITCH = REV + P
        SHIFTED = PITCH * P + P
        shift_dram = nc.dram_tensor("bias_shifted", [NH, SHIFTED], F32)
        shift_out = sem("shift_out")

        def w_in(l, o, n):
            return t["w_in"][l].rearrange("(k p) n -> p k n", p=P)[:, :, o:o + n]

        def chunk_source(l, n):
            kind, o, width = CHUNKS[n]
            if kind == "in":
                return w_in(l, o, width), KD * width
            if kind == "br_a":
                return t["w_br_a"][l].rearrange("(k p) n -> p k n", p=P), 4 * D
            name = "w_br_b" if kind == "br_b" else "w_o"
            return t[name][l].rearrange("(k p) n -> p k n", p=P)[:, :, o:o + width], KD * width

        def slot(n, k, width):
            return ring[:, n % RING, 0:k * width].rearrange("p (k n) -> p k n", k=k)

        def weights_in(eng, l, n):
            eng.wait_ge(landed[n % RING].sem, landed[n % RING].at(l, 32 * (n // RING + 1)))

        LAST = {0: ("q", 1), 1: ("ksvs",), 2: ("gate",), 3: ("qr", 1), 4: ("kr", 1), 5: ("vr", 0, 1), 6: ("vr", 1, 1),
                7: ("gr", 0, 1), 8: ("gr", 1, 1), 9: ("ma", 1), 10: ("ma", 3), 11: ("wa", 3), 12: ("mb", 1),
                13: ("mb", 3), 14: ("wb", 1), 15: ("wb", 3), 16: ("wo", 0, 1), 17: ("wo", 1, 1)}

        def wait_chunk_used(eng, l, n):
            if LAST[n] in PJ_AT:
                eng.wait_ge(pj_ready.sem, pj_ready.at(l, PJ_AT[LAST[n]] + 1))
            else:
                eng.wait_ge(sc_ready.sem, sc_ready.at(l, SC_AT[LAST[n]] + 1))

        block = ctx.enter_context(nc.Block())

        @block.sync
        def _(sp):
            def load(n, dst_floats, src, k, width):
                dst = slot(n, k, width)
                for a in (0, 64):
                    sp.dma_start(dst[a:a + 64], src[a:a + 64]).then_inc(landed[n % RING].sem, 16)

            def load_expert(l, e, u):
                half = NCH + 3 * u
                for i, name in enumerate(("moe_w_gate", "moe_w_up", "moe_w_down")):
                    src = t[name][l].rearrange("e a b -> (e a) b")
                    rows, width = (D, FE) if i < 2 else (FE, D)
                    src = src[bass.ds(e * rows, rows), :].rearrange("(k p) n -> p k n", p=P)
                    yield half + i, src, rows // P, width

            for l in range(DEPTH):
                for n in range(NCH):
                    if n >= RING:
                        wait_chunk_used(sp, l, n - RING)
                    elif l > 0:
                        e = NE - 2 + n // 3
                        freed = (g_ready, u_ready, y_ready)[n % 3]
                        sp.wait_ge(freed.sem, freed.at(l - 1, (2 * e + 2, 2 * e + 2, 4 * e + 4)[n % 3]))
                    src, floats = chunk_source(l, n)
                    load(n, floats, src, *((4, D) if CHUNKS[n][0] == "br_a" else (KD, CHUNKS[n][2])))
                    if l == 0 and n == 0:
                        sp.dma_start(x[:], t["x"][0].rearrange("(t p) d -> p t d", p=P)).then_inc(x_in.sem, 16)
                for e in range(2):
                    for i, (n, src, k, width) in enumerate(load_expert(l, e, e)):
                        wait_chunk_used(sp, l, NCH - RING + 3 * e + i)
                        load(n, SLOT, src, k, width)
                with sp.Fori(1, NE // 2) as pair:
                    for u in range(2):
                        for i, (n, src, k, width) in enumerate(load_expert(l, pair * 2 + u, u)):
                            done = (g_ready, u_ready, y_ready)[i]
                            per = (2, 2, 4)[i]
                            sp.wait_ge(done.sem, done.at(l, pair * (2 * per) + per * (u - 1)))
                            sp.sem_inc(sp_paced.sem, 1)
                            load(n, SLOT, src, k, width)
            sp.wait_ge(x_ready.sem, x_ready.at(DEPTH - 1, 2))
            sp.dma_start(t["out"][0].rearrange("(t p) d -> p t d", p=P), x[:]).then_inc(out_done.sem, 16)
            sp.wait_ge(out_done.sem, 16)

        @block.gpsimd
        def _(pool):
            def zero_halves(l, buf, n):
                for i, (rows, first) in enumerate(((slice(64, P), 0), (slice(0, 64), 1))):
                    pool.memset(buf[rows, first:NH:2, :], 0.0).then_inc(zeroed.sem, 1)
                    pool.wait_ge(zeroed.sem, zeroed.at(l, n + i + 1))

            pool.memset(kcd[:], 0.0).then_inc(zero_once.sem, 1)
            pool.memset(gv[:], 0.0).then_inc(zero_once.sem, 1)
            pool.wait_ge(zero_once.sem, 2)
            for l in range(DEPTH):
                if l > 0:
                    pool.wait_ge(x_ready.sem, x_ready.at(l - 1, 2))
                for v in range(2):
                    pool.dma_start(cmpw[:, v], t["cmp_w1"][l, v].rearrange("(l q) m -> q l m", q=P)).then_inc(cw_in.sem, 16)
                    pool.dma_start(w2[64 * v:64 * v + 64, :], t["cmp_w2"][l, v]).then_inc(cw_in.sem, 16)
                    pool.dma_start(pos[:, v, :], t["cmp_pos"][l, v]).then_inc(cw_in.sem, 16)
                if l > 0:
                    pool.wait_ge(sc_ready.sem, sc_ready.at(l - 1, SC_AT[("wo", 1, 1)] + 1))
                zero_halves(l, qz, 0)
                zero_halves(l, qrz, 2)
                pool.wait_ge(sc_ready.sem, sc_ready.at(l, SC_AT[("wa", 3)] + 1))
                for i, name in enumerate(("ln1_g", "ln1_b")):
                    pool.dma_start(lnw[:, i, :], t[name][l:l + 1, :].broadcast_to([P, D])).then_inc(lnw_in.sem, 16)
                pool.wait_ge(x_ready.sem, x_ready.at(l, 1))
                for i, name in enumerate(("ln2_g", "ln2_b")):
                    pool.dma_start(lnw[:, i, :], t[name][l:l + 1, :].broadcast_to([P, D])).then_inc(lnw_in.sem, 16)

        @block.tensor
        def _(pe):
            mm = pe.matmul
            pe.sem_inc(ht_ready.sem, 2)
            pe.sem_inc(y_ready.sem, 4)

            def take(banks, done, index, l, step):
                i = index[step]
                pe.wait_ge(done.sem, done.at(l, max(i - 1, 0)))
                return banks[i % 2]

            def columns(l, step, bankap, chunk, col, off):
                w = slot(chunk, KD, CHUNKS[chunk][2])
                for k in range(KD):
                    ins = mm(bankap[:, off:off + SEQ], w[:, k, col:col + P], xT[:, k, :], start=(k == 0), stop=(k == KD - 1))
                return ins

            def rows(tile, out, chunk, col, width, lhs=None):
                w = slot(chunk, KD, CHUNKS[chunk][2])
                lhs = xT if lhs is None else lhs
                for k in range(KD):
                    ins = mm(out, lhs[:, k, tile * P:(tile + 1) * P], w[:, k, col:col + width],
                             start=(k == 0), stop=(k == KD - 1))
                return ins

            pe.wait_ge(consts_in.sem, 80)
            mm(sc[0][0:NH, 0:REV], t["s_rel"], t["s_rev"], start=True, stop=True).then_inc(setup_mm.sem, 1)
            for qt in range(NT):
                for c in range(CP):
                    o = FWD0 + qt * P - NSTRIDE * c - (NLEN - 1)
                    ins = mm(sc[1][:, (qt * CP + c) * NH:(qt * CP + c + 1) * NH], t["s_fwd"][:, o:o + P], t["s_rel"],
                             start=True, stop=True)
            ins.then_inc(setup_mm.sem, 1)
            pe.wait_ge(setup_bc.sem, 1)

            for l in range(DEPTH):
                for step in STEPS:
                    kind = step[0]
                    if kind in ("xT", "x1T", "ybT"):
                        _, tile, c = step
                        if c == 0 and tile == 0:
                            if kind == "ybT":
                                pe.wait_ge(yb_ready.sem, yb_ready.at(l, 1))
                            elif kind == "x1T":
                                pe.wait_ge(x_ready.sem, x_ready.at(l, 1))
                            elif l == 0:
                                pe.wait_ge(x_in.sem, 16)
                            else:
                                pe.wait_ge(x_ready.sem, x_ready.at(l - 1, 2))
                        src = yb if kind == "ybT" else x
                        b = take(tp, tp_done, TP_AT, l, step)
                        for i in range(4):
                            ins = pe.transpose(b[:, i * P:(i + 1) * P], src[:, tile, (4 * c + i) * P:(4 * c + i + 1) * P], ident)
                        ins.then_inc(tp_ready.sem, 1)
                    elif kind in ("q", "qr", "kr", "ma", "mb"):
                        i = step[1]
                        chunk = CHUNK_OF[kind] if kind in CHUNK_OF else (9 if kind == "ma" else 12) + i // 2
                        first = i % 2 == 0
                        if first:
                            weights_in(pe, l, chunk)
                        if kind == "q" and i == 0:
                            pe.wait_ge(tp_done.sem, tp_done.at(l, TP_AT[("xT", 1, 1)] + 1))
                        b = take(pj, pj_done, PJ_AT, l, step)
                        columns(l, step, b, chunk, (i % 2) * SEQ, 0)
                        columns(l, step, b, chunk, (i % 2) * SEQ + P, SEQ).then_inc(pj_ready.sem, 1)
                    elif kind == "kcvc":
                        weights_in(pe, l, 1)
                        b = take(pj, pj_done, PJ_AT, l, step)
                        columns(l, step, b, 1, 0, 0)
                        columns(l, step, b, 1, P, SEQ).then_inc(pj_ready.sem, 1)
                    elif kind in ("ksvs", "kwvw"):
                        chunk, col = (1, 2 * P) if kind == "ksvs" else (2, 0)
                        weights_in(pe, l, chunk)
                        b = take(pj, pj_done, PJ_AT, l, step)
                        columns(l, step, b, chunk, col, 0)
                        rows(0, b[:, SEQ:SEQ + P], chunk, col + P, P)
                        rows(1, b[:, SEQ + P:SEQ + 2 * P], chunk, col + P, P).then_inc(pj_ready.sem, 1)
                    elif kind == "gate":
                        b = take(pj, pj_done, PJ_AT, l, step)
                        rows(0, b[:, 0:NG3], 2, 2 * P, NG3)
                        rows(1, b[:, NG3:2 * NG3], 2, 2 * P, NG3).then_inc(pj_ready.sem, 1)
                    elif kind in ("vr", "gr"):
                        _, c, tile = step
                        chunk = (5 if kind == "vr" else 7) + c
                        if tile == 0:
                            weights_in(pe, l, chunk)
                        b = take(pj, pj_done, PJ_AT, l, step)
                        rows(tile, b[:], chunk, 0, 512).then_inc(pj_ready.sem, 1)
                    elif kind == "H":
                        pe.wait_ge(win_ready.sem, win_ready.at(l, 1))
                        b = take(pj, pj_done, PJ_AT, l, step)
                        for i in range(L2):
                            for v in range(2):
                                ins = mm(b[64 * v:64 * v + 64, 0:2 * NC], cmpw[:, v, i, :],
                                         win[:, v, i].rearrange("p g c -> p (g c)"), start=(i == 0), stop=(i == L2 - 1))
                        ins.then_inc(pj_ready.sem, 1)
                    elif kind == "KC":
                        pe.wait_ge(pj_done.sem, pj_done.at(l, PJ_AT[("H",)] + 1))
                        b = take(pj, pj_done, PJ_AT, l, step)
                        for g in range(GROUPS):
                            for a in (0, 64):
                                ins = mm(b[a:a + 64, g * NC:(g + 1) * NC], w2[0:64, :], gk[0:64, g, :], start=True, stop=True)
                        ins.then_inc(pj_ready.sem, 1)
                    elif kind == "VC":
                        b = take(sc, sc_done, SC_AT, l, step)
                        mm(b[:, 0:HD], gv[64:P].rearrange("p g r c -> p (g r c)"), w2[64:P, :],
                           start=True, stop=True).then_inc(sc_ready.sem, 1)
                    elif kind == "CS":
                        pe.wait_ge(pj_done.sem, pj_done.at(l, PJ_AT[("KC",)] + 1))
                        b = take(sc, sc_done, SC_AT, l, step)
                        for qt in range(NT):
                            for h in range(NH):
                                o = (qt * NH + h) * CP
                                ins = mm(b[:, o:o + CP], qz[:, h, qt * P:(qt + 1) * P], kcd[:, h // HPG, :], start=True, stop=True)
                        ins.then_inc(sc_ready.sem, 1)
                    elif kind == "S":
                        h = step[1]
                        if h == 0:
                            pe.wait_ge(pj_done.sem, pj_done.at(l, PJ_AT[("kwvw",)] + 1))
                            pe.wait_ge(zeroed.sem, zeroed.at(l, 2))
                        for qt in range(NT):
                            b = take(sc, sc_done, SC_AT, l, step + (qt,))
                            n = (qt + 1) * P
                            mm(b[:, 0:2 * n].rearrange("p (r k) -> p r k", r=2), qz[:, h, qt * P:(qt + 1) * P],
                               kTd[:, h // HPG, :, 0:n], start=True, stop=True).then_inc(sc_ready.sem, 1)
                    elif kind == "rot":
                        i = step[1]
                        src = ("qr", "kr")[i // 2], i % 2
                        pe.wait_ge(pj_done.sem, pj_done.at(l, PJ_AT[src] + 1))
                        b = take(sc, sc_done, SC_AT, l, step)
                        mm(b[:], const[:, C_SWAP:C_SWAP + P], rraw[:, i % 2].rearrange("p b s -> p (b s)"),
                           start=True, stop=True).then_inc(sc_ready.sem, 1)
                    elif kind == "CT":
                        pe.wait_ge(p_ready.sem, p_ready.at(l, 1))
                        b = take(tp, tp_done, TP_AT, l, step)
                        for qt in range(NT):
                            ins = pe.transpose(b[:, qt * P:(qt + 1) * P],
                                               scmp[:, qt * NH:(qt + 1) * NH, :].rearrange("p h c -> p (h c)"), ident)
                        ins.then_inc(tp_ready.sem, 1)
                    elif kind == "T":
                        h = step[1]
                        pe.wait_ge(p_ready.sem, p_ready.at(l, h + 2))
                        b = take(tp, tp_done, TP_AT, l, step + (0,))
                        for r in range(2):
                            pe.transpose(b[:, r * SEQ:r * SEQ + P], sbuf_s[:, r * P:(r + 1) * P], ident)
                            ins = pe.transpose(b[:, r * SEQ + P:(r + 1) * SEQ], sbuf_s[:, SEQ + r * SEQ:SEQ + r * SEQ + P], ident)
                        ins.then_inc(tp_ready.sem, 1)
                        b = take(tp, tp_done, TP_AT, l, step + (1,))
                        for r in range(2):
                            ins = pe.transpose(b[:, r * P:(r + 1) * P], sbuf_s[:, SEQ + r * SEQ + P:SEQ + (r + 1) * SEQ], ident)
                        ins.then_inc(tp_ready.sem, 1)
                    elif kind == "V":
                        h = step[1]
                        i = PV_AT[("V", h | 1)]
                        if h % 2 == 0:
                            pe.wait_ge(pv_done.sem, pv_done.at(l, max(i - 1, 0)))
                        pe.wait_ge(tp_done.sem, tp_done.at(l, TP_AT[("T", h, 1)] + 1))
                        if h == 0:
                            pe.wait_ge(sc_done.sem, sc_done.at(l, SC_AT[("VC",)] + 1))
                        o = pv[i % 2][64 * (h % 2):64 * (h % 2) + 64, :]
                        g = h // HPG
                        mm(o[:, 0:SEQ], vcz[:, h, :], pcT[:], start=True, stop=False, skip_group_check=True)
                        for r in range(2):
                            mm(o[:, 0:SEQ], vn[:, 0, r, g * HD:(g + 1) * HD], pT[:, r * SEQ:(r + 1) * SEQ],
                               start=False, stop=False, skip_group_check=True)
                        for r in range(2):
                            ins = mm(o[:, P:SEQ], vn[:, 1, r, g * HD:(g + 1) * HD], pT[:, 512 + r * P:512 + (r + 1) * P],
                                     start=False, stop=(r == 1), skip_group_check=True)
                        if h % 2:
                            ins.then_inc(pv_ready.sem, 1)
                    elif kind == "ST":
                        h = step[1]
                        if h == 0:
                            pe.wait_ge(sc_done.sem, sc_done.at(l, SC_AT[("rot", 3)] + 1))
                        b = take(sc, sc_done, SC_AT, l, step)
                        mm(b[:, 0:SEQ], krT[:, h // 2, 0:P], qrz[:, h, :], start=True, stop=True)
                        mm(b[:, SEQ:SEQ + P], krT[:, h // 2, P:SEQ], qrz[:, h, P:SEQ], start=True, stop=True)\
                            .then_inc(sc_ready.sem, 1)
                    elif kind == "Y":
                        h = step[1]
                        if h == 0:
                            pe.wait_ge(pj_done.sem, pj_done.at(l, PJ_AT[("vr", 1, 1)] + 1))
                        pe.wait_ge(sc_done.sem, sc_done.at(l, SC_AT[("ST", h)] + 1))
                        b = take(pv, pv_done, PV_AT, l, step)
                        s = st[:, h % 2, :]
                        v = [vr[:, j, h * P:(h + 1) * P] for j in range(NT)]
                        mm(b[:, 0:P], s[:, 0:P], v[0], start=True, stop=True)
                        mm(b[:, P:SEQ], s[:, P:SEQ], v[0], start=True, stop=False)
                        mm(b[:, P:SEQ], s[:, SEQ:SEQ + P], v[1], start=False, stop=True).then_inc(pv_ready.sem, 1)
                    elif kind in ("wa", "wb"):
                        i = step[1]
                        if kind == "wa":
                            w, rhs, nk, col = slot(11, 4, D), yaT, 4, 2 * i * P
                            if i == 0:
                                weights_in(pe, l, 11)
                                pe.wait_ge(pv_done.sem, pv_done.at(l, PV_AT[("V", NH - 1)] + 1))
                        else:
                            w, rhs, nk, col = slot(14 + i // 2, KD, 512), ybT, KD, 2 * (i % 2) * P
                            if i % 2 == 0:
                                weights_in(pe, l, 14 + i // 2)
                            if i == 0:
                                pe.wait_ge(tp_done.sem, tp_done.at(l, TP_AT[("ybT", 1, 1)] + 1))
                        b = take(sc, sc_done, SC_AT, l, step)
                        for j in range(2):
                            for k in range(nk):
                                ins = mm(b[:, j * SEQ:(j + 1) * SEQ], w[:, k, col + j * P:col + (j + 1) * P], rhs[:, k, :],
                                         start=(k == 0), stop=(k == nk - 1))
                        ins.then_inc(sc_ready.sem, 1)
                    elif kind == "wo":
                        _, c, tile = step
                        if tile == 0:
                            weights_in(pe, l, 16 + c)
                        if c == 0 and tile == 0:
                            pe.wait_ge(sc_done.sem, sc_done.at(l, SC_AT[("wb", 3)] + 1))
                        b = take(sc, sc_done, SC_AT, l, step)
                        rows(tile, b[:], 16 + c, 0, 512, merged).then_inc(sc_ready.sem, 1)
                    elif kind == "R":
                        pe.wait_ge(tp_done.sem, tp_done.at(l, TP_AT[("x1T", 1, 1)] + 1))
                        b = take(sc, sc_done, SC_AT, l, step)
                        for tile in range(NT):
                            for k in range(KD):
                                ins = mm(b[:, tile * NE:(tile + 1) * NE], xT[:, k, tile * P:(tile + 1) * P], wrt[:, k, :],
                                         start=(k == 0), stop=(k == KD - 1))
                        ins.then_inc(sc_ready.sem, 1)

                pe.wait_ge(pj_done.sem, pj_done.at(l, len(PJ)))
                pe.wait_ge(sc_done.sem, sc_done.at(l, len(SC)))
                pe.wait_ge(pv_done.sem, pv_done.at(l, len(PV)))
                with pe.Fori(0, NE // 2) as pair:
                    for u in range(2):
                        def n(per, c):
                            return pair * (2 * per) + per * u + c
                        wg, wu, wd = slot(3 * u, KD, FE), slot(3 * u + 1, KD, FE), slot(3 * u + 2, 4, D)

                        def here(i):
                            pe.wait_ge(landed[3 * u + i].sem, landed[3 * u + i].at(l, pair * 32 + 32 * (NCH // RING + 1)))
                        for tile in range(NT):
                            for i, (w, banks, done, ready) in enumerate(((wg, pj, silu_done, g_ready), (wu, pv, h_ready, u_ready))):
                                if tile == 0:
                                    here(i)
                                pe.wait_ge(done.sem, done.at(l, n(2, tile - 1)))
                                for k in range(KD):
                                    ins = mm(banks[tile][:], xT[:, k, tile * P:(tile + 1) * P], w[:, k, :],
                                             start=(k == 0), stop=(k == KD - 1))
                                ins.then_inc(ready.sem, 1)
                        here(2)
                        for tile in range(NT):
                            pe.wait_ge(h_ready.sem, h_ready.at(l, n(2, tile + 1)))
                            pe.wait_ge(ht_done.sem, ht_done.at(l, n(2, tile - 1)))
                            for f in range(4):
                                ins = pe.transpose(tp[tile][:, f * P:(f + 1) * P], hh[:, tile, f * P:(f + 1) * P], ident)
                            ins.then_inc(ht_ready.sem, 1)
                            pe.wait_ge(ht_done.sem, ht_done.at(l, n(2, tile + 1)))
                            for half in range(2):
                                pe.wait_ge(y_done.sem, y_done.at(l, n(4, 2 * tile + half - 1)))
                                for f in range(4):
                                    ins = mm(sc[half][:], hT[:, tile, f, :], wd[:, f, half * 512:(half + 1) * 512],
                                             start=(f == 0), stop=(f == 3))
                                ins.then_inc(y_ready.sem, 1)

        @block.scalar
        def _(act):
            A = act.activation
            act.sem_inc(silu_done.sem, 2)
            act.sem_inc(ht_done.sem, 2)
            act.dma_start(const[:], t["c_pack"]).then_inc(consts_in.sem, 16)
            act.dma_start(t["s_rel"], t["rel_bias"]).then_inc(consts_in.sem, 16)
            act.dma_start(t["s_rev"], t["c_rev"]).then_inc(consts_in.sem, 16)
            act.dma_start(t["s_fwd"], t["c_fwd"]).then_inc(consts_in.sem, 16)
            act.dma_start(t["s_neg"], t["c_neg"]).then_inc(consts_in.sem, 16)
            act.dma_start(wrt[:], t["w_router"].rearrange("(k p) e -> p k e", p=P)).then_inc(bias_in.sem, 16)
            act.dma_start(t["s_rb"], t["router_bias"].rearrange("(a e) -> a e", a=1).broadcast_to([P, NE])).then_inc(bias_in.sem, 16)
            act.dma_start(decay[:], t["c_decay"]).then_inc(bias_in.sem, 16)
            act.wait_ge(setup_rows.sem, 1)
            act.dma_start(rows_dram[:, :], t["s_rows"]).then_inc(rows_out.sem, 16)
            act.wait_ge(rows_out.sem, 16)
            act.dma_start(bass.AP(shift_dram, 0, [[PITCH + 1, P], [SHIFTED, NH], [1, REV]]),
                          bass.AP(rows_dram, 0, [[0, P], [REV, NH], [1, REV]])).then_inc(shift_out.sem, 16)
            act.wait_ge(shift_out.sem, 16)
            act.dma_start(bias[:], bass.AP(shift_dram, P - 1, [[PITCH, P], [SHIFTED, NH], [1, SEQ]])).then_inc(toep_in.sem, 16)

            for l in range(DEPTH):
                for step in STEPS:
                    kind = step[0]
                    if step in PJ_AT:
                        i = PJ_AT[step]
                        b = pj[i % 2]
                        pair = b[:].rearrange("p (b s) -> p b s", b=2)
                        if kind == "q":
                            o = 4 * step[1]
                            if step[1] == 0:
                                act.wait_ge(zeroed.sem, zeroed.at(l, 2))
                        elif kind == "gr" and step[1:] == (0, 0):
                            act.wait_ge(sc_done.sem, sc_done.at(l, SC_AT[("rot", 3)] + 1))
                        elif kind == "kr":
                            act.wait_ge(sc_done.sem, sc_done.at(l, SC_AT[("rot", step[1])] + 1))
                        elif kind == "KC":
                            act.wait_ge(zero_once.sem, 2)
                        elif kind == "H":
                            act.wait_ge(zero_once.sem, 2)
                        act.wait_ge(pj_ready.sem, pj_ready.at(l, i + 1))
                        if kind == "q":
                            A(qz[0:64, o:o + 4:2, :], pair[0:64], ACT.Copy, scale=HD ** -0.5)
                            ins = A(qz[64:P, o + 1:o + 4:2, :], pair[64:P], ACT.Copy, scale=HD ** -0.5)
                        elif kind == "kcvc":
                            for g in range(GROUPS):
                                src = pair[64 * g:64 * g + 64]
                                A(kv2[0:64, :, g, :], src, ACT.Copy)
                                ins = A(kv2[64:P, :, g, 0:SEQ - 1], src[:, :, 1:SEQ], ACT.Copy)
                        elif kind in ("ksvs", "kwvw"):
                            r = 0 if kind == "ksvs" else 1
                            for g in range(GROUPS):
                                for a in (0, 64):
                                    A(kTd[a:a + 64, g, r, :], b[64 * g:64 * g + 64, 0:SEQ], ACT.Copy)
                            ins = A(vn[:, :, r, :], b[:, SEQ:2 * SEQ].rearrange("p (t d) -> p t d", t=NT), ACT.Copy)
                        elif kind == "gate":
                            ins = A(gates[:].rearrange("p t n -> p (t n)"), b[:, 0:2 * NG3], ACT.Sigmoid)
                        elif kind == "H":
                            A(gk[0:64].rearrange("p g c -> p (g c)"), b[0:64, 0:2 * NC], ACT.Gelu_apprx_tanh)
                            ins = A(gv[64:P, :, :, 0:NC],
                                    b[64:P, 0:2 * NC].rearrange("p (g r c) -> p g r c", g=GROUPS, r=1)
                                    .broadcast_to([64, GROUPS, HPG, NC]), ACT.Gelu_apprx_tanh)
                        elif kind == "KC":
                            ins = A(kcd[:, :, 0:NC], b[:, 0:2 * NC].rearrange("p (g c) -> p g c", g=GROUPS), ACT.Copy)
                        elif kind in ("qr", "kr"):
                            ins = A(rraw[:, step[1]], pair, ACT.Copy)
                        elif kind == "vr":
                            ins = A(vr[:, step[2], step[1] * 512:(step[1] + 1) * 512], b[:], ACT.Copy)
                        elif kind == "gr":
                            ins = A(yb[:, step[2], step[1] * 512:(step[1] + 1) * 512], b[:], ACT.Silu)
                        elif kind == "ma":
                            ins = A(merged[:, 2 * step[1]:2 * step[1] + 2, :], pair, ACT.Sigmoid)
                        elif kind == "mb":
                            ins = A(gateb[:, 2 * step[1]:2 * step[1] + 2, :], pair, ACT.Sigmoid)
                        ins.then_inc(pj_done.sem, 1)
                    elif kind in ("xT", "x1T", "ybT"):
                        _, tile, c = step
                        i = TP_AT[step]
                        if kind == "ybT" and c == 0 and tile == 0:
                            pass
                        act.wait_ge(tp_ready.sem, tp_ready.at(l, i + 1))
                        dst = ybT if kind == "ybT" else xT
                        A(dst[:, 4 * c:4 * c + 4, tile * P:(tile + 1) * P], tp[i % 2][:].rearrange("p (b s) -> p b s", b=4),
                          ACT.Copy).then_inc(tp_done.sem, 1)
                    elif kind == "CT":
                        i = TP_AT[step]
                        act.wait_ge(tp_ready.sem, tp_ready.at(l, i + 1))
                        A(pcT[:], tp[i % 2][:, 0:SEQ], ACT.Copy).then_inc(tp_done.sem, 1)
                    elif kind == "T":
                        for half, (o, n) in enumerate(((0, 512), (512, 256))):
                            i = TP_AT[step + (half,)]
                            act.wait_ge(tp_ready.sem, tp_ready.at(l, i + 1))
                            A(pT[:, o:o + n], tp[i % 2][:, 0:n], ACT.Copy).then_inc(tp_done.sem, 1)
                    elif kind == "CN":
                        act.wait_ge(soft_in.sem, soft_in.at(l, 2))
                        A(scmp[:].rearrange("p n c -> p (n c)"), scmp[:].rearrange("p n c -> p (n c)"), ACT.Exp)\
                            .then_inc(exp_done.sem, 1)
                    elif kind == "N":
                        h = step[1]
                        act.wait_ge(soft_in.sem, soft_in.at(l, h + 2 if h else 1))
                        for j in range(4):
                            n = P if j < 2 else SEQ
                            o = (j % 2) * n + (0 if j < 2 else SEQ)
                            ins = A(sbuf_s[:, o:o + n], sbuf_s[:, o:o + n], ACT.Exp, bias=nmax[:, j:j + 1],
                                    accum_out=psum4[:, j:j + 1])
                        ins.then_inc(exp_done.sem, 1)
                    elif kind in ("GN", "LN1"):
                        n = 0 if kind == "GN" else 1
                        act.wait_ge(var_ready.sem, var_ready.at(l, n + 1))
                        w = 16 if kind == "GN" else 2
                        A(sdev[:, 0:w], vare[:, 0:w], ACT.Sqrt).then_inc(sqrt_done.sem, 1)
                    elif kind == "R":
                        act.wait_ge(soft_in.sem, soft_in.at(l, 10))
                        A(rt[:, 0].rearrange("p t e -> p (t e)"), rt[:, 0].rearrange("p t e -> p (t e)"), ACT.Exp)\
                            .then_inc(exp_done.sem, 1)
                with act.Fori(0, NE // 2) as pair:
                    for u in range(2):
                        def n(per, c):
                            return pair * (2 * per) + per * u + c
                        for tile in range(NT):
                            act.wait_ge(g_ready.sem, g_ready.at(l, n(2, tile + 1)))
                            act.wait_ge(h_ready.sem, h_ready.at(l, n(2, tile - 1)))
                            A(hs[:, tile, :], pj[tile][:], ACT.Silu).then_inc(silu_done.sem, 1)
                        for tile in range(NT):
                            act.wait_ge(ht_ready.sem, ht_ready.at(l, n(2, tile + 1)))
                            act.wait_ge(y_ready.sem, y_ready.at(l, n(4, 2 * tile - 2)))
                            A(hT[:, tile].rearrange("p f s -> p (f s)"), tp[tile][:], ACT.Copy).then_inc(ht_done.sem, 1)
                act.wait_ge(var_ready.sem, var_ready.at(l, 3))
                A(sdev[:, 0:2], vare[:, 0:2], ACT.Sqrt).then_inc(sqrt_done.sem, 1)

        @block.vector
        def _(dve):
            v = dve
            steps_done = [0]
            dve.sem_inc(h_ready.sem, 2)
            dve.sem_inc(y_done.sem, 4)

            def then(ins):
                ins.then_inc(dve_step.sem, 1)
                steps_done[0] += 1
                dve.wait_ge(dve_step.sem, steps_done[0])

            def norm(l, which, dst_stats):
                for tile in range(NT):
                    for c in range(2):
                        ins = v.bn_stats(lstats[:, tile, c, :], x[:, tile, c * 512:(c + 1) * 512])
                then(ins)
                for tile in range(NT):
                    ins = v.bn_aggr(lmv[:, tile, :], lstats[:, tile].rearrange("p c n -> p (c n)"))
                then(ins)
                v.tensor_scalar(vare[:, 0:2], lmv[:, :, 1], LN_EPS, None, ALU.add).then_inc(var_ready.sem, 1)
                v.wait_ge(sqrt_done.sem, sqrt_done.at(l, which + 2))
                then(v.reciprocal(rstd[:, 0:2], sdev[:, 0:2]))
                for tile in range(NT):
                    ins = v.tensor_scalar(x[:, tile, :], x[:, tile, :], lmv[:, tile, 0:1], rstd[:, tile:tile + 1],
                                          ALU.subtract, ALU.mult)
                then(ins)
                v.wait_ge(lnw_in.sem, lnw_in.at(l, 32 * (which + 1)))
                for tile in range(NT):
                    ins = v.tensor_tensor(x[:, tile, :], x[:, tile, :], lnw[:, 0, :], ALU.mult)
                then(ins)
                for tile in range(NT):
                    ins = v.tensor_tensor(x[:, tile, :], x[:, tile, :], lnw[:, 1, :], ALU.add)
                ins.then_inc(x_ready.sem, 1)

            def route(l, b):
                lg, pr, sel, msk, o1, o2, tmp, w = (rt[:, i] for i in (0, 1, 2, 3, 4, 5, 6, 11))
                pair6 = rt[:, 7:10].rearrange("p a t e -> p (a t e)")[:, 0:48].rearrange("p (t g s) -> p t g s", t=NT, g=EG)
                g4 = rt[:, 10].rearrange("p t e -> p (t e)")
                gs, ge = (g4[:, i * 8:i * 8 + 8].rearrange("p (t g) -> p t g", t=NT) for i in range(2))
                s2 = g4[:, 16:18]
                s2b = g4[:, 18:20]
                wide = [P, NT, NE]

                def grp(a):
                    return a.rearrange("p t (g s) -> p t g s", g=EG)

                def b2(a):
                    return a.rearrange("p (t a) -> p t a", a=1).broadcast_to(wide)

                def b2g(a):
                    return a.rearrange("p (t a) -> p t a", a=1).broadcast_to([P, NT, EG])
                eidx = const[:, C_EIDX:C_EIDX + NE].rearrange("p (a e) -> p a e", a=1).broadcast_to(wide)
                gidx = const[:, C_GIDX:C_GIDX + EG].rearrange("p (a e) -> p a e", a=1).broadcast_to([P, NT, EG])
                rb = t["s_rb"].rearrange("p (a e) -> p a e", a=1).broadcast_to(wide)
                TT = v.tensor_tensor
                if l == 0:
                    dve.wait_ge(bias_in.sem, 48)
                then(v.tensor_reduce(s2, b, AX.X, ALU.max))
                TT(lg, b, b2(s2), ALU.subtract).then_inc(soft_in.sem, 1)
                v.wait_ge(exp_done.sem, exp_done.at(l, 10))
                then(v.tensor_reduce(s2, lg, AX.X, ALU.add))
                then(v.reciprocal(s2b, s2))
                then(TT(pr, lg, b2(s2b), ALU.mult))
                then(TT(sel, pr, rb, ALU.add))
                sg = grp(sel)
                TT(pair6[:, :, :, 0:3], sg[:, :, :, 0:3], sg[:, :, :, 1:4], ALU.add)
                TT(pair6[:, :, :, 3:5], sg[:, :, :, 0:2], sg[:, :, :, 2:4], ALU.add)
                then(TT(pair6[:, :, :, 5:6], sg[:, :, :, 0:1], sg[:, :, :, 3:4], ALU.add))
                then(v.tensor_reduce(gs, pair6, AX.X, ALU.max))
                then(v.tensor_reduce(s2, gs, AX.X, ALU.max))
                then(TT(ge, gs, b2g(s2), ALU.is_equal))
                then(TT(gs, ge, gidx, ALU.mult))
                then(v.tensor_reduce(s2, gs, AX.X, ALU.max))
                then(TT(ge, gs, b2g(s2), ALU.is_equal))
                ins = v.tensor_scalar(grp(msk), ge.rearrange("p t (g s) -> p t g s", s=1).broadcast_to([P, NT, EG, EG]),
                                      -MASKED, MASKED, ALU.mult, ALU.add)
                then(ins)
                then(TT(msk, msk, sel, ALU.add))
                for pick in (o1, o2):
                    then(v.tensor_reduce(s2, msk, AX.X, ALU.max))
                    then(TT(tmp, msk, b2(s2), ALU.is_equal))
                    then(TT(tmp, tmp, eidx, ALU.mult))
                    then(v.tensor_reduce(s2, tmp, AX.X, ALU.max))
                    then(TT(pick, tmp, b2(s2), ALU.is_equal))
                    if pick is o1:
                        then(v.scalar_tensor_tensor(out=msk, in0=o1, scalar=3 * MASKED, in1=msk, op0=ALU.mult, op1=ALU.add))
                then(TT(tmp, o1, o2, ALU.add))
                then(TT(tmp, tmp, pr, ALU.mult))
                then(v.tensor_reduce(s2, tmp, AX.X, ALU.add))
                then(v.reciprocal(s2b, s2))
                then(TT(w, tmp, b2(s2b), ALU.mult))

            dve.wait_ge(setup_mm.sem, 1)
            v.tensor_tensor(t["s_rows"], sc[0][0:NH, 0:REV], t["s_neg"], ALU.add).then_inc(setup_rows.sem, 1)
            dve.wait_ge(setup_mm.sem, 2)
            cadd = const[:, C_CADD:C_CADD + NT * CP].rearrange("p (t a c) -> p t a c", t=NT, a=1)
            cmul = const[:, C_CMUL:C_CMUL + NT * CP].rearrange("p (t a c) -> p t a c", t=NT, a=1)
            v.tensor_tensor(bcmp[:], sc[1][:, 0:NT * NH * CP].rearrange("p (t c h) -> p t h c", t=NT, c=CP),
                            cadd.broadcast_to([P, NT, NH, CP]), ALU.add).then_inc(setup_bc.sem, 1)
            dve.wait_ge(toep_in.sem, 16)

            for l in range(DEPTH):
                for step in STEPS:
                    kind = step[0]
                    if step in SC_AT:
                        i = SC_AT[step]
                        b = sc[i % 2]
                        v.wait_ge(sc_ready.sem, sc_ready.at(l, i + 1))
                    if kind == "win":
                        v.wait_ge(pj_done.sem, pj_done.at(l, PJ_AT[("kcvc",)] + 1))
                        v.wait_ge(cw_in.sem, cw_in.at(l, 96))
                        for a in range(2):
                            for g in range(GROUPS):
                                src = bass.AP(kv2.tensor, kv2[:, a, g, 0:1].offset,
                                              [list(kv2.ap[0]), [2, L2], [NSTRIDE, NC]])
                                ins = v.tensor_tensor(win[:, a, :, g, :], src,
                                                      pos[:, a, :].rearrange("p (l c) -> p l c", c=1).broadcast_to([P, L2, NC]), ALU.add)
                        ins.then_inc(win_ready.sem, 1)
                    elif kind == "VC":
                        blk = const[:, C_BLK:C_BLK + NH].rearrange("p (h d) -> p h d", d=1).broadcast_to([P, NH, HD])
                        v.tensor_tensor(vcz[:], b[:, 0:HD].rearrange("p (h d) -> p h d", h=1).broadcast_to([P, NH, HD]), blk,
                                        ALU.mult).then_inc(sc_done.sem, 1)
                    elif kind == "CS":
                        v.tensor_tensor(scmp[:].rearrange("p n c -> p (n c)"), b[:, 0:NT * NH * CP],
                                        bcmp[:].rearrange("p t h c -> p (t h c)"), ALU.add).then_inc(sc_done.sem, 1)
                        v.wait_ge(sc_done.sem, sc_done.at(l, i + 1))
                        then(v.tensor_reduce(cmax, scmp[:], AX.X, ALU.max))
                        v.tensor_tensor(scmp[:], scmp[:], cmax.rearrange("p (n c) -> p n c", c=1).broadcast_to([P, NT * NH, CP]),
                                        ALU.subtract).then_inc(soft_in.sem, 1)
                    elif kind == "CN":
                        v.wait_ge(exp_done.sem, exp_done.at(l, 1))
                        sview = scmp[:].rearrange("p (t h) c -> p t h c", t=NT)
                        then(v.tensor_tensor(sview, sview, cmul.broadcast_to([P, NT, NH, CP]), ALU.mult))
                        then(v.tensor_reduce(csum, scmp[:], AX.X, ALU.add))
                        then(v.tensor_scalar(csum, csum, 1e-30, None, ALU.max))
                        then(v.reciprocal(crec, csum))
                        v.wait_ge(pj_done.sem, pj_done.at(l, PJ_AT[("gate",)] + 1))
                        then(v.tensor_tensor(crec.rearrange("p (t h) -> p t h", t=NT), crec.rearrange("p (t h) -> p t h", t=NT),
                                             gates[:, :, 0:NG3:3], ALU.mult))
                        v.tensor_tensor(scmp[:], scmp[:], crec.rearrange("p (n c) -> p n c", c=1).broadcast_to([P, NT * NH, CP]),
                                        ALU.mult).then_inc(p_ready.sem, 1)
                    elif kind == "S":
                        h = step[1]
                        for qt in range(NT):
                            i = SC_AT[step + (qt,)]
                            n = (qt + 1) * P
                            o = qt * SEQ
                            v.wait_ge(sc_ready.sem, sc_ready.at(l, i + 1))
                            v.tensor_tensor(sbuf_s[:, o:o + 2 * n].rearrange("p (r k) -> p r k", r=2),
                                            sc[i % 2][:, 0:2 * n].rearrange("p (r k) -> p r k", r=2),
                                            bias[:, h:h + 1, SEQ - n:SEQ].broadcast_to([P, 2, n]), ALU.add).then_inc(sc_done.sem, 1)
                        v.wait_ge(sc_done.sem, sc_done.at(l, i))
                        v.tensor_reduce(nmax[:, 0:2], sbuf_s[:, 0:SEQ].rearrange("p (r k) -> p r k", r=2), AX.X, ALU.max, negate=True)
                        v.wait_ge(sc_done.sem, sc_done.at(l, i + 1))
                        v.tensor_reduce(nmax[:, 2:4], sbuf_s[:, SEQ:3 * SEQ].rearrange("p (r k) -> p r k", r=2), AX.X, ALU.max,
                                        negate=True).then_inc(soft_in.sem, 1)
                    elif kind == "N":
                        h = step[1]
                        v.wait_ge(exp_done.sem, exp_done.at(l, h + 2))
                        then(v.reciprocal(r4, psum4))
                        r22 = r4.rearrange("p (t r) -> p t r", t=NT)
                        then(v.tensor_tensor(r22, r22, gates[:, :, 3 * h + 1:3 * h + 3], ALU.mult))
                        for qt in range(NT):
                            n = (qt + 1) * P
                            s = sbuf_s[:, qt * SEQ:qt * SEQ + 2 * n].rearrange("p (r k) -> p r k", r=2)
                            ins = v.tensor_tensor(s, s, r4[:, 2 * qt:2 * qt + 2].rearrange("p (r k) -> p r k", k=1).broadcast_to([P, 2, n]),
                                                  ALU.mult)
                        ins.then_inc(p_ready.sem, 1)
                    elif kind == "V" and step[1] % 2:
                        i = PV_AT[step]
                        v.wait_ge(pv_ready.sem, pv_ready.at(l, i + 1))
                        v.tensor_copy(yaT[:, step[1] // 2, :], pv[i % 2][:, 0:SEQ]).then_inc(pv_done.sem, 1)
                    elif kind == "rot":
                        r = step[1]
                        half = [P, 2, SEQ]
                        sinb = sinT.rearrange("p (b s) -> p b s", b=1).broadcast_to(half)
                        cosb = cosT.rearrange("p (b s) -> p b s", b=1).broadcast_to(half)
                        v.tensor_tensor(rtmp, b[:].rearrange("p (b s) -> p b s", b=2), sinb, ALU.mult)
                        then(v.tensor_tensor(rsum, rraw[:, r % 2], cosb, ALU.mult))
                        if r < 2:
                            v.wait_ge(zeroed.sem, zeroed.at(l, 4))
                            v.tensor_tensor(qrz[0:64, 4 * r:4 * r + 4:2, :], rtmp[0:64], rsum[0:64], ALU.add)
                            v.tensor_tensor(qrz[64:P, 4 * r + 1:4 * r + 4:2, :], rtmp[64:P], rsum[64:P], ALU.add)\
                                .then_inc(sc_done.sem, 1)
                        else:
                            v.tensor_tensor(krT[:, 2 * (r - 2):2 * (r - 2) + 2, :], rtmp, rsum, ALU.add).then_inc(sc_done.sem, 1)
                        v.wait_ge(sc_done.sem, sc_done.at(l, i + 1))
                    elif kind == "ST":
                        h = step[1]
                        if h >= 2:
                            v.wait_ge(pv_ready.sem, pv_ready.at(l, PV_AT[("Y", h - 2)] + 1))
                        if l == 0 and h == 0:
                            dve.wait_ge(bias_in.sem, 48)
                        s = st[:, h % 2, :]
                        v.tensor_tensor(s[:, 0:SEQ], b[:, 0:SEQ], decay[:, h, :], ALU.mult)
                        v.tensor_tensor(s[:, SEQ:SEQ + P], b[:, SEQ:SEQ + P], decay[:, h, 0:P], ALU.mult).then_inc(sc_done.sem, 1)
                    elif kind == "Y":
                        h = step[1]
                        i = PV_AT[step]
                        v.wait_ge(pv_ready.sem, pv_ready.at(l, i + 1))
                        v.tensor_copy(yraw[:, :, h * P:(h + 1) * P], pv[i % 2][:, 0:SEQ].rearrange("p (t d) -> p t d", t=NT))\
                            .then_inc(pv_done.sem, 1)
                        v.wait_ge(pv_done.sem, pv_done.at(l, i + 1))
                        for tile in range(NT):
                            ins = v.bn_stats(stats[:, tile, h, :], yraw[:, tile, h * P:(h + 1) * P])
                        if h == NH - 1:
                            then(ins)
                    elif kind == "GN":
                        for tile in range(NT):
                            for h in range(NH):
                                ins = v.bn_aggr(mv[:, tile, h, :], stats[:, tile, h, :])
                        then(ins)
                        v.tensor_scalar(vare.rearrange("p (t h) -> p t h", t=NT), mv[:, :, :, 1], LN_EPS, None, ALU.add)\
                            .then_inc(var_ready.sem, 1)
                        v.wait_ge(sqrt_done.sem, sqrt_done.at(l, 1))
                        then(v.reciprocal(rstd, sdev))
                        for tile in range(NT):
                            for h in range(NH):
                                y = yraw[:, tile, h * P:(h + 1) * P]
                                ins = v.tensor_scalar(y, y, mv[:, tile, h, 0:1], rstd[:, tile * NH + h:tile * NH + h + 1],
                                                      ALU.subtract, ALU.mult)
                        then(ins)
                        v.wait_ge(pj_done.sem, pj_done.at(l, PJ_AT[("gr", 1, 1)] + 1))
                        for tile in range(NT):
                            ins = v.tensor_tensor(yb[:, tile, :], yb[:, tile, :], yraw[:, tile, :], ALU.mult)
                        ins.then_inc(yb_ready.sem, 1)
                    elif kind in ("wa", "wb"):
                        j = step[1]
                        m = merged[:, 2 * j:2 * j + 2, :]
                        product = b[:].rearrange("p (b s) -> p b s", b=2)
                        if kind == "wa":
                            v.wait_ge(pj_done.sem, pj_done.at(l, PJ_AT[("ma", j)] + 1))
                            v.tensor_tensor(m, product, m, ALU.mult).then_inc(sc_done.sem, 1)
                        else:
                            v.wait_ge(pj_done.sem, pj_done.at(l, PJ_AT[("mb", j)] + 1))
                            g = gateb[:, 2 * j:2 * j + 2, :]
                            then(v.tensor_tensor(g, product, g, ALU.mult))
                            v.tensor_tensor(m, m, g, ALU.add).then_inc(sc_done.sem, 1)
                    elif kind == "wo":
                        _, c, tile = step
                        xs = x[:, tile, c * 512:(c + 1) * 512]
                        v.scalar_tensor_tensor(out=xs, in0=xs, scalar=ALPHA, in1=b[:], op0=ALU.mult, op1=ALU.add)\
                            .then_inc(sc_done.sem, 1)
                    elif kind == "LN1":
                        v.wait_ge(sc_done.sem, sc_done.at(l, SC_AT[("wo", 1, 1)] + 1))
                        norm(l, 0, lstats)
                    elif kind == "R":
                        v.tensor_copy(rt[:, 6].rearrange("p t e -> p (t e)"), b[:, 0:NT * NE]).then_inc(sc_done.sem, 1)
                        v.wait_ge(sc_done.sem, sc_done.at(l, i + 1))
                        route(l, rt[:, 6])
                        xall = x[:].rearrange("p t d -> p (t d)")
                        v.wait_ge(x_ready.sem, x_ready.at(l, 1))
                        then(v.tensor_scalar(xall, xall, ALPHA, None, ALU.mult))
                w = rt[:, 11]
                with dve.Fori(0, NE // 2) as pair:
                    for u in range(2):
                        def n(per, c):
                            return pair * (2 * per) + per * u + c
                        for tile in range(NT):
                            v.wait_ge(u_ready.sem, u_ready.at(l, n(2, tile + 1)))
                            v.wait_ge(silu_done.sem, silu_done.at(l, n(2, tile + 1)))
                            v.wait_ge(ht_ready.sem, ht_ready.at(l, n(2, tile - 1)))
                            v.scalar_tensor_tensor(out=hh[:, tile, :], in0=hs[:, tile, :], scalar=w[:, tile, bass.ds(pair * 2 + u, 1)],
                                                   in1=pv[tile][:], op0=ALU.mult, op1=ALU.mult).then_inc(h_ready.sem, 1)
                        for tile in range(NT):
                            for half in range(2):
                                v.wait_ge(y_ready.sem, y_ready.at(l, n(4, 2 * tile + half + 1)))
                                v.wait_ge(y_done.sem, y_done.at(l, n(4, 2 * tile + half - 3)))
                                xs = x[:, tile, half * 512:(half + 1) * 512]
                                v.tensor_tensor(xs, xs, sc[half][:], ALU.add).then_inc(y_done.sem, 1)
                v.wait_ge(y_done.sem, y_done.at(l, 4 * NE))
                norm(l, 1, lstats)


def _constants():
    import numpy as np
    f = np.float32

    def bucket(n):
        n = np.maximum(n, 0)
        nf = np.maximum(n, 1).astype(f)
        large = 16 + (np.log(nf / f(16)) / f(np.log(2048 / 16)) * f(16)).astype(np.int32)
        return np.where(n < 16, n, np.minimum(large, 31))

    def onehot(dist):
        return (bucket(dist)[None, :] == np.arange(32)[:, None]).astype(f)
    pack = np.zeros((P, NCONST), f)
    pack[:, C_ID:C_ID + P] = np.eye(P)
    swap = np.zeros((P, P), f)
    for d in range(P):
        if d % 64 < 32:
            swap[d + 32, d] = -1.0
        else:
            swap[d - 32, d] = 1.0
    pack[:, C_SWAP:C_SWAP + P] = swap
    inv = (f(10000.0) ** (-np.arange(32, dtype=f) * f(2.0) / f(64))).astype(f)
    ang = (np.arange(SEQ, dtype=f)[None, :] * inv[:, None]).astype(f)
    pack[:, C_COS:C_COS + SEQ] = np.tile(np.cos(ang), (4, 1))
    pack[:, C_SIN:C_SIN + SEQ] = np.tile(np.sin(ang), (4, 1))
    tok = (np.arange(NT)[None, :, None] * P + np.arange(P)[:, None, None])
    end = np.arange(CP)[None, None, :] * NSTRIDE + NLEN - 1
    ok = (end <= tok) & (np.arange(CP)[None, None, :] < NC)
    pack[:, C_CADD:C_CADD + 32] = np.where(ok, 0, MASKED).reshape(P, 32)
    pack[:, C_CMUL:C_CMUL + 32] = ok.astype(f).reshape(P, 32)
    pack[:, C_BLK:C_BLK + NH] = (np.arange(P)[:, None] // CP == np.arange(NH)[None, :])
    pack[:, C_EIDX:C_EIDX + NE] = NE - np.arange(NE)
    pack[:, C_GIDX:C_GIDX + EG] = EG - np.arange(EG)
    lg = np.log(1.0 - 2.0 ** (-5.0 - np.arange(NH)))
    diff = np.arange(SEQ)[None, :] - np.arange(P)[:, None]
    decay = np.where(diff[:, None, :] >= 0, np.exp(np.maximum(diff, 0)[:, None, :] * lg[None, :, None]), 0.0) * HD ** -0.5
    neg = np.where(np.arange(REV) > SEQ - 1, MASKED, 0.0)
    return {
        "c_pack": pack, "c_decay": decay.astype(f), "c_neg": np.tile(neg, (NH, 1)).astype(f),
        "c_rev": onehot(SEQ - 1 - np.arange(REV)), "c_fwd": onehot(np.arange(FWD) - FWD0),
    }


def launch_program(nc, t):
    build(nc, t)


_INS = ["x", "w_in", "cmp_pos", "cmp_w1", "cmp_w2", "w_br_a", "w_br_b", "w_o", "ln1_g", "ln1_b",
        "w_router", "router_bias", "moe_w_gate", "moe_w_up", "moe_w_down", "ln2_g", "ln2_b", "rel_bias"]


def kernel(**inputs):
    import numpy as np
    import concourse.bacc as bacc
    from concourse import mybir as mb
    from concourse.bass_utils import run_bass_kernel_spmd as run

    nc = bacc.Bacc("TRN2", target_bir_lowering=False, num_devices=1)
    arrays, t = {}, {}
    given = {name: np.ascontiguousarray(inputs[name]) for name in _INS}
    given.update(_constants())
    given["cmp_pos"] = np.ascontiguousarray(given["cmp_pos"].reshape(DEPTH, 2, L2, 2 * HD).transpose(0, 1, 3, 2))
    for name, a in given.items():
        arrays[f"in_{name}"] = a
        t[name] = nc.dram_tensor(f"in_{name}", a.shape, mb.dt.from_np(a.dtype), kind="ExternalInput").ap()
    t["out"] = nc.dram_tensor("out_0", (1, SEQ, D), mb.dt.float32, kind="ExternalOutput").ap()
    launch_program(nc, t)
    r = run(nc, [arrays], core_ids=[0])
    return r.results[0]["out_0"]
```

```python
import concourse.bass as bass
from concourse import mybir
from contextlib import ExitStack

F32 = mybir.dt.float32
ALU = mybir.AluOpType
ACT = mybir.ActivationFunctionType
AX = mybir.AxisListType

P = 128
D = 1024
SEQ = 256
DEPTH = 2
NT = SEQ // P
KD = D // P
NH = 8
HD = 64
GROUPS = 2
HPG = NH // GROUPS
NSTRIDE, NLEN = 16, 32
NC = (SEQ - NLEN) // NSTRIDE + 1
CP = 16
L2 = NLEN // 2
NE = 16
EG = 4
FE = 512
NG3 = 3 * NH
ALPHA = float((2 * DEPTH) ** 0.25)
LN_EPS = 1e-5
MASKED = -1e30

SLOT = KD * 512
RING = 6
O_Q, O_KC, O_KW = 0, 512, 1024
O_QR, O_KR, O_VR, O_GR, O_MA, O_MB = 1304, 1816, 2328, 3352, 4376, 5400
ROW = 6424
CHUNKS = [("in", O_Q, 512), ("in", O_KC, 512), ("in", O_KW, 280), ("in", O_QR, 512), ("in", O_KR, 512),
          ("in", O_VR, 512), ("in", O_VR + 512, 512), ("in", O_GR, 512), ("in", O_GR + 512, 512),
          ("in", O_MA, 512), ("in", O_MA + 512, 512), ("br_a", 0, 1024),
          ("in", O_MB, 512), ("in", O_MB + 512, 512), ("br_b", 0, 512), ("br_b", 512, 512),
          ("o", 0, 512), ("o", 512, 512)]
NCH = len(CHUNKS)
USES = NCH // RING
SLOTS = 64
PAIRS = NE // 2

STEPS = [("xT", t, c) for t in range(NT) for c in range(2)]
STEPS += [("q", 0), ("q", 1), ("kcvc",), ("ksvs",), ("kwvw",), ("gate",), ("win",), ("S", 0), ("qr", 0), ("N", 0), ("H",),
          ("qr", 1), ("KC",), ("VC",), ("CS",), ("S", 1), ("CN",), ("rot", 0), ("kr", 0), ("rot", 1), ("N", 1), ("CT",)]
_side = [("kr", 1)] + [("vr", c, t) for c in range(2) for t in range(NT)] \
    + [("gr", c, t) for c in range(2) for t in range(NT)]
for _h in range(NH):
    STEPS += [("T", _h)] + ([("S", _h + 2)] if _h < NH - 2 else []) + [_side[_h]]
    if _h < 2:
        STEPS += [("rot", _h + 2)]
    STEPS += [("V", _h)] + ([("N", _h + 2)] if _h < NH - 2 else [])
STEPS += [_side[8], ("ST", 0)]
_side = [("ma", i) for i in range(4)] + [("wa", i) for i in range(4)]
for _h in range(NH):
    STEPS += [_side[_h]] + ([("ST", _h + 1)] if _h < NH - 1 else []) + [("Y", _h)]
STEPS += [("GN",)] + [("mb", i) for i in range(4)]
STEPS += [("ybT", t, c) for t in range(NT) for c in range(2)]
STEPS += [("wb", i) for i in range(4)]
for _t in range(NT):
    STEPS += [("wo", c, _t) for c in range(2)] + [("LN1", _t)]
for _t in range(NT):
    STEPS += [("x1T", _t, c) for c in range(2)] + [("R", _t)]
STEPS += [("route",), ("K",)]
SOFT_AT = {s: i for i, s in enumerate([s for s in STEPS if s[0] in ("S", "CS", "route")])}
EXP_AT = {s: i for i, s in enumerate([s for s in STEPS if s[0] in ("N", "CN", "route")])}

CHUNK_OF = {"q": 0, "kcvc": 1, "ksvs": 1, "kwvw": 2, "gate": 2, "qr": 3, "kr": 4}
PJ = [s for s in STEPS if s[0] in ("q", "kcvc", "ksvs", "kwvw", "gate", "qr", "kr", "vr", "gr", "ma", "mb", "H", "KC")]
TP, SC, PV = [], [], []
for _s in STEPS:
    if _s[0] in ("xT", "CT", "ybT", "x1T"):
        TP.append(_s)
    if _s[0] == "T":
        TP += [_s + (0,), _s + (1,)]
    if _s[0] in ("CS", "VC", "rot", "ST", "wa", "wb", "wo", "R", "K"):
        SC.append(_s)
    if _s[0] == "S":
        SC += [_s + (0,), _s + (1,)]
    if _s[0] == "Y" or (_s[0] == "V" and _s[1] % 2):
        PV.append(_s)
PJ_AT = {s: i for i, s in enumerate(PJ)}
TP_AT = {s: i for i, s in enumerate(TP)}
SC_AT = {s: i for i, s in enumerate(SC)}
PV_AT = {s: i for i, s in enumerate(PV)}

C_ID, C_SWAP, C_COS, C_SIN, C_CADD, C_CMUL, C_BLK, C_EIDX, C_GIDX = 0, 128, 256, 512, 768, 800, 832, 840, 856
C_TRI, C_ONES, C_IOTA = 860, 988, 1116
NCONST = 1180
FWD, FWD0, REV = 528, 272, 384


class Signal:

    def __init__(self, sem, per_layer, credit=0):
        self.sem, self.per_layer, self.credit = sem, per_layer, credit

    def at(self, l, n):
        return l * self.per_layer + n + self.credit

    def after(self, n):
        return n + self.credit


def build(nc, t):
    with ExitStack() as ctx:
        def sb(name, *shape):
            return ctx.enter_context(nc.sbuf_tensor(name, [P, *shape], F32))

        def bank(name):
            return ctx.enter_context(nc.psum_tensor(name, [P, 512], F32))

        def sem(name, per_layer=0, credit=0):
            return Signal(ctx.enter_context(nc.semaphore(name)), per_layer, credit)

        ring = sb("ring", RING, SLOT)
        x = sb("x", NT, D)
        xT = sb("xT", KD, SEQ)
        merged = sb("merged", KD, SEQ)
        qz = merged
        ybT = sb("ybT", KD, SEQ)
        qrz = ybT
        lnw = sb("lnw", 2, D)
        krT = lnw[:, 0, :].rearrange("p (b s) -> p b s", s=SEQ)
        yaT = lnw[:, 1, :].rearrange("p (b s) -> p b s", s=SEQ)
        vr = sb("vr", NT, D)
        gateb = vr[:].rearrange("p t d -> p (t d)").rearrange("p (b s) -> p b s", s=SEQ)
        yb = sb("yb", NT, D)
        yraw = sb("yraw", NT, D)
        bias = sb("bias", NH, SEQ)
        decay = sb("decay", NH, SEQ)
        kTd = sb("kTd", GROUPS, 2, SEQ)
        vn = sb("vn", NT, 2, P)
        sbuf_s = sb("scores", 768)
        pT = sb("pT", 768)
        const = sb("const", NCONST)
        wrt = sb("wrt", KD, NE)
        bcmp = sb("bcmp", NT, NH, CP)
        scmp = sb("scmp", NT * NH, CP)
        pcT = sb("pcT", SEQ)
        vcz = sb("vcz", NH, HD)
        kcd = sb("kcd", GROUPS, CP)
        gk = sb("gk", GROUPS, NC)
        gv = sb("gv", GROUPS, HPG, CP)
        gates = sb("gates", NT, NG3)
        w2 = sb("w2", HD)
        pos = sb("pos", 2, L2)
        small = sb("small", 512)
        cmpw = vr[:].rearrange("p a d -> p (a d)").rearrange("p (v l m) -> p v l m", v=2, l=L2)
        yflat = yraw[:].rearrange("p t d -> p (t d)")
        kv2 = yflat[:, 0:1024].rearrange("p (v g s) -> p v g s", v=2, g=GROUPS)
        win = yflat[:, 1024:1024 + 2 * L2 * 30].rearrange("p (v l g c) -> p v l g c", v=2, l=L2, g=GROUPS)
        ybf = yb[:].rearrange("p t d -> p (t d)")
        rraw = ybf[:, 0:1024].rearrange("p (u b s) -> p u b s", u=2, b=2)
        rtmp = ybf[:, 1024:1536].rearrange("p (b s) -> p b s", b=2)
        rsum = ybf[:, 1536:2048].rearrange("p (b s) -> p b s", b=2)
        st = sbuf_s[:].rearrange("p (u n) -> p u n", u=2)
        scores = [sbuf_s[:], yflat[:, 0:768]]
        hs = ybf[:, 0:FE]
        hh = ybf[:, FE:2 * FE]
        hT = ybf[:, 2 * FE:3 * FE].rearrange("p (f s) -> p f s", s=P)
        xg = yflat[:, 0:D].rearrange("p (k s) -> p k s", s=P)
        vflat = vr[:].rearrange("p t d -> p (t d)")
        ysb = vflat[:, 0:D]
        disp = vflat[:, D:D + 256].rearrange("p (t e s) -> p t e s", t=NT, e=2)
        dispw = vflat[:, D + 256:D + 512].rearrange("p (t e s) -> p t e s", t=NT, e=2)
        dispwT = vflat[:, D + 512:D + 768]
        acc = merged[:].rearrange("p k s -> p (k s)").rearrange("p (t d) -> p t d", t=NT)
        key = sb("key", NT, NE + 2)
        wpad = sb("wpad", NT, NE + 2)
        passes_sb = ctx.enter_context(nc.sbuf_tensor("passes", [P, 1], mybir.dt.int32))
        for name, rows_, o, n in (("s_rel4", P, 0, 4 * NH), ("s_rev", 32, 40, REV), ("s_fwd", P, 440, FWD),
                                  ("s_neg", NH, 1000, REV), ("s_rows", NH, 1400, REV)):
            t[name] = ybf[0:rows_, o:o + n]
        t["s_rb"] = sb("router_bias_rows", NE)[:]
        ident = const[:, C_ID:C_ID + P]
        cosT = const[:, C_COS:C_COS + SEQ]
        sinT = const[:, C_SIN:C_SIN + SEQ]

        at = [0]

        def piece(n):
            at[0] += n
            return small[:, at[0] - n:at[0]]
        nmax, psum4, r4 = piece(4), piece(4), piece(4)
        cmax, csum, crec = piece(16), piece(16), piece(16)
        stats = piece(NT * NH * 6).rearrange("p (t h n) -> p t h n", t=NT, h=NH)
        mv = piece(NT * NH * 2).rearrange("p (t h n) -> p t h n", t=NT, h=NH)
        vare, sdev, rstd = piece(16), piece(16), piece(16)
        lstats = piece(24).rearrange("p (t c n) -> p t c n", t=NT, c=2)
        lmv = piece(4).rearrange("p (t n) -> p t n", t=NT)
        rt = sb("rt", 12, NT, NE)
        npf = sb("passes_float", 4)

        pj = [bank(f"pj{i}") for i in range(2)]
        tp = [bank(f"tp{i}") for i in range(2)]
        sc = [bank(f"sc{i}") for i in range(2)]
        pv = [bank(f"pv{i}") for i in range(2)]

        landed = [sem(f"landed{i}", 32 * USES) for i in range(RING)]
        landed_e = [sem(f"landed_expert{i}") for i in range(RING)]
        consts_in, setup_in, rel_in, x_in = sem("consts_in"), sem("setup_in"), sem("rel_in"), sem("x_in")
        rows_out, bias_in, toep_in = sem("rows_out"), sem("bias_in"), sem("toep_in")
        setup_mm, setup_rows, setup_bc, zero_once = sem("setup_mm"), sem("setup_rows"), sem("setup_bc"), sem("zero_once")
        cw_in, lnw_in = sem("cw_in", 96), sem("lnw_in", 64)
        zeroed = sem("zeroed", 4)
        pj_ready, pj_done = sem("pj_ready", len(PJ)), sem("pj_done", len(PJ))
        tp_ready, tp_done = sem("tp_ready", len(TP)), sem("tp_done", len(TP))
        sc_ready, sc_done = sem("sc_ready", len(SC)), sem("sc_done", len(SC))
        pv_ready, pv_done = sem("pv_ready", len(PV)), sem("pv_done", len(PV))
        win_ready, soft_in, exp_done, p_ready = sem("win_ready", 1), sem("soft_in", len(SOFT_AT)), sem("exp_done", len(EXP_AT)), sem("p_ready", len(EXP_AT) - 1)
        var_ready, sqrt_done, yb_ready, x_ready = sem("var_ready", 5), sem("sqrt_done", 5), sem("yb_ready", 1), sem("x_ready", 4)
        passes_ready, oh_ready = sem("passes_ready", 1), sem("oh_ready", 1)
        disp_made, disp_ready, key_moved = sem("disp_made"), sem("disp_ready"), sem("key_moved")
        xg_ready, xg_done = sem("xg_ready", 0, 2), sem("xg_done")
        g_ready, u_ready, silu_done, h_ready = sem("g_ready"), sem("u_ready"), sem("silu_done"), sem("h_ready")
        dt_ready, dt_done = sem("dt_ready", 0, 1), sem("dt_done", 0, 1)
        ht_ready, ht_done = sem("ht_ready"), sem("ht_done", 0, 1)
        y_ready, y_done = sem("y_ready"), sem("y_done", 0, 2)
        c_ready, acc_done = sem("c_ready"), sem("acc_done", 0, 4)
        dve_step, sp_paced, pe_paced, dve_paced = sem("dve_step"), sem("sp_paced"), sem("pe_paced"), sem("dve_paced")
        out_done = sem("out_done")

        rows_dram = nc.dram_tensor("bias_rows", [NH, REV], F32)
        PITCH = REV + P
        SHIFTED = PITCH * P + P
        shift_dram = nc.dram_tensor("bias_shifted", [NH, SHIFTED], F32)
        shift_out = sem("shift_out")

        def w_in(l, o, n):
            return t["w_in"][l].rearrange("(k p) n -> p k n", p=P)[:, :, o:o + n]

        def chunk_source(l, n):
            kind, o, width = CHUNKS[n]
            if kind == "in":
                return w_in(l, o, width), KD * width
            if kind == "br_a":
                return t["w_br_a"][l].rearrange("(k p) n -> p k n", p=P), 4 * D
            name = "w_br_b" if kind == "br_b" else "w_o"
            return t[name][l].rearrange("(k p) n -> p k n", p=P)[:, :, o:o + width], KD * width

        def slot(n, k, width):
            return ring[:, n % RING, 0:k * width].rearrange("p (k n) -> p k n", k=k)

        def weights_in(eng, l, n):
            eng.wait_ge(landed[n % RING].sem, landed[n % RING].at(l, 32 * (n // RING + 1)))

        LAST = {0: ("q", 1), 1: ("ksvs",), 2: ("gate",), 3: ("qr", 1), 4: ("kr", 1), 5: ("vr", 0, 1), 6: ("vr", 1, 1),
                7: ("gr", 0, 1), 8: ("gr", 1, 1), 9: ("ma", 1), 10: ("ma", 3), 11: ("wa", 3), 12: ("mb", 1),
                13: ("mb", 3), 14: ("wb", 1), 15: ("wb", 3), 16: ("wo", 0, 1), 17: ("wo", 1, 1)}

        def wait_chunk_used(eng, l, n):
            if LAST[n] in PJ_AT:
                eng.wait_ge(pj_ready.sem, pj_ready.at(l, PJ_AT[LAST[n]] + 1))
            else:
                eng.wait_ge(sc_ready.sem, sc_ready.at(l, SC_AT[LAST[n]] + 1))

        block = ctx.enter_context(nc.Block())

        @block.sync
        def _(sp):
            def load(n, dst_floats, src, k, width):
                dst = slot(n, k, width)
                for a in (0, 64):
                    sp.dma_start(dst[a:a + 64], src[a:a + 64]).then_inc(landed[n % RING].sem, 16)

            def load_expert(l, i, e, u):
                src = t[("moe_w_gate", "moe_w_up", "moe_w_down")[i]][l].rearrange("e a b -> (e a) b")
                rows, width = (D, FE) if i < 2 else (FE, D)
                src = src[bass.ds(e * rows, rows), :].rearrange("(k p) n -> p k n", p=P)
                dst = slot(2 * i + u, rows // P, width)
                for a in (0, 64):
                    sp.dma_start(dst[a:a + 64], src[a:a + 64]).then_inc(landed_e[2 * i + u].sem, 16)

            def load_pair(l, pair, before):
                for i, freed in enumerate((g_ready, u_ready, y_ready)):
                    sp.wait_ge(freed.sem, freed.after(before * (2 if i == 2 else 1)))
                    sp.sem_inc(sp_paced.sem, 1)
                    for u in range(2):
                        load_expert(l, i, pair * 2 + u, u)

            pairs_before = 0
            for l in range(DEPTH):
                for n in range(NCH):
                    if n >= RING:
                        wait_chunk_used(sp, l, n - RING)
                    elif l > 0 and n % 2 == 0:
                        freed = (g_ready, u_ready, y_ready)[n // 2]
                        sp.wait_ge(freed.sem, freed.after(pairs_before * (2 if n == 4 else 1)))
                        sp.sem_inc(sp_paced.sem, 1)
                    if l == 0 and n == 0:
                        for tile in range(NT):
                            sp.dma_start(x[:, tile, :], t["x"][0, tile * P:(tile + 1) * P, :]).then_inc(x_in.sem, 16)
                    src, floats = chunk_source(l, n)
                    load(n, floats, src, *((4, D) if CHUNKS[n][0] == "br_a" else (KD, CHUNKS[n][2])))
                for i in range(3):
                    for u in range(2):
                        wait_chunk_used(sp, l, NCH - RING + 2 * i + u)
                        load_expert(l, i, u, u)
                with sp.Fori(1, PAIRS) as pair:
                    load_pair(l, pair, sp.snap(pairs_before + pair))
                sp.wait_ge(passes_ready.sem, passes_ready.at(l, 1))
                passes = sp.value_load(passes_sb[0:1, 0:1], min_val=1, max_val=SEQ // SLOTS)
                with sp.If(passes > 1):
                    with sp.Fori(1, passes) as r:
                        with sp.Fori(0, PAIRS) as pair:
                            load_pair(l, pair, sp.snap(pairs_before + r * PAIRS + pair))
                pairs_before = sp.snap(pairs_before + passes * PAIRS)
            for tile in range(NT):
                sp.wait_ge(x_ready.sem, x_ready.at(DEPTH - 1, 3 + tile))
                sp.dma_start(t["out"][0, tile * P:(tile + 1) * P, :], x[:, tile, :]).then_inc(out_done.sem, 16)
            sp.wait_ge(out_done.sem, 32)

        @block.gpsimd
        def _(pool):
            def zero_halves(l, buf, n):
                for i, (rows, first) in enumerate(((slice(64, P), 0), (slice(0, 64), 1))):
                    pool.memset(buf[rows, first:NH:2, :], 0.0).then_inc(zeroed.sem, 1)
                    pool.wait_ge(zeroed.sem, zeroed.at(l, n + i + 1))

            pool.memset(t["s_rel4"], 0.0).then_inc(zero_once.sem, 1)
            pool.memset(kcd[:], 0.0).then_inc(zero_once.sem, 1)
            pool.memset(gv[:], 0.0).then_inc(zero_once.sem, 1)
            pool.wait_ge(zero_once.sem, 1)
            for j in range(4):
                pool.dma_start(t["s_rel4"][32 * j:32 * j + 32, NH * j:NH * j + NH], t["rel_bias"]).then_inc(rel_in.sem, 16)
            pool.wait_ge(zero_once.sem, 3)
            for l in range(DEPTH):
                if l == 0:
                    zero_halves(l, qz, 0)
                    pool.wait_ge(setup_rows.sem, 1)
                    pool.dma_start(rows_dram[:, :], t["s_rows"]).then_inc(rows_out.sem, 16)
                    zero_halves(l, qrz, 2)
                    pool.wait_ge(rows_out.sem, 16)
                    pool.dma_start(bass.AP(shift_dram, 0, [[PITCH + 1, P], [SHIFTED, NH], [1, REV]]),
                                   bass.AP(rows_dram, 0, [[0, P], [REV, NH], [1, REV]])).then_inc(shift_out.sem, 16)
                    pool.wait_ge(shift_out.sem, 16)
                    pool.dma_start(bias[:], bass.AP(shift_dram, P - 1, [[PITCH, P], [SHIFTED, NH], [1, SEQ]])).then_inc(toep_in.sem, 16)
                else:
                    pool.wait_ge(x_ready.sem, x_ready.at(l - 1, 4))
                    zero_halves(l, qz, 0)
                for v in range(2):
                    pool.dma_start(cmpw[:, v], t["cmp_w1"][l, v].rearrange("(l q) m -> q l m", q=P)).then_inc(cw_in.sem, 16)
                    pool.dma_start(w2[64 * v:64 * v + 64, :], t["cmp_w2"][l, v]).then_inc(cw_in.sem, 16)
                    pool.dma_start(pos[:, v, :], t["cmp_pos"][l, v]).then_inc(cw_in.sem, 16)
                if l == 0:
                    pool.dma_start(wrt[:], t["w_router"].rearrange("(k p) e -> p k e", p=P)).then_inc(bias_in.sem, 16)
                    pool.dma_start(t["s_rb"], t["router_bias"].rearrange("(a e) -> a e", a=1).broadcast_to([P, NE])).then_inc(bias_in.sem, 16)
                    pool.dma_start(decay[:], t["c_decay"]).then_inc(bias_in.sem, 16)
                else:
                    zero_halves(l, qrz, 2)
                pool.wait_ge(sc_ready.sem, sc_ready.at(l, SC_AT[("wa", 3)] + 1))
                for i, name in enumerate(("ln1_g", "ln1_b")):
                    pool.dma_start(lnw[:, i, :], t[name][l:l + 1, :].broadcast_to([P, D])).then_inc(lnw_in.sem, 16)
                pool.wait_ge(x_ready.sem, x_ready.at(l, 2))
                for i, name in enumerate(("ln2_g", "ln2_b")):
                    pool.dma_start(lnw[:, i, :], t[name][l:l + 1, :].broadcast_to([P, D])).then_inc(lnw_in.sem, 16)

        @block.tensor
        def _(pe):
            mm = pe.matmul
            pe.sem_inc(xg_ready.sem, xg_ready.credit)
            pe.sem_inc(dt_ready.sem, dt_ready.credit)

            def take(banks, done, index, l, step):
                i = index[step]
                pe.wait_ge(done.sem, done.at(l, max(i - 1, 0)))
                return banks[i % 2]

            def columns(l, step, bankap, chunk, col, off):
                w = slot(chunk, KD, CHUNKS[chunk][2])
                for k in range(KD):
                    ins = mm(bankap[:, off:off + SEQ], w[:, k, col:col + P], xT[:, k, :], start=(k == 0), stop=(k == KD - 1))
                return ins

            def rows(tile, out, chunk, col, width, lhs=None):
                w = slot(chunk, KD, CHUNKS[chunk][2])
                lhs = xT if lhs is None else lhs
                for k in range(KD):
                    ins = mm(out, lhs[:, k, tile * P:(tile + 1) * P], w[:, k, col:col + width],
                             start=(k == 0), stop=(k == KD - 1))
                return ins

            def bias_products():
                pe.wait_ge(rel_in.sem, 64)
                pe.wait_ge(setup_in.sem, 48)
                mm(sc[0][0:NH, 0:REV], t["s_rel4"][0:32, 0:NH], t["s_rev"], start=True, stop=True).then_inc(setup_mm.sem, 1)
                for qt in range(NT):
                    for c in range(0, CP, 4):
                        o = FWD0 + qt * P - NSTRIDE * c - (NLEN - 1)
                        ins = mm(sc[1][:, (qt * CP + c) * NH:(qt * CP + c + 4) * NH], t["s_fwd"][:, o:o + P], t["s_rel4"],
                                 start=True, stop=True)
                ins.then_inc(setup_mm.sem, 1)

            pairs_before = gathers_before = 0
            for l in range(DEPTH):
                for step in STEPS:
                    kind = step[0]
                    if kind in ("xT", "x1T", "ybT"):
                        _, tile, c = step
                        if c == 0:
                            if kind == "ybT":
                                pe.wait_ge(yb_ready.sem, yb_ready.at(l, 1))
                            elif kind == "x1T":
                                pe.wait_ge(x_ready.sem, x_ready.at(l, 1 + tile))
                            elif l == 0:
                                pe.wait_ge(consts_in.sem, 16)
                                pe.wait_ge(x_in.sem, 32)
                            else:
                                pe.wait_ge(x_ready.sem, x_ready.at(l - 1, 3 + tile))
                        src = yb if kind == "ybT" else x
                        b = take(tp, tp_done, TP_AT, l, step)
                        for i in range(4):
                            ins = pe.transpose(b[:, i * P:(i + 1) * P], src[:, tile, (4 * c + i) * P:(4 * c + i + 1) * P], ident)
                        ins.then_inc(tp_ready.sem, 1)
                        if l == 0 and step == ("xT", NT - 1, 1):
                            bias_products()
                    elif kind in ("q", "qr", "kr", "ma", "mb"):
                        i = step[1]
                        chunk = CHUNK_OF[kind] if kind in CHUNK_OF else (9 if kind == "ma" else 12) + i // 2
                        first = i % 2 == 0
                        if first:
                            weights_in(pe, l, chunk)
                        if kind == "q" and i == 0:
                            pe.wait_ge(tp_done.sem, tp_done.at(l, TP_AT[("xT", 1, 1)] + 1))
                        b = take(pj, pj_done, PJ_AT, l, step)
                        columns(l, step, b, chunk, (i % 2) * SEQ, 0)
                        columns(l, step, b, chunk, (i % 2) * SEQ + P, SEQ).then_inc(pj_ready.sem, 1)
                    elif kind == "kcvc":
                        weights_in(pe, l, 1)
                        b = take(pj, pj_done, PJ_AT, l, step)
                        columns(l, step, b, 1, 0, 0)
                        columns(l, step, b, 1, P, SEQ).then_inc(pj_ready.sem, 1)
                    elif kind in ("ksvs", "kwvw"):
                        chunk, col = (1, 2 * P) if kind == "ksvs" else (2, 0)
                        weights_in(pe, l, chunk)
                        b = take(pj, pj_done, PJ_AT, l, step)
                        columns(l, step, b, chunk, col, 0)
                        rows(0, b[:, SEQ:SEQ + P], chunk, col + P, P)
                        rows(1, b[:, SEQ + P:SEQ + 2 * P], chunk, col + P, P).then_inc(pj_ready.sem, 1)
                    elif kind == "gate":
                        b = take(pj, pj_done, PJ_AT, l, step)
                        rows(0, b[:, 0:NG3], 2, 2 * P, NG3)
                        rows(1, b[:, NG3:2 * NG3], 2, 2 * P, NG3).then_inc(pj_ready.sem, 1)
                    elif kind in ("vr", "gr"):
                        _, c, tile = step
                        chunk = (5 if kind == "vr" else 7) + c
                        if tile == 0:
                            weights_in(pe, l, chunk)
                        b = take(pj, pj_done, PJ_AT, l, step)
                        rows(tile, b[:], chunk, 0, 512).then_inc(pj_ready.sem, 1)
                    elif kind == "H":
                        pe.wait_ge(win_ready.sem, win_ready.at(l, 1))
                        b = take(pj, pj_done, PJ_AT, l, step)
                        for i in range(L2):
                            for v in range(2):
                                ins = mm(b[64 * v:64 * v + 64, 0:2 * NC], cmpw[:, v, i, :],
                                         win[:, v, i].rearrange("p g c -> p (g c)"), start=(i == 0), stop=(i == L2 - 1))
                        ins.then_inc(pj_ready.sem, 1)
                    elif kind == "KC":
                        pe.wait_ge(pj_done.sem, pj_done.at(l, PJ_AT[("H",)] + 1))
                        b = take(pj, pj_done, PJ_AT, l, step)
                        for g in range(GROUPS):
                            for a in (0, 64):
                                ins = mm(b[a:a + 64, g * NC:(g + 1) * NC], w2[0:64, :], gk[0:64, g, :], start=True, stop=True)
                        ins.then_inc(pj_ready.sem, 1)
                    elif kind == "VC":
                        b = take(sc, sc_done, SC_AT, l, step)
                        mm(b[:, 0:HD], gv[64:P].rearrange("p g r c -> p (g r c)"), w2[64:P, :],
                           start=True, stop=True).then_inc(sc_ready.sem, 1)
                    elif kind == "CS":
                        pe.wait_ge(pj_done.sem, pj_done.at(l, PJ_AT[("KC",)] + 1))
                        b = take(sc, sc_done, SC_AT, l, step)
                        for qt in range(NT):
                            for h in range(NH):
                                o = (qt * NH + h) * CP
                                ins = mm(b[:, o:o + CP], qz[:, h, qt * P:(qt + 1) * P], kcd[:, h // HPG, :], start=True, stop=True)
                        ins.then_inc(sc_ready.sem, 1)
                    elif kind == "S":
                        h = step[1]
                        if h == 0:
                            pe.wait_ge(pj_done.sem, pj_done.at(l, PJ_AT[("kwvw",)] + 1))
                            pe.wait_ge(zeroed.sem, zeroed.at(l, 2))
                            if l == 0:
                                pe.wait_ge(setup_bc.sem, 1)
                        for qt in range(NT):
                            b = take(sc, sc_done, SC_AT, l, step + (qt,))
                            n = (qt + 1) * P
                            mm(b[:, 0:2 * n].rearrange("p (r k) -> p r k", r=2), qz[:, h, qt * P:(qt + 1) * P],
                               kTd[:, h // HPG, :, 0:n], start=True, stop=True).then_inc(sc_ready.sem, 1)
                    elif kind == "rot":
                        i = step[1]
                        src = ("qr", "kr")[i // 2], i % 2
                        pe.wait_ge(pj_done.sem, pj_done.at(l, PJ_AT[src] + 1))
                        b = take(sc, sc_done, SC_AT, l, step)
                        mm(b[:], const[:, C_SWAP:C_SWAP + P], rraw[:, i % 2].rearrange("p b s -> p (b s)"),
                           start=True, stop=True).then_inc(sc_ready.sem, 1)
                    elif kind == "CT":
                        pe.wait_ge(p_ready.sem, p_ready.at(l, EXP_AT[("CN",)] + 1))
                        b = take(tp, tp_done, TP_AT, l, step)
                        for qt in range(NT):
                            ins = pe.transpose(b[:, qt * P:(qt + 1) * P],
                                               scmp[:, qt * NH:(qt + 1) * NH, :].rearrange("p h c -> p (h c)"), ident)
                        ins.then_inc(tp_ready.sem, 1)
                    elif kind == "T":
                        h = step[1]
                        pe.wait_ge(p_ready.sem, p_ready.at(l, EXP_AT[("N", h)] + 1))
                        s = scores[h % 2]
                        b = take(tp, tp_done, TP_AT, l, step + (0,))
                        for r in range(2):
                            pe.transpose(b[:, r * SEQ:r * SEQ + P], s[:, r * P:(r + 1) * P], ident)
                            ins = pe.transpose(b[:, r * SEQ + P:(r + 1) * SEQ], s[:, SEQ + r * SEQ:SEQ + r * SEQ + P], ident)
                        ins.then_inc(tp_ready.sem, 1)
                        b = take(tp, tp_done, TP_AT, l, step + (1,))
                        for r in range(2):
                            ins = pe.transpose(b[:, r * P:(r + 1) * P], s[:, SEQ + r * SEQ + P:SEQ + (r + 1) * SEQ], ident)
                        ins.then_inc(tp_ready.sem, 1)
                    elif kind == "V":
                        h = step[1]
                        i = PV_AT[("V", h | 1)]
                        if h % 2 == 0:
                            pe.wait_ge(pv_done.sem, pv_done.at(l, max(i - 1, 0)))
                        pe.wait_ge(tp_done.sem, tp_done.at(l, TP_AT[("T", h, 1)] + 1))
                        if h == 0:
                            pe.wait_ge(sc_done.sem, sc_done.at(l, SC_AT[("VC",)] + 1))
                        o = pv[i % 2][64 * (h % 2):64 * (h % 2) + 64, :]
                        g = h // HPG
                        mm(o[:, 0:SEQ], vcz[:, h, :], pcT[:], start=True, stop=False, skip_group_check=True)
                        for r in range(2):
                            mm(o[:, 0:SEQ], vn[:, 0, r, g * HD:(g + 1) * HD], pT[:, r * SEQ:(r + 1) * SEQ],
                               start=False, stop=False, skip_group_check=True)
                        for r in range(2):
                            ins = mm(o[:, P:SEQ], vn[:, 1, r, g * HD:(g + 1) * HD], pT[:, 512 + r * P:512 + (r + 1) * P],
                                     start=False, stop=(r == 1), skip_group_check=True)
                        if h % 2:
                            ins.then_inc(pv_ready.sem, 1)
                    elif kind == "ST":
                        h = step[1]
                        if h == 0:
                            pe.wait_ge(sc_done.sem, sc_done.at(l, SC_AT[("rot", 3)] + 1))
                        b = take(sc, sc_done, SC_AT, l, step)
                        mm(b[:, 0:SEQ], krT[:, h // 2, 0:P], qrz[:, h, :], start=True, stop=True)
                        mm(b[:, SEQ:SEQ + P], krT[:, h // 2, P:SEQ], qrz[:, h, P:SEQ], start=True, stop=True)\
                            .then_inc(sc_ready.sem, 1)
                    elif kind == "Y":
                        h = step[1]
                        if h == 0:
                            pe.wait_ge(pj_done.sem, pj_done.at(l, PJ_AT[("vr", 1, 1)] + 1))
                        pe.wait_ge(sc_done.sem, sc_done.at(l, SC_AT[("ST", h)] + 1))
                        b = take(pv, pv_done, PV_AT, l, step)
                        s = st[:, h % 2, :]
                        v = [vr[:, j, h * P:(h + 1) * P] for j in range(NT)]
                        mm(b[:, 0:P], s[:, 0:P], v[0], start=True, stop=True)
                        mm(b[:, P:SEQ], s[:, P:SEQ], v[0], start=True, stop=False)
                        mm(b[:, P:SEQ], s[:, SEQ:SEQ + P], v[1], start=False, stop=True).then_inc(pv_ready.sem, 1)
                    elif kind in ("wa", "wb"):
                        i = step[1]
                        if kind == "wa":
                            w, rhs, nk, col = slot(11, 4, D), yaT, 4, 2 * i * P
                            if i == 0:
                                weights_in(pe, l, 11)
                                pe.wait_ge(pv_done.sem, pv_done.at(l, PV_AT[("V", NH - 1)] + 1))
                        else:
                            w, rhs, nk, col = slot(14 + i // 2, KD, 512), ybT, KD, 2 * (i % 2) * P
                            if i % 2 == 0:
                                weights_in(pe, l, 14 + i // 2)
                            if i == 0:
                                pe.wait_ge(tp_done.sem, tp_done.at(l, TP_AT[("ybT", 1, 1)] + 1))
                        b = take(sc, sc_done, SC_AT, l, step)
                        for j in range(2):
                            for k in range(nk):
                                ins = mm(b[:, j * SEQ:(j + 1) * SEQ], w[:, k, col + j * P:col + (j + 1) * P], rhs[:, k, :],
                                         start=(k == 0), stop=(k == nk - 1))
                        ins.then_inc(sc_ready.sem, 1)
                    elif kind == "wo":
                        _, c, tile = step
                        if tile == 0:
                            weights_in(pe, l, 16 + c)
                        if c == 0 and tile == 0:
                            pe.wait_ge(sc_done.sem, sc_done.at(l, SC_AT[("wb", 3)] + 1))
                        b = take(sc, sc_done, SC_AT, l, step)
                        rows(tile, b[:], 16 + c, 0, 512, merged).then_inc(sc_ready.sem, 1)
                    elif kind == "R":
                        tile = step[1]
                        pe.wait_ge(tp_done.sem, tp_done.at(l, TP_AT[("x1T", tile, 1)] + 1))
                        if l == 0 and tile == 0:
                            pe.wait_ge(bias_in.sem, 48)
                        b = take(sc, sc_done, SC_AT, l, step)
                        for k in range(KD):
                            ins = mm(b[:, 0:NE], xT[:, k, tile * P:(tile + 1) * P], wrt[:, k, :],
                                     start=(k == 0), stop=(k == KD - 1))
                        ins.then_inc(sc_ready.sem, 1)
                    elif kind == "K":
                        pe.wait_ge(oh_ready.sem, oh_ready.at(l, 1))
                        b = take(sc, sc_done, SC_AT, l, step)
                        oh, tri, ones = rt[:, 6], const[:, C_TRI:C_TRI + P], const[:, C_ONES:C_ONES + P]
                        mm(b[:, 0:NE], tri, oh[:, 0, :], start=True, stop=True)
                        mm(b[:, NE:2 * NE], ones, oh[:, 0, :], start=True, stop=False)
                        mm(b[:, NE:2 * NE], tri, oh[:, 1, :], start=False, stop=True)
                        mm(b[:, 2 * NE:3 * NE], ones, oh[:, 0, :], start=True, stop=False)
                        mm(b[:, 2 * NE:3 * NE], ones, oh[:, 1, :], start=False, stop=True).then_inc(sc_ready.sem, 1)

                def gather(c, x_no):
                    pe.wait_ge(disp_ready.sem, disp_ready.after(x_no + 1))
                    pe.sem_inc(pe_paced.sem, 1)
                    for i in range(4):
                        for tile in range(NT):
                            k = 4 * c + i
                            ins = mm(pv[c][:, i * P:(i + 1) * P], x[:, tile, k * P:(k + 1) * P],
                                     disp[:, tile].rearrange("p e s -> p (e s)"), start=(tile == 0), stop=(tile == NT - 1))
                    ins.then_inc(xg_ready.sem, 1)

                pe.wait_ge(pj_done.sem, pj_done.at(l, len(PJ)))
                pe.wait_ge(tp_done.sem, tp_done.at(l, len(TP)))
                pe.wait_ge(sc_done.sem, sc_done.at(l, len(SC)))
                pe.wait_ge(pv_done.sem, pv_done.at(l, len(PV)))
                pe.wait_ge(passes_ready.sem, passes_ready.at(l, 1))
                passes = pe.value_load(passes_sb[0:1, 0:1], min_val=1, max_val=SEQ // SLOTS)
                with pe.Fori(0, passes) as r:
                    x0 = pe.snap(gathers_before + r * (PAIRS + 1))
                    g0 = pe.snap(pairs_before + r * PAIRS)
                    pe.wait_ge(acc_done.sem, acc_done.after(g0 * 4))
                    gather(0, x0)
                    gather(1, x0)
                    with pe.Fori(0, PAIRS) as pair:
                        g = pe.snap(g0 + pair)
                        xn = pe.snap(x0 + pair)
                        pe.wait_ge(dt_done.sem, dt_done.after(g))
                        pe.sem_inc(pe_paced.sem, 1)
                        for tile in range(NT):
                            ins = pe.transpose(tp[1][:, tile * P:(tile + 1) * P], dispw[:, tile].rearrange("p e s -> p (e s)"), ident)
                        ins.then_inc(dt_ready.sem, 1)
                        pe.wait_ge(xg_done.sem, xg_done.after(xn * 2 + 2))
                        for i, ready in enumerate((g_ready, u_ready)):
                            pe.wait_ge(landed_e[2 * i].sem, landed_e[2 * i].after(g * 32 + 32))
                            pe.wait_ge(landed_e[2 * i + 1].sem, landed_e[2 * i + 1].after(g * 32 + 32))
                            pe.wait_ge(acc_done.sem, acc_done.after(g * 4 - 3 + i))
                            pe.sem_inc(pe_paced.sem, 1)
                            for k in range(KD):
                                for u in range(2):
                                    ins = mm(pj[i][64 * u:64 * u + 64, :], xg[:, k, 64 * u:64 * u + 64],
                                             slot(2 * i + u, KD, FE)[:, k, :], start=(k == 0), stop=(k == KD - 1))
                            ins.then_inc(ready.sem, 1)
                        pe.wait_ge(acc_done.sem, acc_done.after(g * 4 - 1))
                        gather(0, pe.snap(xn + 1))
                        pe.wait_ge(h_ready.sem, h_ready.after(g + 1))
                        pe.wait_ge(ht_done.sem, ht_done.after(g))
                        pe.sem_inc(pe_paced.sem, 1)
                        for f in range(4):
                            ins = pe.transpose(tp[0][:, f * P:(f + 1) * P], hh[:, f * P:(f + 1) * P], ident)
                        ins.then_inc(ht_ready.sem, 1)
                        pe.wait_ge(acc_done.sem, acc_done.after(g * 4))
                        gather(1, pe.snap(xn + 1))
                        pe.wait_ge(ht_done.sem, ht_done.after(g + 1))
                        pe.wait_ge(landed_e[4].sem, landed_e[4].after(g * 32 + 32))
                        pe.wait_ge(landed_e[5].sem, landed_e[5].after(g * 32 + 32))
                        for half in range(2):
                            pe.wait_ge(y_done.sem, y_done.after(g * 2 - 1 + half))
                            pe.sem_inc(pe_paced.sem, 1)
                            for f in range(4):
                                for u in range(2):
                                    ins = mm(sc[half][64 * u:64 * u + 64, :], hT[:, f, 64 * u:64 * u + 64],
                                             slot(4 + u, 4, D)[:, f, half * 512:(half + 1) * 512], start=(f == 0), stop=(f == 3))
                            ins.then_inc(y_ready.sem, 1)
                        pe.wait_ge(dt_done.sem, dt_done.after(g + 1))
                        for half in range(2):
                            pe.wait_ge(y_done.sem, y_done.after(g * 2 + 1 + half))
                            if half == 1:
                                pe.wait_ge(xg_done.sem, xg_done.after(xn * 2 + 4))
                            pe.sem_inc(pe_paced.sem, 1)
                            for tile in range(NT):
                                mm((pj, pv)[half][tile][:], dispwT[:, tile * P:(tile + 1) * P], ysb[:, half * 512:(half + 1) * 512],
                                   start=True, stop=True).then_inc(c_ready.sem, 1)
                pairs_before = pe.snap(pairs_before + passes * PAIRS)
                gathers_before = pe.snap(gathers_before + passes * (PAIRS + 1))

        @block.scalar
        def _(act):
            A = act.activation
            act.sem_inc(dt_done.sem, dt_done.credit)
            act.sem_inc(ht_done.sem, ht_done.credit)
            act.sem_inc(y_done.sem, y_done.credit)
            act.dma_start(const[:], t["c_pack"]).then_inc(consts_in.sem, 16)
            act.dma_start(t["s_rev"], t["c_rev"]).then_inc(setup_in.sem, 16)
            act.dma_start(t["s_fwd"], t["c_fwd"]).then_inc(setup_in.sem, 16)
            act.dma_start(t["s_neg"], t["c_neg"]).then_inc(setup_in.sem, 16)

            pairs_before = gathers_before = 0
            for l in range(DEPTH):
                for step in STEPS:
                    kind = step[0]
                    if step in PJ_AT:
                        i = PJ_AT[step]
                        b = pj[i % 2]
                        pair = b[:].rearrange("p (b s) -> p b s", b=2)
                        if kind == "q":
                            o = 4 * step[1]
                            if step[1] == 0:
                                act.wait_ge(zeroed.sem, zeroed.at(l, 2))
                        elif kind == "gr" and step[1:] == (0, 0):
                            act.wait_ge(sc_done.sem, sc_done.at(l, SC_AT[("rot", 3)] + 1))
                        elif kind == "kr":
                            act.wait_ge(sc_done.sem, sc_done.at(l, SC_AT[("rot", step[1])] + 1))
                        elif kind == "KC":
                            act.wait_ge(zero_once.sem, 3)
                        elif kind == "H":
                            act.wait_ge(zero_once.sem, 3)
                        act.wait_ge(pj_ready.sem, pj_ready.at(l, i + 1))
                        if kind == "q":
                            A(qz[0:64, o:o + 4:2, :], pair[0:64], ACT.Copy, scale=HD ** -0.5)
                            ins = A(qz[64:P, o + 1:o + 4:2, :], pair[64:P], ACT.Copy, scale=HD ** -0.5)
                        elif kind == "kcvc":
                            for g in range(GROUPS):
                                src = pair[64 * g:64 * g + 64]
                                A(kv2[0:64, :, g, :], src, ACT.Copy)
                                ins = A(kv2[64:P, :, g, 0:SEQ - 1], src[:, :, 1:SEQ], ACT.Copy)
                        elif kind in ("ksvs", "kwvw"):
                            r = 0 if kind == "ksvs" else 1
                            for g in range(GROUPS):
                                for a in (0, 64):
                                    A(kTd[a:a + 64, g, r, :], b[64 * g:64 * g + 64, 0:SEQ], ACT.Copy)
                            ins = A(vn[:, :, r, :], b[:, SEQ:2 * SEQ].rearrange("p (t d) -> p t d", t=NT), ACT.Copy)
                        elif kind == "gate":
                            ins = A(gates[:].rearrange("p t n -> p (t n)"), b[:, 0:2 * NG3], ACT.Sigmoid)
                        elif kind == "H":
                            A(gk[0:64].rearrange("p g c -> p (g c)"), b[0:64, 0:2 * NC], ACT.Gelu_apprx_tanh)
                            ins = A(gv[64:P, :, :, 0:NC],
                                    b[64:P, 0:2 * NC].rearrange("p (g r c) -> p g r c", g=GROUPS, r=1)
                                    .broadcast_to([64, GROUPS, HPG, NC]), ACT.Gelu_apprx_tanh)
                        elif kind == "KC":
                            ins = A(kcd[:, :, 0:NC], b[:, 0:2 * NC].rearrange("p (g c) -> p g c", g=GROUPS), ACT.Copy)
                        elif kind in ("qr", "kr"):
                            ins = A(rraw[:, step[1]], pair, ACT.Copy)
                        elif kind == "vr":
                            ins = A(vr[:, step[2], step[1] * 512:(step[1] + 1) * 512], b[:], ACT.Copy)
                        elif kind == "gr":
                            ins = A(yb[:, step[2], step[1] * 512:(step[1] + 1) * 512], b[:], ACT.Silu)
                        elif kind == "ma":
                            ins = A(merged[:, 2 * step[1]:2 * step[1] + 2, :], pair, ACT.Sigmoid)
                        elif kind == "mb":
                            ins = A(gateb[:, 2 * step[1]:2 * step[1] + 2, :], pair, ACT.Sigmoid)
                        ins.then_inc(pj_done.sem, 1)
                    elif kind in ("xT", "x1T", "ybT"):
                        _, tile, c = step
                        i = TP_AT[step]
                        if kind == "ybT" and c == 0 and tile == 0:
                            pass
                        act.wait_ge(tp_ready.sem, tp_ready.at(l, i + 1))
                        dst = ybT if kind == "ybT" else xT
                        A(dst[:, 4 * c:4 * c + 4, tile * P:(tile + 1) * P], tp[i % 2][:].rearrange("p (b s) -> p b s", b=4),
                          ACT.Copy).then_inc(tp_done.sem, 1)
                    elif kind == "CT":
                        i = TP_AT[step]
                        act.wait_ge(tp_ready.sem, tp_ready.at(l, i + 1))
                        A(pcT[:], tp[i % 2][:, 0:SEQ], ACT.Copy).then_inc(tp_done.sem, 1)
                    elif kind == "T":
                        for half, (o, n) in enumerate(((0, 512), (512, 256))):
                            i = TP_AT[step + (half,)]
                            act.wait_ge(tp_ready.sem, tp_ready.at(l, i + 1))
                            A(pT[:, o:o + n], tp[i % 2][:, 0:n], ACT.Copy).then_inc(tp_done.sem, 1)
                    elif kind == "CN":
                        act.wait_ge(soft_in.sem, soft_in.at(l, SOFT_AT[("CS",)] + 1))
                        A(scmp[:].rearrange("p n c -> p (n c)"), scmp[:].rearrange("p n c -> p (n c)"), ACT.Exp)\
                            .then_inc(exp_done.sem, 1)
                    elif kind == "N":
                        h = step[1]
                        act.wait_ge(soft_in.sem, soft_in.at(l, SOFT_AT[("S", h)] + 1))
                        s = scores[h % 2]
                        for j in range(4):
                            n = P if j < 2 else SEQ
                            o = (j % 2) * n + (0 if j < 2 else SEQ)
                            ins = A(s[:, o:o + n], s[:, o:o + n], ACT.Exp, bias=nmax[:, j:j + 1],
                                    accum_out=psum4[:, j:j + 1])
                        ins.then_inc(exp_done.sem, 1)
                    elif kind == "GN":
                        act.wait_ge(var_ready.sem, var_ready.at(l, 1))
                        A(sdev, vare, ACT.Sqrt).then_inc(sqrt_done.sem, 1)
                    elif kind == "LN1":
                        tile = step[1]
                        act.wait_ge(var_ready.sem, var_ready.at(l, 2 + tile))
                        A(sdev[:, tile:tile + 1], vare[:, tile:tile + 1], ACT.Sqrt).then_inc(sqrt_done.sem, 1)
                    elif kind == "route":
                        act.wait_ge(x_ready.sem, x_ready.at(l, 2))
                        A(acc.rearrange("p t d -> p (t d)"), x[:].rearrange("p t d -> p (t d)"), ACT.Copy, scale=ALPHA)
                        act.wait_ge(soft_in.sem, soft_in.at(l, SOFT_AT[("route",)] + 1))
                        A(rt[:, 0].rearrange("p t e -> p (t e)"), rt[:, 0].rearrange("p t e -> p (t e)"), ACT.Exp)\
                            .then_inc(exp_done.sem, 1)

                def take_gathered(c, x_no):
                    act.wait_ge(xg_ready.sem, xg_ready.after(x_no * 2 + 1 + c))
                    A(xg[:, 4 * c:4 * c + 4, :], pv[c][:].rearrange("p (k s) -> p k s", s=P), ACT.Copy).then_inc(xg_done.sem, 1)

                act.wait_ge(passes_ready.sem, passes_ready.at(l, 1))
                passes = act.value_load(passes_sb[0:1, 0:1], min_val=1, max_val=SEQ // SLOTS)
                with act.Fori(0, passes) as r:
                    x0 = act.snap(gathers_before + r * (PAIRS + 1))
                    g0 = act.snap(pairs_before + r * PAIRS)
                    take_gathered(0, x0)
                    take_gathered(1, x0)
                    with act.Fori(0, PAIRS) as pair:
                        g = act.snap(g0 + pair)
                        xn = act.snap(x0 + pair)
                        act.wait_ge(dt_ready.sem, dt_ready.after(g + 1))
                        A(dispwT, tp[1][:, 0:SEQ], ACT.Copy).then_inc(dt_done.sem, 1)
                        act.wait_ge(g_ready.sem, g_ready.after(g + 1))
                        A(hs, pj[0][:], ACT.Silu).then_inc(silu_done.sem, 1)
                        take_gathered(0, act.snap(xn + 1))
                        act.wait_ge(ht_ready.sem, ht_ready.after(g + 1))
                        A(hT.rearrange("p f s -> p (f s)"), tp[0][:], ACT.Copy).then_inc(ht_done.sem, 1)
                        take_gathered(1, act.snap(xn + 1))
                        for half in range(2):
                            act.wait_ge(y_ready.sem, y_ready.after(g * 2 + 1 + half))
                            A(ysb[:, half * 512:(half + 1) * 512], sc[half][:], ACT.Copy).then_inc(y_done.sem, 1)
                pairs_before = act.snap(pairs_before + passes * PAIRS)
                gathers_before = act.snap(gathers_before + passes * (PAIRS + 1))
                for tile in range(NT):
                    act.wait_ge(var_ready.sem, var_ready.at(l, 4 + tile))
                    A(sdev[:, tile:tile + 1], vare[:, tile:tile + 1], ACT.Sqrt).then_inc(sqrt_done.sem, 1)

        @block.vector
        def _(dve):
            v = dve
            steps_done = [0]
            dve.sem_inc(acc_done.sem, acc_done.credit)

            def then(ins):
                ins.then_inc(dve_step.sem, 1)
                steps_done[0] += 1
                dve.wait_ge(dve_step.sem, steps_done[0])

            def norm(l, which, src, tile):
                xt, st_, one = x[:, tile, :], src[:, tile, :], slice(tile, tile + 1)
                for c in range(2):
                    ins = v.bn_stats(lstats[:, tile, c, :], st_[:, c * 512:(c + 1) * 512])
                then(ins)
                then(v.bn_aggr(lmv[:, tile, :], lstats[:, tile].rearrange("p c n -> p (c n)")))
                v.tensor_scalar(vare[:, one], lmv[:, tile, 1:2], LN_EPS, None, ALU.add).then_inc(var_ready.sem, 1)
                v.wait_ge(lnw_in.sem, lnw_in.at(l, 32 * (which + 1)))
                v.scalar_tensor_tensor(out=xt, in0=st_, scalar=lmv[:, tile, 0:1], in1=lnw[:, 0, :], op0=ALU.subtract, op1=ALU.mult)
                v.wait_ge(sqrt_done.sem, sqrt_done.at(l, 2 * which + tile + 2))
                then(v.reciprocal(rstd[:, one], sdev[:, one]))
                v.scalar_tensor_tensor(out=xt, in0=xt, scalar=rstd[:, one], in1=lnw[:, 1, :], op0=ALU.mult, op1=ALU.add)\
                    .then_inc(x_ready.sem, 1)

            def route(l, b):
                lg, pr, sel, msk, o1, o2, tmp, both = (rt[:, i] for i in (0, 1, 2, 3, 4, 5, 11, 6))
                w = wpad[:, :, 0:NE]
                pair6 = rt[:, 7:10].rearrange("p a t e -> p (a t e)")[:, 0:48].rearrange("p (t g s) -> p t g s", t=NT, g=EG)
                g4 = rt[:, 10].rearrange("p t e -> p (t e)")
                gs, ge = (g4[:, i * 8:i * 8 + 8].rearrange("p (t g) -> p t g", t=NT) for i in range(2))
                s2 = g4[:, 16:18]
                s2b = g4[:, 18:20]
                wide = [P, NT, NE]

                def grp(a):
                    return a.rearrange("p t (g s) -> p t g s", g=EG)

                def b2(a):
                    return a.rearrange("p (t a) -> p t a", a=1).broadcast_to(wide)

                def b2g(a):
                    return a.rearrange("p (t a) -> p t a", a=1).broadcast_to([P, NT, EG])
                eidx = const[:, C_EIDX:C_EIDX + NE].rearrange("p (a e) -> p a e", a=1).broadcast_to(wide)
                gidx = const[:, C_GIDX:C_GIDX + EG].rearrange("p (a e) -> p a e", a=1).broadcast_to([P, NT, EG])
                rb = t["s_rb"].rearrange("p (a e) -> p a e", a=1).broadcast_to(wide)
                TT = v.tensor_tensor
                then(v.tensor_reduce(s2, b, AX.X, ALU.max))
                TT(lg, b, b2(s2), ALU.subtract).then_inc(soft_in.sem, 1)
                v.wait_ge(exp_done.sem, exp_done.at(l, len(EXP_AT)))
                then(v.tensor_reduce(s2, lg, AX.X, ALU.add))
                then(v.reciprocal(s2b, s2))
                then(TT(pr, lg, b2(s2b), ALU.mult))
                then(TT(sel, pr, rb, ALU.add))
                sg = grp(sel)
                TT(pair6[:, :, :, 0:3], sg[:, :, :, 0:3], sg[:, :, :, 1:4], ALU.add)
                TT(pair6[:, :, :, 3:5], sg[:, :, :, 0:2], sg[:, :, :, 2:4], ALU.add)
                then(TT(pair6[:, :, :, 5:6], sg[:, :, :, 0:1], sg[:, :, :, 3:4], ALU.add))
                then(v.tensor_reduce(gs, pair6, AX.X, ALU.max))
                then(v.tensor_reduce(s2, gs, AX.X, ALU.max))
                then(TT(ge, gs, b2g(s2), ALU.is_equal))
                then(TT(gs, ge, gidx, ALU.mult))
                then(v.tensor_reduce(s2, gs, AX.X, ALU.max))
                then(TT(ge, gs, b2g(s2), ALU.is_equal))
                ins = v.tensor_scalar(grp(msk), ge.rearrange("p t (g s) -> p t g s", s=1).broadcast_to([P, NT, EG, EG]),
                                      -MASKED, MASKED, ALU.mult, ALU.add)
                then(ins)
                then(TT(msk, msk, sel, ALU.add))
                for pick in (o1, o2):
                    then(v.tensor_reduce(s2, msk, AX.X, ALU.max))
                    then(TT(tmp, msk, b2(s2), ALU.is_equal))
                    then(TT(tmp, tmp, eidx, ALU.mult))
                    then(v.tensor_reduce(s2, tmp, AX.X, ALU.max))
                    then(TT(pick, tmp, b2(s2), ALU.is_equal))
                    if pick is o1:
                        then(v.scalar_tensor_tensor(out=msk, in0=o1, scalar=3 * MASKED, in1=msk, op0=ALU.mult, op1=ALU.add))
                TT(both, o1, o2, ALU.add).then_inc(oh_ready.sem, 1)
                v.wait_ge(oh_ready.sem, oh_ready.at(l, 1))
                then(TT(tmp, both, pr, ALU.mult))
                then(v.tensor_reduce(s2, tmp, AX.X, ALU.add))
                then(v.reciprocal(s2b, s2))
                then(TT(w, tmp, b2(s2b), ALU.mult))

            dve.wait_ge(setup_mm.sem, 1)
            v.tensor_tensor(t["s_rows"], sc[0][0:NH, 0:REV], t["s_neg"], ALU.add).then_inc(setup_rows.sem, 1)
            dve.wait_ge(setup_mm.sem, 2)
            cadd = const[:, C_CADD:C_CADD + NT * CP].rearrange("p (t a c) -> p t a c", t=NT, a=1)
            cmul = const[:, C_CMUL:C_CMUL + NT * CP].rearrange("p (t a c) -> p t a c", t=NT, a=1)
            v.tensor_tensor(bcmp[:], sc[1][:, 0:NT * NH * CP].rearrange("p (t c h) -> p t h c", t=NT, c=CP),
                            cadd.broadcast_to([P, NT, NH, CP]), ALU.add).then_inc(setup_bc.sem, 1)

            pairs_before = gathers_before = passes_before = 0
            for l in range(DEPTH):
                for step in STEPS:
                    kind = step[0]
                    if step in SC_AT:
                        i = SC_AT[step]
                        b = sc[i % 2]
                        v.wait_ge(sc_ready.sem, sc_ready.at(l, i + 1))
                    if kind == "win":
                        v.wait_ge(pj_done.sem, pj_done.at(l, PJ_AT[("kcvc",)] + 1))
                        v.wait_ge(cw_in.sem, cw_in.at(l, 96))
                        for a in range(2):
                            for g in range(GROUPS):
                                src = bass.AP(kv2.tensor, kv2[:, a, g, 0:1].offset,
                                              [list(kv2.ap[0]), [2, L2], [NSTRIDE, NC]])
                                ins = v.tensor_tensor(win[:, a, :, g, :], src,
                                                      pos[:, a, :].rearrange("p (l c) -> p l c", c=1).broadcast_to([P, L2, NC]), ALU.add)
                        ins.then_inc(win_ready.sem, 1)
                    elif kind == "VC":
                        blk = const[:, C_BLK:C_BLK + NH].rearrange("p (h d) -> p h d", d=1).broadcast_to([P, NH, HD])
                        v.tensor_tensor(vcz[:], b[:, 0:HD].rearrange("p (h d) -> p h d", h=1).broadcast_to([P, NH, HD]), blk,
                                        ALU.mult).then_inc(sc_done.sem, 1)
                    elif kind == "CS":
                        v.tensor_tensor(scmp[:].rearrange("p n c -> p (n c)"), b[:, 0:NT * NH * CP],
                                        bcmp[:].rearrange("p t h c -> p (t h c)"), ALU.add).then_inc(sc_done.sem, 1)
                        v.wait_ge(sc_done.sem, sc_done.at(l, i + 1))
                        then(v.tensor_reduce(cmax, scmp[:], AX.X, ALU.max))
                        v.tensor_tensor(scmp[:], scmp[:], cmax.rearrange("p (n c) -> p n c", c=1).broadcast_to([P, NT * NH, CP]),
                                        ALU.subtract).then_inc(soft_in.sem, 1)
                    elif kind == "CN":
                        v.wait_ge(exp_done.sem, exp_done.at(l, EXP_AT[("CN",)] + 1))
                        sview = scmp[:].rearrange("p (t h) c -> p t h c", t=NT)
                        then(v.tensor_tensor(sview, sview, cmul.broadcast_to([P, NT, NH, CP]), ALU.mult))
                        then(v.tensor_reduce(csum, scmp[:], AX.X, ALU.add))
                        then(v.tensor_scalar(csum, csum, 1e-30, None, ALU.max))
                        then(v.reciprocal(crec, csum))
                        v.wait_ge(pj_done.sem, pj_done.at(l, PJ_AT[("gate",)] + 1))
                        then(v.tensor_tensor(crec.rearrange("p (t h) -> p t h", t=NT), crec.rearrange("p (t h) -> p t h", t=NT),
                                             gates[:, :, 0:NG3:3], ALU.mult))
                        v.tensor_tensor(scmp[:], scmp[:], crec.rearrange("p (n c) -> p n c", c=1).broadcast_to([P, NT * NH, CP]),
                                        ALU.mult).then_inc(p_ready.sem, 1)
                    elif kind == "S":
                        h = step[1]
                        s = scores[h % 2]
                        if l == 0 and h == 0:
                            v.wait_ge(toep_in.sem, 16)
                        for qt in range(NT):
                            i = SC_AT[step + (qt,)]
                            n = (qt + 1) * P
                            o = qt * SEQ
                            v.wait_ge(sc_ready.sem, sc_ready.at(l, i + 1))
                            v.tensor_tensor(s[:, o:o + 2 * n].rearrange("p (r k) -> p r k", r=2),
                                            sc[i % 2][:, 0:2 * n].rearrange("p (r k) -> p r k", r=2),
                                            bias[:, h:h + 1, SEQ - n:SEQ].broadcast_to([P, 2, n]), ALU.add).then_inc(sc_done.sem, 1)
                        v.wait_ge(sc_done.sem, sc_done.at(l, i))
                        v.tensor_reduce(nmax[:, 0:2], s[:, 0:SEQ].rearrange("p (r k) -> p r k", r=2), AX.X, ALU.max, negate=True)
                        v.wait_ge(sc_done.sem, sc_done.at(l, i + 1))
                        v.tensor_reduce(nmax[:, 2:4], s[:, SEQ:3 * SEQ].rearrange("p (r k) -> p r k", r=2), AX.X, ALU.max,
                                        negate=True).then_inc(soft_in.sem, 1)
                    elif kind == "N":
                        h = step[1]
                        v.wait_ge(exp_done.sem, exp_done.at(l, EXP_AT[step] + 1))
                        then(v.reciprocal(r4, psum4))
                        r22 = r4.rearrange("p (t r) -> p t r", t=NT)
                        then(v.tensor_tensor(r22, r22, gates[:, :, 3 * h + 1:3 * h + 3], ALU.mult))
                        for qt in range(NT):
                            n = (qt + 1) * P
                            s = scores[h % 2][:, qt * SEQ:qt * SEQ + 2 * n].rearrange("p (r k) -> p r k", r=2)
                            ins = v.tensor_tensor(s, s, r4[:, 2 * qt:2 * qt + 2].rearrange("p (r k) -> p r k", k=1).broadcast_to([P, 2, n]),
                                                  ALU.mult)
                        ins.then_inc(p_ready.sem, 1)
                    elif kind == "V" and step[1] % 2:
                        i = PV_AT[step]
                        v.wait_ge(pv_ready.sem, pv_ready.at(l, i + 1))
                        v.tensor_copy(yaT[:, step[1] // 2, :], pv[i % 2][:, 0:SEQ]).then_inc(pv_done.sem, 1)
                    elif kind == "rot":
                        r = step[1]
                        half = [P, 2, SEQ]
                        sinb = sinT.rearrange("p (b s) -> p b s", b=1).broadcast_to(half)
                        cosb = cosT.rearrange("p (b s) -> p b s", b=1).broadcast_to(half)
                        v.tensor_tensor(rtmp, b[:].rearrange("p (b s) -> p b s", b=2), sinb, ALU.mult)
                        then(v.tensor_tensor(rsum, rraw[:, r % 2], cosb, ALU.mult))
                        if r < 2:
                            v.wait_ge(zeroed.sem, zeroed.at(l, 4))
                            v.tensor_tensor(qrz[0:64, 4 * r:4 * r + 4:2, :], rtmp[0:64], rsum[0:64], ALU.add)
                            v.tensor_tensor(qrz[64:P, 4 * r + 1:4 * r + 4:2, :], rtmp[64:P], rsum[64:P], ALU.add)\
                                .then_inc(sc_done.sem, 1)
                        else:
                            v.tensor_tensor(krT[:, 2 * (r - 2):2 * (r - 2) + 2, :], rtmp, rsum, ALU.add).then_inc(sc_done.sem, 1)
                        v.wait_ge(sc_done.sem, sc_done.at(l, i + 1))
                    elif kind == "ST":
                        h = step[1]
                        if h >= 2:
                            v.wait_ge(pv_ready.sem, pv_ready.at(l, PV_AT[("Y", h - 2)] + 1))
                        if l == 0 and h == 0:
                            dve.wait_ge(bias_in.sem, 48)
                        s = st[:, h % 2, :]
                        v.tensor_tensor(s[:, 0:SEQ], b[:, 0:SEQ], decay[:, h, :], ALU.mult)
                        v.tensor_tensor(s[:, SEQ:SEQ + P], b[:, SEQ:SEQ + P], decay[:, h, 0:P], ALU.mult).then_inc(sc_done.sem, 1)
                    elif kind == "Y":
                        h = step[1]
                        i = PV_AT[step]
                        v.wait_ge(pv_ready.sem, pv_ready.at(l, i + 1))
                        v.tensor_copy(yraw[:, :, h * P:(h + 1) * P], pv[i % 2][:, 0:SEQ].rearrange("p (t d) -> p t d", t=NT))\
                            .then_inc(pv_done.sem, 1)
                        v.wait_ge(pv_done.sem, pv_done.at(l, i + 1))
                        for tile in range(NT):
                            ins = v.bn_stats(stats[:, tile, h, :], yraw[:, tile, h * P:(h + 1) * P])
                        if h == NH - 1:
                            then(ins)
                    elif kind == "GN":
                        for tile in range(NT):
                            for h in range(NH):
                                ins = v.bn_aggr(mv[:, tile, h, :], stats[:, tile, h, :])
                        then(ins)
                        v.tensor_scalar(vare.rearrange("p (t h) -> p t h", t=NT), mv[:, :, :, 1], LN_EPS, None, ALU.add)\
                            .then_inc(var_ready.sem, 1)
                        v.wait_ge(sqrt_done.sem, sqrt_done.at(l, 1))
                        then(v.reciprocal(rstd, sdev))
                        for tile in range(NT):
                            for h in range(NH):
                                y = yraw[:, tile, h * P:(h + 1) * P]
                                ins = v.tensor_scalar(y, y, mv[:, tile, h, 0:1], rstd[:, tile * NH + h:tile * NH + h + 1],
                                                      ALU.subtract, ALU.mult)
                        then(ins)
                        v.wait_ge(pj_done.sem, pj_done.at(l, PJ_AT[("gr", 1, 1)] + 1))
                        for tile in range(NT):
                            ins = v.tensor_tensor(yb[:, tile, :], yb[:, tile, :], yraw[:, tile, :], ALU.mult)
                        ins.then_inc(yb_ready.sem, 1)
                    elif kind in ("wa", "wb"):
                        j = step[1]
                        m = merged[:, 2 * j:2 * j + 2, :]
                        product = b[:].rearrange("p (b s) -> p b s", b=2)
                        if kind == "wa":
                            v.wait_ge(pj_done.sem, pj_done.at(l, PJ_AT[("ma", j)] + 1))
                            v.tensor_tensor(m, product, m, ALU.mult).then_inc(sc_done.sem, 1)
                        else:
                            v.wait_ge(pj_done.sem, pj_done.at(l, PJ_AT[("mb", j)] + 1))
                            g = gateb[:, 2 * j:2 * j + 2, :]
                            then(v.tensor_tensor(g, product, g, ALU.mult))
                            v.tensor_tensor(m, m, g, ALU.add).then_inc(sc_done.sem, 1)
                    elif kind == "wo":
                        _, c, tile = step
                        xs = x[:, tile, c * 512:(c + 1) * 512]
                        v.scalar_tensor_tensor(out=xs, in0=xs, scalar=ALPHA, in1=b[:], op0=ALU.mult, op1=ALU.add)\
                            .then_inc(sc_done.sem, 1)
                    elif kind == "LN1":
                        v.wait_ge(sc_done.sem, sc_done.at(l, SC_AT[("wo", 1, step[1])] + 1))
                        norm(l, 0, x, step[1])
                    elif kind == "R":
                        v.tensor_copy(rt[:, 6, step[1], :], b[:, 0:NE]).then_inc(sc_done.sem, 1)
                    elif kind == "route":
                        v.wait_ge(sc_done.sem, sc_done.at(l, SC_AT[("R", NT - 1)] + 1))
                        route(l, rt[:, 6])
                    elif kind == "K":
                        both, pad = rt[:, 6], [P, NT, 2]
                        rank = b[:, 0:NT * NE].rearrange("p (t e) -> p t e", t=NT)
                        if l == 0:
                            v.memset(key[:, :, NE:NE + 2], -1.0)
                            v.memset(wpad[:, :, NE:NE + 2], 0.0)
                        ks = key[:, :, 0:NE]
                        then(v.scalar_tensor_tensor(out=ks, in0=rank, scalar=1.0, in1=both, op0=ALU.add, op1=ALU.mult))
                        v.tensor_scalar(ks, ks, -1.0, None, ALU.add)
                        most, over = npf[:, 0:1], npf[:, 1:4]
                        then(v.tensor_reduce(most, b[:, 2 * NE:3 * NE], AX.X, ALU.max))
                        for i in range(3):
                            ins = v.tensor_scalar(over[:, i:i + 1], most, float(SLOTS * (i + 1)), None, ALU.is_gt)
                        then(ins)
                        then(v.tensor_reduce(most, over, AX.X, ALU.add))
                        then(v.tensor_scalar(passes_sb[:], most, 1.0, None, ALU.add))
                        v.sem_inc(passes_ready.sem, 1)
                        v.sem_inc(sc_done.sem, 1)

                def dispatch(pair, x_no, g):
                    wide = [P, NT, 2, SLOTS]
                    iota = const[:, C_IOTA:C_IOTA + SLOTS].rearrange("p (t e s) -> p t e s", t=1, e=1).broadcast_to(wide)
                    cols = bass.ds(pair * 2, 2)
                    v.wait_ge(xg_ready.sem, xg_ready.after(x_no * 2))
                    v.wait_ge(dt_ready.sem, dt_ready.after(g))
                    v.sem_inc(dve_paced.sem, 1)
                    v.tensor_tensor(disp, iota, key[:, :, cols].rearrange("p t (e s) -> p t e s", s=1).broadcast_to(wide), ALU.is_equal)\
                        .then_inc(disp_made.sem, 1)
                    v.wait_ge(disp_made.sem, disp_made.after(x_no + 1))
                    v.sem_inc(dve_paced.sem, 1)
                    v.tensor_tensor(dispw, disp, wpad[:, :, cols].rearrange("p t (e s) -> p t e s", s=1).broadcast_to(wide), ALU.mult)\
                        .then_inc(disp_ready.sem, 1)

                v.wait_ge(passes_ready.sem, passes_ready.at(l, 1))
                passes = v.value_load(passes_sb[0:1, 0:1], min_val=1, max_val=SEQ // SLOTS)
                with dve.Fori(0, passes) as r:
                    x0 = v.snap(gathers_before + r * (PAIRS + 1))
                    g0 = v.snap(pairs_before + r * PAIRS)
                    dispatch(0, x0, g0)
                    with dve.Fori(0, PAIRS) as pair:
                        g = v.snap(g0 + pair)
                        dispatch(v.snap(pair + 1), v.snap(x0 + pair + 1), v.snap(g + 1))
                        v.wait_ge(u_ready.sem, u_ready.after(g + 1))
                        v.wait_ge(silu_done.sem, silu_done.after(g + 1))
                        v.sem_inc(dve_paced.sem, 1)
                        v.tensor_tensor(hh, hs, pj[1][:], ALU.mult).then_inc(h_ready.sem, 1)
                        for half in range(2):
                            for tile in range(NT):
                                i = 2 * half + tile
                                v.wait_ge(c_ready.sem, c_ready.after(g * 4 + 1 + i))
                                v.wait_ge(acc_done.sem, acc_done.after(g * 4 - 3 + i))
                                v.sem_inc(dve_paced.sem, 1)
                                xs = acc[:, tile, half * 512:(half + 1) * 512]
                                v.tensor_tensor(xs, xs, (pj, pv)[half][tile][:], ALU.add).then_inc(acc_done.sem, 1)
                    v.wait_ge(disp_ready.sem, disp_ready.after(x0 + PAIRS + 1))
                    v.sem_inc(dve_paced.sem, 1)
                    v.tensor_scalar(key[:], key[:], -float(SLOTS), None, ALU.add).then_inc(key_moved.sem, 1)
                    v.wait_ge(key_moved.sem, key_moved.after(v.snap(passes_before + r) + 1))
                    v.sem_inc(dve_paced.sem, 1)
                passes_before = v.snap(passes_before + passes)
                pairs_before = v.snap(pairs_before + passes * PAIRS)
                gathers_before = v.snap(gathers_before + passes * (PAIRS + 1))
                v.wait_ge(acc_done.sem, acc_done.after(pairs_before * 4))
                v.sem_inc(dve_paced.sem, 1)
                for tile in range(NT):
                    norm(l, 1, acc, tile)


def _constants():
    import numpy as np
    f = np.float32

    def bucket(n):
        n = np.maximum(n, 0)
        nf = np.maximum(n, 1).astype(f)
        large = 16 + (np.log(nf / f(16)) / f(np.log(2048 / 16)) * f(16)).astype(np.int32)
        return np.where(n < 16, n, np.minimum(large, 31))

    def onehot(dist):
        return (bucket(dist)[None, :] == np.arange(32)[:, None]).astype(f)
    pack = np.zeros((P, NCONST), f)
    pack[:, C_ID:C_ID + P] = np.eye(P)
    swap = np.zeros((P, P), f)
    for d in range(P):
        if d % 64 < 32:
            swap[d + 32, d] = -1.0
        else:
            swap[d - 32, d] = 1.0
    pack[:, C_SWAP:C_SWAP + P] = swap
    inv = (f(10000.0) ** (-np.arange(32, dtype=f) * f(2.0) / f(64))).astype(f)
    ang = (np.arange(SEQ, dtype=f)[None, :] * inv[:, None]).astype(f)
    pack[:, C_COS:C_COS + SEQ] = np.tile(np.cos(ang), (4, 1))
    pack[:, C_SIN:C_SIN + SEQ] = np.tile(np.sin(ang), (4, 1))
    tok = (np.arange(NT)[None, :, None] * P + np.arange(P)[:, None, None])
    end = np.arange(CP)[None, None, :] * NSTRIDE + NLEN - 1
    ok = (end <= tok) & (np.arange(CP)[None, None, :] < NC)
    pack[:, C_CADD:C_CADD + 32] = np.where(ok, 0, MASKED).reshape(P, 32)
    pack[:, C_CMUL:C_CMUL + 32] = ok.astype(f).reshape(P, 32)
    pack[:, C_BLK:C_BLK + NH] = (np.arange(P)[:, None] // CP == np.arange(NH)[None, :])
    pack[:, C_EIDX:C_EIDX + NE] = NE - np.arange(NE)
    pack[:, C_GIDX:C_GIDX + EG] = EG - np.arange(EG)
    pack[:, C_TRI:C_TRI + P] = np.triu(np.ones((P, P)), 1)
    pack[:, C_ONES:C_ONES + P] = 1.0
    pack[:, C_IOTA:C_IOTA + SLOTS] = np.arange(SLOTS)
    lg = np.log(1.0 - 2.0 ** (-5.0 - np.arange(NH)))
    diff = np.arange(SEQ)[None, :] - np.arange(P)[:, None]
    decay = np.where(diff[:, None, :] >= 0, np.exp(np.maximum(diff, 0)[:, None, :] * lg[None, :, None]), 0.0) * HD ** -0.5
    neg = np.where(np.arange(REV) > SEQ - 1, MASKED, 0.0)
    return {
        "c_pack": pack, "c_decay": decay.astype(f), "c_neg": np.tile(neg, (NH, 1)).astype(f),
        "c_rev": onehot(SEQ - 1 - np.arange(REV)), "c_fwd": np.concatenate([onehot(np.arange(FWD) - FWD0 - NSTRIDE * j) for j in range(4)]),
    }


def launch_program(nc, t):
    build(nc, t)


_INS = ["x", "w_in", "cmp_pos", "cmp_w1", "cmp_w2", "w_br_a", "w_br_b", "w_o", "ln1_g", "ln1_b",
        "w_router", "router_bias", "moe_w_gate", "moe_w_up", "moe_w_down", "ln2_g", "ln2_b", "rel_bias"]


def kernel(**inputs):
    import numpy as np
    import concourse.bacc as bacc
    from concourse import mybir as mb
    from concourse.bass_utils import run_bass_kernel_spmd as run

    nc = bacc.Bacc("TRN2", target_bir_lowering=False, num_devices=1)
    arrays, t = {}, {}
    given = {name: np.ascontiguousarray(inputs[name]) for name in _INS}
    given.update(_constants())
    given["cmp_pos"] = np.ascontiguousarray(given["cmp_pos"].reshape(DEPTH, 2, L2, 2 * HD).transpose(0, 1, 3, 2))
    for name, a in given.items():
        arrays[f"in_{name}"] = a
        t[name] = nc.dram_tensor(f"in_{name}", a.shape, mb.dt.from_np(a.dtype), kind="ExternalInput").ap()
    t["out"] = nc.dram_tensor("out_0", (1, SEQ, D), mb.dt.float32, kind="ExternalOutput").ap()
    launch_program(nc, t)
    r = run(nc, [arrays], core_ids=[0])
    return r.results[0]["out_0"]
```

```python
import concourse.bass as bass
from concourse import mybir
from contextlib import ExitStack

F32 = mybir.dt.float32
F32R = mybir.dt.float32r
ALU = mybir.AluOpType
ACT = mybir.ActivationFunctionType
AX = mybir.AxisListType

P = 128
D = 1024
SEQ = 256
DEPTH = 2
NT = SEQ // P
KD = D // P
NH = 8
HD = 64
GROUPS = 2
HPG = NH // GROUPS
NSTRIDE, NLEN = 16, 32
NC = (SEQ - NLEN) // NSTRIDE + 1
CP = 16
L2 = NLEN // 2
NE = 16
EG = 4
FE = 512
NG3 = 3 * NH
ALPHA = float((2 * DEPTH) ** 0.25)
LN_EPS = 1e-5
MASKED = -1e30

SLOT = KD * 512
RING = 8
O_Q, O_KC, O_KW = 0, 512, 1024
O_QR, O_KR, O_VR, O_GR, O_MA, O_MB = 1304, 1816, 2328, 3352, 4376, 5400
ROW = 6424
CHUNKS = [("in", O_Q, 512), ("in", O_KC, 512), ("in", O_KW, 280), ("in", O_QR, 512), ("in", O_KR, 512),
          ("in", O_VR, 512), ("in", O_VR + 512, 512), ("in", O_GR, 512), ("in", O_GR + 512, 512),
          ("in", O_MA, 512), ("in", O_MA + 512, 512), ("br_a", 0, 1024),
          ("in", O_MB, 512), ("in", O_MB + 512, 512), ("br_b", 0, 512), ("br_b", 512, 512),
          ("o", 0, 512), ("o", 512, 512)]
NCH = len(CHUNKS)
MRAW = 4
EXPERT_SLOT = (2, 3, 0, 1, 4, 5, 6, 7)
SLOTS = 64
PAIRS = NE // 2

STEPS = [("xT", t, c) for t in range(NT) for c in range(2)]
STEPS += [("q", 0), ("q", 1), ("kcvc",), ("ksvs",), ("kwvw",), ("gate",), ("win",), ("S", 0), ("qr", 0), ("N", 0), ("H",),
          ("qr", 1), ("KC",), ("VC",), ("CS",), ("S", 1), ("CN",), ("rot", 0), ("kr", 0), ("rot", 1), ("N", 1), ("CT",)]
_side = [("kr", 1)] + [("vr", c, t) for c in range(2) for t in range(NT)] \
    + [("gr", c, t) for c in range(2) for t in range(NT)]
for _h in range(NH):
    STEPS += [("T", _h)] + ([("S", _h + 2)] if _h < NH - 2 else []) + [_side[_h]]
    if _h < 2:
        STEPS += [("rot", _h + 2)]
    STEPS += [("V", _h)] + ([("N", _h + 2)] if _h < NH - 2 else [])
STEPS += [_side[8], ("ST", 0)]
_side = [("ma", i) for i in range(4)] + [("wa", i) for i in range(4)]
for _h in range(NH):
    STEPS += [_side[_h]] + ([("ST", _h + 1)] if _h < NH - 1 else []) + [("Y", _h)]
STEPS += [("GN",)] + [("mb", i) for i in range(4)]
STEPS += [("ybT", t, c) for t in range(NT) for c in range(2)]
STEPS += [("wb", i) for i in range(4)]
for _t in range(NT):
    STEPS += [("wo", c, _t) for c in range(2)] + [("LN1", _t)]
for _t in range(NT):
    STEPS += [("x1T", _t, c) for c in range(2)] + [("R", _t)]
STEPS += [("route",), ("K",)]
LAST = {0: ("q", 1), 1: ("ksvs",), 2: ("gate",), 3: ("qr", 1), 4: ("kr", 1), 5: ("vr", 0, 1), 6: ("vr", 1, 1),
        7: ("gr", 0, 1), 8: ("gr", 1, 1), 9: ("ma", 1), 10: ("ma", 3), 11: ("wa", 3), 12: ("mb", 1),
        13: ("mb", 3), 14: ("wb", 1), 15: ("wb", 3), 16: ("wo", 0, 1), 17: ("wo", 1, 1)}
for _j in range(4):
    STEPS.insert(STEPS.index(("wb", _j)) + 1, ("mS", _j))
SPLIT_AFTER = {0: (("xT", 0, 1), ("xT", 0, 1)), 1: (("xT", 1, 1), ("q", 0)), 2: (("q", 1), ("kcvc",)), 3: (("ksvs",), ("kwvw",)),
               4: (("S", 0), ("N", 0)), 5: (("N", 1), ("S", 2)), 6: (("N", 2), ("N", 3)), 7: (("N", 4), ("N", 5)),
               8: (("N", 6), ("N", 7)), 9: (("V", 6), ("V", 7)), 10: (("ST", 0), ("Y", 0)), 11: (("Y", 1), ("Y", 2)),
               12: (("Y", 3), ("Y", 4)), 13: (("wa", 3), ("Y", 7)), 14: (("mb", 1), ("mb", 2)), 15: (("ybT", 1, 1), ("wb", 0)),
               16: (("wb", 1), ("wb", 1)), 17: (("mS", 3), ("mS", 3))}
for _n in range(NCH):
    for _half in (1, 0):
        STEPS.insert(STEPS.index(SPLIT_AFTER[_n][_half]) + 1, ("split", _n, _half))
    assert _n < 2 or STEPS.index(("split", _n, 0)) > STEPS.index(LAST[_n - 2])
STEPS.insert(STEPS.index(("V", NH - 1)) + 1, ("yaS",))
SOFT_AT = {s: i for i, s in enumerate([s for s in STEPS if s[0] in ("S", "CS", "route")])}
EXP_AT = {s: i for i, s in enumerate([s for s in STEPS if s[0] in ("N", "CN", "route")])}

CHUNK_OF = {"q": 0, "kcvc": 1, "ksvs": 1, "kwvw": 2, "gate": 2, "qr": 3, "kr": 4}
PJ = [s for s in STEPS if s[0] in ("q", "kcvc", "ksvs", "kwvw", "gate", "qr", "kr", "vr", "gr", "ma", "mb", "H", "KC")]
TP, SC, PV = [], [], []
for _s in STEPS:
    if _s[0] in ("xT", "CT", "ybT", "x1T"):
        TP.append(_s)
    if _s[0] == "T":
        TP += [_s + (0,), _s + (1,)]
    if _s[0] in ("CS", "VC", "rot", "ST", "wa", "wb", "wo", "R", "K"):
        SC.append(_s)
    if _s[0] == "S":
        SC += [_s + (0,), _s + (1,)]
    if _s[0] == "Y" or (_s[0] == "V" and _s[1] % 2):
        PV.append(_s)
PJ_AT = {s: i for i, s in enumerate(PJ)}
TP_AT = {s: i for i, s in enumerate(TP)}
SC_AT = {s: i for i, s in enumerate(SC)}
PV_AT = {s: i for i, s in enumerate(PV)}
LO_AT = {s: i for i, s in enumerate([s for s in TP if s[0] in ("xT", "ybT")])}

C_ID, C_SWAP, C_COS, C_SIN, C_CADD, C_CMUL, C_BLK, C_EIDX, C_GIDX = 0, 128, 256, 512, 768, 800, 832, 840, 856
C_TRI, C_ONES, C_IOTA = 860, 988, 1116
NCONST = 1180
FWD, FWD0, REV = 528, 272, 384


class Signal:

    def __init__(self, sem, per_layer, credit=0):
        self.sem, self.per_layer, self.credit = sem, per_layer, credit

    def at(self, l, n):
        return l * self.per_layer + n + self.credit

    def after(self, n):
        return n + self.credit


def build(nc, t):
    with ExitStack() as ctx:
        def sb(name, *shape):
            return ctx.enter_context(nc.sbuf_tensor(name, [P, *shape], F32))

        def sb_both(name, *shape):
            tensor = sb(name, *shape)
            size = 4
            for n in shape:
                size *= n
            return tensor, nc.alloc_sbuf_tensor_at(name + "_r", [P, *shape], F32R, offset=nc.sbuf_base - size)

        def bank(name):
            return ctx.enter_context(nc.psum_tensor(name, [P, 512], F32))

        def sem(name, per_layer=0, credit=0):
            return Signal(ctx.enter_context(nc.semaphore(name)), per_layer, credit)

        ring, ring_r = zip(*[sb_both(f"slot{i}", SLOT) for i in range(RING)])

        def blocks(a, slot_, half):
            return a[slot_][:, half * KD * SEQ:(half + 1) * KD * SEQ].rearrange("p (k s) -> p k s", s=SEQ)

        xT, xT_r = blocks(ring, 6, 0), blocks(ring_r, 6, 0)
        xhi_r = blocks(ring_r, 6, 1)
        ybT, ybT_r = blocks(ring, 7, 0), blocks(ring_r, 7, 0)
        bias = blocks(ring, 7, 1)
        x = sb("x", NT, D)
        merged, merged_r = sb_both("merged", KD, SEQ)
        qz = merged
        qrz = ybT
        lnw, lnw_r = sb_both("lnw", 2, D)
        krT = lnw[:, 0, :].rearrange("p (b s) -> p b s", s=SEQ)
        yaT = lnw[:, 1, :].rearrange("p (b s) -> p b s", s=SEQ)
        vr = sb("vr", NT, D)
        gateb = vr[:].rearrange("p t d -> p (t d)").rearrange("p (b s) -> p b s", s=SEQ)
        yb = sb("yb", NT, D)
        yraw = sb("yraw", NT, D)
        decay = bias
        kTd, kTd_r = sb_both("kTd", GROUPS, 2, SEQ)
        vn = sb("vn", NT, 2, P)
        sbuf_s = sb("scores", 768)
        pT = sb("pT", 768)
        const = sb("const", NCONST)
        wrt = sb("wrt", KD, NE)
        bcmp = sb("bcmp", NT, NH, CP)
        scmp = sb("scmp", NT * NH, CP)
        pcT = sb("pcT", SEQ)
        vcz = sb("vcz", NH, HD)
        kcd = sb("kcd", GROUPS, CP)
        gk = sb("gk", GROUPS, NC)
        gv = sb("gv", GROUPS, HPG, CP)
        gates = sb("gates", NT, NG3)
        w2 = sb("w2", HD)
        pos = sb("pos", 2, L2)
        small = sb("small", 512)
        cmpw = vr[:].rearrange("p a d -> p (a d)").rearrange("p (v l m) -> p v l m", v=2, l=L2)
        yflat = yraw[:].rearrange("p t d -> p (t d)")
        kv2 = yflat[:, 0:1024].rearrange("p (v g s) -> p v g s", v=2, g=GROUPS)
        win = yflat[:, 1024:1024 + 2 * L2 * 30].rearrange("p (v l g c) -> p v l g c", v=2, l=L2, g=GROUPS)
        ybf = yb[:].rearrange("p t d -> p (t d)")
        rraw = ybf[:, 0:1024].rearrange("p (u b s) -> p u b s", u=2, b=2)
        rtmp = ybf[:, 1024:1536].rearrange("p (b s) -> p b s", b=2)
        rsum = ybf[:, 1536:2048].rearrange("p (b s) -> p b s", b=2)
        st = sbuf_s[:].rearrange("p (u n) -> p u n", u=2)
        scores = [sbuf_s[:], yflat[:, 0:768]]
        x_parts = xhi_r, xT_r
        yb_parts = xhi_r, ybT_r
        ya_hi = kTd[:].rearrange("p g r s -> p (g r) s")
        ya_hi_r = kTd_r[:].rearrange("p g r s -> p (g r) s")
        yaT_r = lnw_r[:, 1, :].rearrange("p (b s) -> p b s", s=SEQ)
        ya_parts = ya_hi_r, yaT_r
        m_parts = xT_r, merged_r
        hs = ybf[:, 0:FE]
        hh = ybf[:, FE:2 * FE]
        hT = ybf[:, 2 * FE:3 * FE].rearrange("p (f s) -> p f s", s=P)
        xg = yflat[:, 0:D].rearrange("p (k s) -> p k s", s=P)
        vflat = vr[:].rearrange("p t d -> p (t d)")
        ysb = vflat[:, 0:D]
        disp = vflat[:, D:D + 256].rearrange("p (t e s) -> p t e s", t=NT, e=2)
        dispw = vflat[:, D + 256:D + 512].rearrange("p (t e s) -> p t e s", t=NT, e=2)
        dispwT = vflat[:, D + 512:D + 768]
        acc = merged[:].rearrange("p k s -> p (k s)").rearrange("p (t d) -> p t d", t=NT)
        key = sb("key", NT, NE + 2)
        wpad = sb("wpad", NT, NE + 2)
        passes_sb = ctx.enter_context(nc.sbuf_tensor("passes", [P, 1], mybir.dt.int32))
        for name, rows_, o, n in (("s_rel4", P, 0, 4 * NH), ("s_rev", 32, 40, REV), ("s_fwd", P, 440, FWD),
                                  ("s_neg", NH, 1000, REV), ("s_rows", NH, 1400, REV)):
            t[name] = ybf[0:rows_, o:o + n]
        t["s_rb"] = sb("router_bias_rows", NE)[:]
        ident = const[:, C_ID:C_ID + P]
        cosT = const[:, C_COS:C_COS + SEQ]
        sinT = const[:, C_SIN:C_SIN + SEQ]

        at = [0]

        def piece(n):
            at[0] += n
            return small[:, at[0] - n:at[0]]
        nmax, psum4, r4 = piece(4), piece(4), piece(4)
        cmax, csum, crec = piece(16), piece(16), piece(16)
        stats = piece(NT * NH * 6).rearrange("p (t h n) -> p t h n", t=NT, h=NH)
        mv = piece(NT * NH * 2).rearrange("p (t h n) -> p t h n", t=NT, h=NH)
        vare, sdev, rstd = piece(16), piece(16), piece(16)
        lstats = piece(24).rearrange("p (t c n) -> p t c n", t=NT, c=2)
        lmv = piece(4).rearrange("p (t n) -> p t n", t=NT)
        rt = sb("rt", 12, NT, NE)
        npf = sb("passes_float", 4)

        pj = [bank(f"pj{i}") for i in range(2)]
        tp = [bank(f"tp{i}") for i in range(2)]
        sc = [bank(f"sc{i}") for i in range(2)]
        pv = [bank(f"pv{i}") for i in range(2)]

        landed = [sem(f"landed{i}", 32 * len(range(i, NCH, MRAW))) for i in range(MRAW)]
        hi_done, split_done = sem("hi_done", 2 * NCH), sem("split_done", 2 * NCH)
        lo_done, ya_hi_done, ya_lo_done, m_hi_done, m_lo_done = (
            sem("lo_done", 8), sem("ya_hi_done", 1), sem("ya_lo_done", 1), sem("m_hi_done", 4), sem("m_lo_done", 4))
        landed_e = [sem(f"landed_expert{i}") for i in range(len(EXPERT_SLOT))]
        consts_in, setup_in, rel_in, x_in = sem("consts_in"), sem("setup_in"), sem("rel_in"), sem("x_in")
        rows_out, router_in, toep_in, decay_in = sem("rows_out"), sem("router_in"), sem("toep_in", 16), sem("decay_in", 16)
        setup_mm, setup_rows, setup_bc, zero_once = sem("setup_mm"), sem("setup_rows"), sem("setup_bc"), sem("zero_once")
        cw_in, lnw_in = sem("cw_in", 96), sem("lnw_in", 64)
        zeroed = sem("zeroed", 4)
        pj_ready, pj_done = sem("pj_ready", len(PJ)), sem("pj_done", len(PJ))
        tp_ready, tp_done = sem("tp_ready", len(TP)), sem("tp_done", len(TP))
        sc_ready, sc_done = sem("sc_ready", len(SC)), sem("sc_done", len(SC))
        pv_ready, pv_done = sem("pv_ready", len(PV)), sem("pv_done", len(PV))
        win_ready, soft_in, exp_done, p_ready = sem("win_ready", 1), sem("soft_in", len(SOFT_AT)), sem("exp_done", len(EXP_AT)), sem("p_ready", len(EXP_AT) - 1)
        var_ready, sqrt_done, yb_ready, x_ready = sem("var_ready", 5), sem("sqrt_done", 5), sem("yb_ready", 1), sem("x_ready", 4)
        passes_ready, oh_ready = sem("passes_ready", 1), sem("oh_ready", 1)
        disp_made, disp_ready, key_moved = sem("disp_made"), sem("disp_ready"), sem("key_moved")
        xg_ready, xg_done = sem("xg_ready", 0, 2), sem("xg_done")
        g_ready, u_ready, silu_done, h_ready = sem("g_ready"), sem("u_ready"), sem("silu_done"), sem("h_ready")
        dt_ready, dt_done = sem("dt_ready", 0, 1), sem("dt_done", 0, 1)
        ht_ready, ht_done = sem("ht_ready"), sem("ht_done", 0, 1)
        y_ready, y_done = sem("y_ready"), sem("y_done", 0, 2)
        c_ready, acc_done = sem("c_ready"), sem("acc_done", 0, 4)
        dve_step, sp_paced, pe_paced, dve_paced = sem("dve_step"), sem("sp_paced"), sem("pe_paced"), sem("dve_paced")
        out_done = sem("out_done")

        rows_dram = nc.dram_tensor("bias_rows", [NH, REV], F32)
        PITCH = REV + P
        SHIFTED = PITCH * P + P
        shift_dram = nc.dram_tensor("bias_shifted", [NH, SHIFTED], F32)
        shift_out = sem("shift_out")

        def w_in(l, o, n):
            return t["w_in"][l].rearrange("(k p) n -> p k n", p=P)[:, :, o:o + n]

        def chunk_source(l, n):
            kind, o, width = CHUNKS[n]
            if kind == "in":
                return w_in(l, o, width), KD * width
            if kind == "br_a":
                return t["w_br_a"][l].rearrange("(k p) n -> p k n", p=P), 4 * D
            name = "w_br_b" if kind == "br_b" else "w_o"
            return t[name][l].rearrange("(k p) n -> p k n", p=P)[:, :, o:o + width], KD * width

        def slot(i, k, width, ring=ring):
            return ring[i][:, 0:k * width].rearrange("p (k n) -> p k n", k=k)

        def chunk_parts(n):
            k, width = (4, D) if CHUNKS[n][0] == "br_a" else (KD, CHUNKS[n][2])
            return slot(MRAW + n % 2, k, width, ring_r), slot(n % MRAW, k, width, ring_r)

        def weights_in(eng, l, n):
            eng.wait_ge(split_done.sem, split_done.at(l, 2 * n + 2))

        def wait_chunk_used(eng, l, n):
            if LAST[n] in PJ_AT:
                eng.wait_ge(pj_ready.sem, pj_ready.at(l, PJ_AT[LAST[n]] + 1))
            else:
                eng.wait_ge(sc_ready.sem, sc_ready.at(l, SC_AT[LAST[n]] + 1))

        block = ctx.enter_context(nc.Block())

        @block.sync
        def _(sp):
            def load(n, src, k, width):
                dst = slot(n % MRAW, k, width)
                for a in (0, 64):
                    sp.dma_start(dst[a:a + 64], src[a:a + 64]).then_inc(landed[n % MRAW].sem, 16)

            def load_expert(l, i, pair, u, odd):
                src = t[("moe_w_gate", "moe_w_up", "moe_w_down")[i]][l].rearrange("e a b -> (e a) b")
                rows, width = (D, FE) if i < 2 else (FE, D)
                src = src[bass.ds((pair * 2 + u) * rows, rows), :].rearrange("(k p) n -> p k n", p=P)
                j = 6 + u if i == 0 and odd else 2 * i + u
                dst = slot(EXPERT_SLOT[j], rows // P, width)
                for a in (0, 64):
                    sp.dma_start(dst[a:a + 64], src[a:a + 64]).then_inc(landed_e[j].sem, 16)

            def load_gate(l, pair, g, odd):
                sp.wait_ge(g_ready.sem, g_ready.after(g - 1))
                sp.sem_inc(sp_paced.sem, 1)
                for u in range(2):
                    load_expert(l, 0, pair, u, odd)

            def load_up_down(l, pair, g, odd):
                for i, freed in ((1, u_ready), (2, y_ready)):
                    sp.wait_ge(freed.sem, freed.after(g * i))
                    sp.sem_inc(sp_paced.sem, 1)
                    for u in range(2):
                        load_expert(l, i, pair, u, odd)

            def load_rest(l, g0):
                with sp.Fori(0, PAIRS // 2 - 1) as two:
                    for odd in range(2):
                        pair = sp.snap(two * 2 + 2 + odd)
                        load_gate(l, pair, sp.snap(g0 + pair), odd)
                        load_up_down(l, sp.snap(pair - 1), sp.snap(g0 + pair - 1), 1 - odd)
                load_up_down(l, PAIRS - 1, g0 + (PAIRS - 1), 1)

            pairs_before = 0
            for l in range(DEPTH):
                for n in range(NCH):
                    if n >= MRAW:
                        wait_chunk_used(sp, l, n - MRAW)
                    elif l > 0 and n % 2 == 0:
                        freed = (u_ready, g_ready)[n // 2]
                        sp.wait_ge(freed.sem, freed.after(pairs_before))
                        sp.sem_inc(sp_paced.sem, 1)
                    if l == 0 and n == 0:
                        for tile in range(NT):
                            sp.dma_start(x[:, tile, :], t["x"][0, tile * P:(tile + 1) * P, :]).then_inc(x_in.sem, 16)
                    src, _ = chunk_source(l, n)
                    load(n, src, *((4, D) if CHUNKS[n][0] == "br_a" else (KD, CHUNKS[n][2])))
                for u in range(2):
                    wait_chunk_used(sp, l, NCH - 4 + u)
                    load_expert(l, 0, 0, u, 0)
                sp.wait_ge(sc_ready.sem, sc_ready.at(l, SC_AT[("wb", 3)] + 1))
                load_expert(l, 0, 1, 1, 1)
                for i in (1, 2):
                    for u in range(2):
                        wait_chunk_used(sp, l, NCH - 2 + u)
                        load_expert(l, i, 0, u, 0)
                sp.wait_ge(sc_ready.sem, sc_ready.at(l, SC_AT[("R", NT - 1)] + 1))
                load_expert(l, 0, 1, 0, 1)
                load_rest(l, pairs_before)
                sp.wait_ge(passes_ready.sem, passes_ready.at(l, 1))
                passes = sp.value_load(passes_sb[0:1, 0:1], min_val=1, max_val=SEQ // SLOTS)
                with sp.If(passes > 1):
                    with sp.Fori(1, passes) as r:
                        g0 = sp.snap(pairs_before + r * PAIRS)
                        load_gate(l, 0, g0, 0)
                        load_gate(l, 1, sp.snap(g0 + 1), 1)
                        load_up_down(l, 0, g0, 0)
                        load_rest(l, g0)
                pairs_before = sp.snap(pairs_before + passes * PAIRS)
            for tile in range(NT):
                sp.wait_ge(x_ready.sem, x_ready.at(DEPTH - 1, 3 + tile))
                sp.dma_start(t["out"][0, tile * P:(tile + 1) * P, :], x[:, tile, :]).then_inc(out_done.sem, 16)
            sp.wait_ge(out_done.sem, 32)

        @block.gpsimd
        def _(pool):
            def zero_halves(l, buf, n):
                for i, (rows, first) in enumerate(((slice(64, P), 0), (slice(0, 64), 1))):
                    pool.memset(buf[rows, first:NH:2, :], 0.0).then_inc(zeroed.sem, 1)
                    pool.wait_ge(zeroed.sem, zeroed.at(l, n + i + 1))

            def load_bias():
                pool.dma_start(bias, bass.AP(shift_dram, P - 1, [[PITCH, P], [SHIFTED, NH], [1, SEQ]])).then_inc(toep_in.sem, 16)

            pool.memset(t["s_rel4"], 0.0).then_inc(zero_once.sem, 1)
            pool.memset(kcd[:], 0.0).then_inc(zero_once.sem, 1)
            pool.memset(gv[:], 0.0).then_inc(zero_once.sem, 1)
            pool.wait_ge(zero_once.sem, 1)
            for j in range(4):
                pool.dma_start(t["s_rel4"][32 * j:32 * j + 32, NH * j:NH * j + NH], t["rel_bias"]).then_inc(rel_in.sem, 16)
            pool.wait_ge(zero_once.sem, 3)
            for l in range(DEPTH):
                if l == 0:
                    zero_halves(l, qz, 0)
                    pool.wait_ge(setup_rows.sem, 1)
                    pool.dma_start(rows_dram[:, :], t["s_rows"]).then_inc(rows_out.sem, 16)
                    zero_halves(l, qrz, 2)
                    pool.wait_ge(rows_out.sem, 16)
                    pool.dma_start(bass.AP(shift_dram, 0, [[PITCH + 1, P], [SHIFTED, NH], [1, REV]]),
                                   bass.AP(rows_dram, 0, [[0, P], [REV, NH], [1, REV]])).then_inc(shift_out.sem, 16)
                    pool.wait_ge(shift_out.sem, 16)
                    load_bias()
                else:
                    pool.wait_ge(x_ready.sem, x_ready.at(l - 1, 4))
                    zero_halves(l, qz, 0)
                    load_bias()
                for v in range(2):
                    pool.dma_start(cmpw[:, v], t["cmp_w1"][l, v].rearrange("(l q) m -> q l m", q=P)).then_inc(cw_in.sem, 16)
                    pool.dma_start(w2[64 * v:64 * v + 64, :], t["cmp_w2"][l, v]).then_inc(cw_in.sem, 16)
                    pool.dma_start(pos[:, v, :], t["cmp_pos"][l, v]).then_inc(cw_in.sem, 16)
                if l == 0:
                    pool.dma_start(wrt[:], t["w_router"].rearrange("(k p) e -> p k e", p=P)).then_inc(router_in.sem, 16)
                    pool.dma_start(t["s_rb"], t["router_bias"].rearrange("(a e) -> a e", a=1).broadcast_to([P, NE])).then_inc(router_in.sem, 16)
                else:
                    zero_halves(l, qrz, 2)
                pool.wait_ge(sc_done.sem, sc_done.at(l, SC_AT[("S", NH - 1, NT - 1)] + 1))
                pool.dma_start(decay, t["c_decay"]).then_inc(decay_in.sem, 16)
                pool.wait_ge(sc_ready.sem, sc_ready.at(l, SC_AT[("wa", 3)] + 1))
                for i, name in enumerate(("ln1_g", "ln1_b")):
                    pool.dma_start(lnw[:, i, :], t[name][l:l + 1, :].broadcast_to([P, D])).then_inc(lnw_in.sem, 16)
                pool.wait_ge(x_ready.sem, x_ready.at(l, 2))
                for i, name in enumerate(("ln2_g", "ln2_b")):
                    pool.dma_start(lnw[:, i, :], t[name][l:l + 1, :].broadcast_to([P, D])).then_inc(lnw_in.sem, 16)

        @block.tensor
        def _(pe):
            mm = pe.matmul
            pe.sem_inc(xg_ready.sem, xg_ready.credit)
            pe.sem_inc(dt_ready.sem, dt_ready.credit)

            def take(banks, done, index, l, step):
                i = index[step]
                pe.wait_ge(done.sem, done.at(l, max(i - 1, 0)))
                if index is TP_AT and i >= 2 and TP[i - 2] in LO_AT:
                    pe.wait_ge(lo_done.sem, lo_done.at(l, LO_AT[TP[i - 2]] + 1))
                return banks[i % 2]

            def split_product(out, stationary, moving, nk):
                for k in range(nk):
                    for n, (a, b) in enumerate(((0, 0), (0, 1), (1, 0))):
                        ins = mm(out, stationary(a, k), moving(b, k), start=(k == 0 and n == 0), stop=(k == nk - 1 and n == 2))
                return ins

            def columns(out, chunk, col, parts=x_parts, nk=KD):
                w = chunk_parts(chunk)
                return split_product(out, lambda a, k: w[a][:, k, col:col + P], lambda b, k: parts[b][:, k, :], nk)

            def rows(tile, out, chunk, col, width, parts=x_parts):
                w = chunk_parts(chunk)
                return split_product(out, lambda a, k: parts[a][:, k, tile * P:(tile + 1) * P],
                                     lambda b, k: w[b][:, k, col:col + width], KD)

            def bias_products():
                pe.wait_ge(rel_in.sem, 64)
                pe.wait_ge(setup_in.sem, 48)
                mm(sc[0][0:NH, 0:REV], t["s_rel4"][0:32, 0:NH], t["s_rev"], start=True, stop=True).then_inc(setup_mm.sem, 1)
                for qt in range(NT):
                    for c in range(0, CP, 4):
                        o = FWD0 + qt * P - NSTRIDE * c - (NLEN - 1)
                        ins = mm(sc[1][:, (qt * CP + c) * NH:(qt * CP + c + 4) * NH], t["s_fwd"][:, o:o + P], t["s_rel4"],
                                 start=True, stop=True)
                ins.then_inc(setup_mm.sem, 1)

            pairs_before = gathers_before = 0
            for l in range(DEPTH):
                for step in STEPS:
                    kind = step[0]
                    if kind in ("xT", "x1T", "ybT"):
                        _, tile, c = step
                        if c == 0:
                            if kind == "ybT":
                                pe.wait_ge(yb_ready.sem, yb_ready.at(l, 1))
                            elif kind == "x1T":
                                pe.wait_ge(x_ready.sem, x_ready.at(l, 1 + tile))
                            elif l == 0:
                                pe.wait_ge(consts_in.sem, 16)
                                pe.wait_ge(x_in.sem, 32)
                            else:
                                pe.wait_ge(x_ready.sem, x_ready.at(l - 1, 3 + tile))
                        src = yb if kind == "ybT" else x
                        b = take(tp, tp_done, TP_AT, l, step)
                        for i in range(4):
                            ins = pe.transpose(b[:, i * P:(i + 1) * P], src[:, tile, (4 * c + i) * P:(4 * c + i + 1) * P], ident)
                        ins.then_inc(tp_ready.sem, 1)
                        if l == 0 and step == ("xT", NT - 1, 1):
                            bias_products()
                    elif kind in ("q", "qr", "kr", "ma", "mb"):
                        i = step[1]
                        chunk = CHUNK_OF[kind] if kind in CHUNK_OF else (9 if kind == "ma" else 12) + i // 2
                        first = i % 2 == 0
                        if first:
                            weights_in(pe, l, chunk)
                        if kind == "q" and i == 0:
                            pe.wait_ge(lo_done.sem, lo_done.at(l, LO_AT[("xT", 1, 1)] + 1))
                        b = take(pj, pj_done, PJ_AT, l, step)
                        columns(b[:, 0:SEQ], chunk, (i % 2) * SEQ)
                        columns(b[:, SEQ:2 * SEQ], chunk, (i % 2) * SEQ + P).then_inc(pj_ready.sem, 1)
                    elif kind == "kcvc":
                        weights_in(pe, l, 1)
                        b = take(pj, pj_done, PJ_AT, l, step)
                        columns(b[:, 0:SEQ], 1, 0)
                        columns(b[:, SEQ:2 * SEQ], 1, P).then_inc(pj_ready.sem, 1)
                    elif kind in ("ksvs", "kwvw"):
                        chunk, col = (1, 2 * P) if kind == "ksvs" else (2, 0)
                        weights_in(pe, l, chunk)
                        b = take(pj, pj_done, PJ_AT, l, step)
                        columns(b[:, 0:SEQ], chunk, col)
                        if kind == "kwvw":
                            rows(0, b[:, SEQ:SEQ + P + NG3], chunk, col + P, P + NG3).then_inc(pj_ready.sem, 1)
                        else:
                            rows(0, b[:, SEQ:SEQ + P], chunk, col + P, P)
                            rows(1, b[:, SEQ + P:SEQ + 2 * P], chunk, col + P, P).then_inc(pj_ready.sem, 1)
                    elif kind == "gate":
                        b = take(pj, pj_done, PJ_AT, l, step)
                        rows(1, b[:, 0:P + NG3], 2, P, P + NG3).then_inc(pj_ready.sem, 1)
                    elif kind in ("vr", "gr"):
                        _, c, tile = step
                        chunk = (5 if kind == "vr" else 7) + c
                        if tile == 0:
                            weights_in(pe, l, chunk)
                        b = take(pj, pj_done, PJ_AT, l, step)
                        rows(tile, b[:], chunk, 0, 512).then_inc(pj_ready.sem, 1)
                    elif kind == "H":
                        pe.wait_ge(win_ready.sem, win_ready.at(l, 1))
                        b = take(pj, pj_done, PJ_AT, l, step)
                        for i in range(L2):
                            for v in range(2):
                                ins = mm(b[64 * v:64 * v + 64, 0:2 * NC], cmpw[:, v, i, :],
                                         win[:, v, i].rearrange("p g c -> p (g c)"), start=(i == 0), stop=(i == L2 - 1))
                        ins.then_inc(pj_ready.sem, 1)
                    elif kind == "KC":
                        pe.wait_ge(pj_done.sem, pj_done.at(l, PJ_AT[("H",)] + 1))
                        b = take(pj, pj_done, PJ_AT, l, step)
                        for g in range(GROUPS):
                            for a in (0, 64):
                                ins = mm(b[a:a + 64, g * NC:(g + 1) * NC], w2[0:64, :], gk[0:64, g, :], start=True, stop=True)
                        ins.then_inc(pj_ready.sem, 1)
                    elif kind == "VC":
                        b = take(sc, sc_done, SC_AT, l, step)
                        mm(b[:, 0:HD], gv[64:P].rearrange("p g r c -> p (g r c)"), w2[64:P, :],
                           start=True, stop=True).then_inc(sc_ready.sem, 1)
                    elif kind == "CS":
                        pe.wait_ge(pj_done.sem, pj_done.at(l, PJ_AT[("KC",)] + 1))
                        b = take(sc, sc_done, SC_AT, l, step)
                        for qt in range(NT):
                            for h in range(NH):
                                o = (qt * NH + h) * CP
                                ins = mm(b[:, o:o + CP], qz[:, h, qt * P:(qt + 1) * P], kcd[:, h // HPG, :], start=True, stop=True)
                        ins.then_inc(sc_ready.sem, 1)
                    elif kind == "S":
                        h = step[1]
                        if h == 0:
                            pe.wait_ge(pj_done.sem, pj_done.at(l, PJ_AT[("kwvw",)] + 1))
                            pe.wait_ge(zeroed.sem, zeroed.at(l, 2))
                            if l == 0:
                                pe.wait_ge(setup_bc.sem, 1)
                        for qt in range(NT):
                            b = take(sc, sc_done, SC_AT, l, step + (qt,))
                            n = (qt + 1) * P
                            mm(b[:, 0:2 * n].rearrange("p (r k) -> p r k", r=2), qz[:, h, qt * P:(qt + 1) * P],
                               kTd[:, h // HPG, :, 0:n], start=True, stop=True).then_inc(sc_ready.sem, 1)
                    elif kind == "rot":
                        i = step[1]
                        src = ("qr", "kr")[i // 2], i % 2
                        pe.wait_ge(pj_done.sem, pj_done.at(l, PJ_AT[src] + 1))
                        b = take(sc, sc_done, SC_AT, l, step)
                        mm(b[:], const[:, C_SWAP:C_SWAP + P], rraw[:, i % 2].rearrange("p b s -> p (b s)"),
                           start=True, stop=True).then_inc(sc_ready.sem, 1)
                    elif kind == "CT":
                        pe.wait_ge(p_ready.sem, p_ready.at(l, EXP_AT[("CN",)] + 1))
                        b = take(tp, tp_done, TP_AT, l, step)
                        for qt in range(NT):
                            ins = pe.transpose(b[:, qt * P:(qt + 1) * P],
                                               scmp[:, qt * NH:(qt + 1) * NH, :].rearrange("p h c -> p (h c)"), ident)
                        ins.then_inc(tp_ready.sem, 1)
                    elif kind == "T":
                        h = step[1]
                        pe.wait_ge(p_ready.sem, p_ready.at(l, EXP_AT[("N", h)] + 1))
                        s = scores[h % 2]
                        b = take(tp, tp_done, TP_AT, l, step + (0,))
                        for r in range(2):
                            pe.transpose(b[:, r * SEQ:r * SEQ + P], s[:, r * P:(r + 1) * P], ident)
                            ins = pe.transpose(b[:, r * SEQ + P:(r + 1) * SEQ], s[:, SEQ + r * SEQ:SEQ + r * SEQ + P], ident)
                        ins.then_inc(tp_ready.sem, 1)
                        b = take(tp, tp_done, TP_AT, l, step + (1,))
                        for r in range(2):
                            ins = pe.transpose(b[:, r * P:(r + 1) * P], s[:, SEQ + r * SEQ + P:SEQ + (r + 1) * SEQ], ident)
                        ins.then_inc(tp_ready.sem, 1)
                    elif kind == "V":
                        h = step[1]
                        i = PV_AT[("V", h | 1)]
                        if h % 2 == 0:
                            pe.wait_ge(pv_done.sem, pv_done.at(l, max(i - 1, 0)))
                        pe.wait_ge(tp_done.sem, tp_done.at(l, TP_AT[("T", h, 1)] + 1))
                        if h == 0:
                            pe.wait_ge(sc_done.sem, sc_done.at(l, SC_AT[("VC",)] + 1))
                        o = pv[i % 2][64 * (h % 2):64 * (h % 2) + 64, :]
                        g = h // HPG
                        mm(o[:, 0:SEQ], vcz[:, h, :], pcT[:], start=True, stop=False, skip_group_check=True)
                        for r in range(2):
                            mm(o[:, 0:SEQ], vn[:, 0, r, g * HD:(g + 1) * HD], pT[:, r * SEQ:(r + 1) * SEQ],
                               start=False, stop=False, skip_group_check=True)
                        for r in range(2):
                            ins = mm(o[:, P:SEQ], vn[:, 1, r, g * HD:(g + 1) * HD], pT[:, 512 + r * P:512 + (r + 1) * P],
                                     start=False, stop=(r == 1), skip_group_check=True)
                        if h % 2:
                            ins.then_inc(pv_ready.sem, 1)
                    elif kind == "ST":
                        h = step[1]
                        if h == 0:
                            pe.wait_ge(sc_done.sem, sc_done.at(l, SC_AT[("rot", 3)] + 1))
                        b = take(sc, sc_done, SC_AT, l, step)
                        mm(b[:, 0:SEQ], krT[:, h // 2, 0:P], qrz[:, h, :], start=True, stop=True)
                        mm(b[:, SEQ:SEQ + P], krT[:, h // 2, P:SEQ], qrz[:, h, P:SEQ], start=True, stop=True)\
                            .then_inc(sc_ready.sem, 1)
                    elif kind == "Y":
                        h = step[1]
                        if h == 0:
                            pe.wait_ge(pj_done.sem, pj_done.at(l, PJ_AT[("vr", 1, 1)] + 1))
                        pe.wait_ge(sc_done.sem, sc_done.at(l, SC_AT[("ST", h)] + 1))
                        b = take(pv, pv_done, PV_AT, l, step)
                        s = st[:, h % 2, :]
                        v = [vr[:, j, h * P:(h + 1) * P] for j in range(NT)]
                        mm(b[:, 0:P], s[:, 0:P], v[0], start=True, stop=True)
                        mm(b[:, P:SEQ], s[:, P:SEQ], v[0], start=True, stop=False)
                        mm(b[:, P:SEQ], s[:, SEQ:SEQ + P], v[1], start=False, stop=True).then_inc(pv_ready.sem, 1)
                    elif kind in ("wa", "wb"):
                        i = step[1]
                        if kind == "wa":
                            chunk, parts, nk, col = 11, ya_parts, 4, 2 * i * P
                            if i == 0:
                                weights_in(pe, l, 11)
                                pe.wait_ge(ya_lo_done.sem, ya_lo_done.at(l, 1))
                        else:
                            chunk, parts, nk, col = 14 + i // 2, yb_parts, KD, 2 * (i % 2) * P
                            if i % 2 == 0:
                                weights_in(pe, l, chunk)
                            if i == 0:
                                pe.wait_ge(lo_done.sem, lo_done.at(l, LO_AT[("ybT", 1, 1)] + 1))
                        b = take(sc, sc_done, SC_AT, l, step)
                        columns(b[:, 0:SEQ], chunk, col, parts, nk)
                        columns(b[:, SEQ:2 * SEQ], chunk, col + P, parts, nk).then_inc(sc_ready.sem, 1)
                    elif kind == "wo":
                        _, c, tile = step
                        if tile == 0:
                            weights_in(pe, l, 16 + c)
                        if c == 0 and tile == 0:
                            pe.wait_ge(m_lo_done.sem, m_lo_done.at(l, 4))
                        b = take(sc, sc_done, SC_AT, l, step)
                        rows(tile, b[:], 16 + c, 0, 512, m_parts).then_inc(sc_ready.sem, 1)
                    elif kind == "R":
                        tile = step[1]
                        pe.wait_ge(tp_done.sem, tp_done.at(l, TP_AT[("x1T", tile, 1)] + 1))
                        if l == 0 and tile == 0:
                            pe.wait_ge(router_in.sem, 32)
                        b = take(sc, sc_done, SC_AT, l, step)
                        for k in range(KD):
                            ins = mm(b[:, 0:NE], xT[:, k, tile * P:(tile + 1) * P], wrt[:, k, :],
                                     start=(k == 0), stop=(k == KD - 1))
                        ins.then_inc(sc_ready.sem, 1)
                    elif kind == "K":
                        pe.wait_ge(oh_ready.sem, oh_ready.at(l, 1))
                        b = take(sc, sc_done, SC_AT, l, step)
                        oh, tri, ones = rt[:, 6], const[:, C_TRI:C_TRI + P], const[:, C_ONES:C_ONES + P]
                        mm(b[:, 0:NE], tri, oh[:, 0, :], start=True, stop=True)
                        mm(b[:, NE:2 * NE], ones, oh[:, 0, :], start=True, stop=False)
                        mm(b[:, NE:2 * NE], tri, oh[:, 1, :], start=False, stop=True)
                        mm(b[:, 2 * NE:3 * NE], ones, oh[:, 0, :], start=True, stop=False)
                        mm(b[:, 2 * NE:3 * NE], ones, oh[:, 1, :], start=False, stop=True).then_inc(sc_ready.sem, 1)

                def gather(c, x_no):
                    pe.wait_ge(disp_ready.sem, disp_ready.after(x_no + 1))
                    pe.sem_inc(pe_paced.sem, 1)
                    for i in range(4):
                        for tile in range(NT):
                            k = 4 * c + i
                            ins = mm(pv[c][:, i * P:(i + 1) * P], x[:, tile, k * P:(k + 1) * P],
                                     disp[:, tile].rearrange("p e s -> p (e s)"), start=(tile == 0), stop=(tile == NT - 1))
                    ins.then_inc(xg_ready.sem, 1)

                pe.wait_ge(pj_done.sem, pj_done.at(l, len(PJ)))
                pe.wait_ge(tp_done.sem, tp_done.at(l, len(TP)))
                pe.wait_ge(sc_done.sem, sc_done.at(l, len(SC)))
                pe.wait_ge(pv_done.sem, pv_done.at(l, len(PV)))
                pe.wait_ge(passes_ready.sem, passes_ready.at(l, 1))
                passes = pe.value_load(passes_sb[0:1, 0:1], min_val=1, max_val=SEQ // SLOTS)
                with pe.Fori(0, passes) as r:
                    x0 = pe.snap(gathers_before + r * (PAIRS + 1))
                    g0 = pe.snap(pairs_before + r * PAIRS)
                    pe.wait_ge(acc_done.sem, acc_done.after(g0 * 4))
                    gather(0, x0)
                    gather(1, x0)
                    with pe.Fori(0, PAIRS // 2) as two:
                        for odd in range(2):
                            pair = pe.snap(two * 2 + odd)
                            g = pe.snap(g0 + pair)
                            xn = pe.snap(x0 + pair)
                            pe.wait_ge(dt_done.sem, dt_done.after(g))
                            pe.sem_inc(pe_paced.sem, 1)
                            for tile in range(NT):
                                ins = pe.transpose(tp[1][:, tile * P:(tile + 1) * P], dispw[:, tile].rearrange("p e s -> p (e s)"), ident)
                            ins.then_inc(dt_ready.sem, 1)
                            pe.wait_ge(xg_done.sem, xg_done.after(xn * 2 + 2))
                            for i, ready in enumerate((g_ready, u_ready)):
                                if i == 0:
                                    w0, loads = 6 * odd, g * 16 + 32 - 16 * odd
                                else:
                                    w0, loads = 2, g * 32 + 32
                                pe.wait_ge(landed_e[w0].sem, landed_e[w0].after(loads))
                                pe.wait_ge(landed_e[w0 + 1].sem, landed_e[w0 + 1].after(loads))
                                pe.wait_ge(acc_done.sem, acc_done.after(g * 4 - 3 + i))
                                pe.sem_inc(pe_paced.sem, 1)
                                for k in range(KD):
                                    for u in range(2):
                                        ins = mm(pj[i][64 * u:64 * u + 64, :], xg[:, k, 64 * u:64 * u + 64],
                                                 slot(EXPERT_SLOT[w0 + u], KD, FE)[:, k, :], start=(k == 0), stop=(k == KD - 1))
                                ins.then_inc(ready.sem, 1)
                            pe.wait_ge(acc_done.sem, acc_done.after(g * 4 - 1))
                            gather(0, pe.snap(xn + 1))
                            pe.wait_ge(h_ready.sem, h_ready.after(g + 1))
                            pe.wait_ge(ht_done.sem, ht_done.after(g))
                            pe.sem_inc(pe_paced.sem, 1)
                            for f in range(4):
                                ins = pe.transpose(tp[0][:, f * P:(f + 1) * P], hh[:, f * P:(f + 1) * P], ident)
                            ins.then_inc(ht_ready.sem, 1)
                            pe.wait_ge(acc_done.sem, acc_done.after(g * 4))
                            gather(1, pe.snap(xn + 1))
                            pe.wait_ge(ht_done.sem, ht_done.after(g + 1))
                            pe.wait_ge(landed_e[4].sem, landed_e[4].after(g * 32 + 32))
                            pe.wait_ge(landed_e[5].sem, landed_e[5].after(g * 32 + 32))
                            for half in range(2):
                                pe.wait_ge(y_done.sem, y_done.after(g * 2 - 1 + half))
                                pe.sem_inc(pe_paced.sem, 1)
                                for f in range(4):
                                    for u in range(2):
                                        ins = mm(sc[half][64 * u:64 * u + 64, :], hT[:, f, 64 * u:64 * u + 64],
                                                 slot(EXPERT_SLOT[4 + u], 4, D)[:, f, half * 512:(half + 1) * 512], start=(f == 0), stop=(f == 3))
                                ins.then_inc(y_ready.sem, 1)
                            pe.wait_ge(dt_done.sem, dt_done.after(g + 1))
                            for half in range(2):
                                pe.wait_ge(y_done.sem, y_done.after(g * 2 + 1 + half))
                                if half == 1:
                                    pe.wait_ge(xg_done.sem, xg_done.after(xn * 2 + 4))
                                pe.sem_inc(pe_paced.sem, 1)
                                for tile in range(NT):
                                    mm((pj, pv)[half][tile][:], dispwT[:, tile * P:(tile + 1) * P], ysb[:, half * 512:(half + 1) * 512],
                                       start=True, stop=True).then_inc(c_ready.sem, 1)
                pairs_before = pe.snap(pairs_before + passes * PAIRS)
                gathers_before = pe.snap(gathers_before + passes * (PAIRS + 1))

        @block.scalar
        def _(act):
            A = act.activation
            act.sem_inc(dt_done.sem, dt_done.credit)
            act.sem_inc(ht_done.sem, ht_done.credit)
            act.sem_inc(y_done.sem, y_done.credit)
            act.dma_start(const[:], t["c_pack"]).then_inc(consts_in.sem, 16)
            act.dma_start(t["s_rev"], t["c_rev"]).then_inc(setup_in.sem, 16)
            act.dma_start(t["s_fwd"], t["c_fwd"]).then_inc(setup_in.sem, 16)
            act.dma_start(t["s_neg"], t["c_neg"]).then_inc(setup_in.sem, 16)

            pairs_before = gathers_before = 0
            for l in range(DEPTH):
                for step in STEPS:
                    kind = step[0]
                    if step in PJ_AT:
                        i = PJ_AT[step]
                        b = pj[i % 2]
                        pair = b[:].rearrange("p (b s) -> p b s", b=2)
                        if kind == "q":
                            o = 4 * step[1]
                            if step[1] == 0:
                                act.wait_ge(zeroed.sem, zeroed.at(l, 2))
                        elif kind == "gr" and step[1:] == (0, 0):
                            act.wait_ge(sc_done.sem, sc_done.at(l, SC_AT[("rot", 3)] + 1))
                        elif kind == "kr":
                            act.wait_ge(sc_done.sem, sc_done.at(l, SC_AT[("rot", step[1])] + 1))
                        elif kind == "KC":
                            act.wait_ge(zero_once.sem, 3)
                        elif kind == "H":
                            act.wait_ge(zero_once.sem, 3)
                        act.wait_ge(pj_ready.sem, pj_ready.at(l, i + 1))
                        if kind == "q":
                            A(qz[0:64, o:o + 4:2, :], pair[0:64], ACT.Copy, scale=HD ** -0.5)
                            ins = A(qz[64:P, o + 1:o + 4:2, :], pair[64:P], ACT.Copy, scale=HD ** -0.5)
                        elif kind == "kcvc":
                            for g in range(GROUPS):
                                src = pair[64 * g:64 * g + 64]
                                A(kv2[0:64, :, g, :], src, ACT.Copy)
                                ins = A(kv2[64:P, :, g, 0:SEQ - 1], src[:, :, 1:SEQ], ACT.Copy)
                        elif kind in ("ksvs", "kwvw"):
                            r = 0 if kind == "ksvs" else 1
                            for g in range(GROUPS):
                                for a in (0, 64):
                                    A(kTd[a:a + 64, g, r, :], b[64 * g:64 * g + 64, 0:SEQ], ACT.Copy)
                            if kind == "ksvs":
                                ins = A(vn[:, :, r, :], b[:, SEQ:2 * SEQ].rearrange("p (t d) -> p t d", t=NT), ACT.Copy)
                            else:
                                A(vn[:, 0, r, :], b[:, SEQ:SEQ + P], ACT.Copy)
                                ins = A(gates[:, 0, :], b[:, SEQ + P:SEQ + P + NG3], ACT.Sigmoid)
                        elif kind == "gate":
                            ins = A(gates[:, 1, :], b[:, P:P + NG3], ACT.Sigmoid)
                            ins = A(vn[:, 1, 1, :], b[:, 0:P], ACT.Copy)
                        elif kind == "H":
                            A(gk[0:64].rearrange("p g c -> p (g c)"), b[0:64, 0:2 * NC], ACT.Gelu_apprx_tanh)
                            ins = A(gv[64:P, :, :, 0:NC],
                                    b[64:P, 0:2 * NC].rearrange("p (g r c) -> p g r c", g=GROUPS, r=1)
                                    .broadcast_to([64, GROUPS, HPG, NC]), ACT.Gelu_apprx_tanh)
                        elif kind == "KC":
                            ins = A(kcd[:, :, 0:NC], b[:, 0:2 * NC].rearrange("p (g c) -> p g c", g=GROUPS), ACT.Copy)
                        elif kind in ("qr", "kr"):
                            ins = A(rraw[:, step[1]], pair, ACT.Copy)
                        elif kind == "vr":
                            ins = A(vr[:, step[2], step[1] * 512:(step[1] + 1) * 512], b[:], ACT.Copy)
                        elif kind == "gr":
                            ins = A(yb[:, step[2], step[1] * 512:(step[1] + 1) * 512], b[:], ACT.Silu)
                        elif kind == "ma":
                            ins = A(merged[:, 2 * step[1]:2 * step[1] + 2, :], pair, ACT.Sigmoid)
                        elif kind == "mb":
                            ins = A(gateb[:, 2 * step[1]:2 * step[1] + 2, :], pair, ACT.Sigmoid)
                        ins.then_inc(pj_done.sem, 1)
                    elif kind in ("xT", "x1T", "ybT"):
                        _, tile, c = step
                        i = TP_AT[step]
                        act.wait_ge(tp_ready.sem, tp_ready.at(l, i + 1))
                        dst = xT if kind == "x1T" else xhi_r
                        A(dst[:, 4 * c:4 * c + 4, tile * P:(tile + 1) * P], tp[i % 2][:].rearrange("p (b s) -> p b s", b=4),
                          ACT.Copy).then_inc(tp_done.sem, 1)
                    elif kind == "split":
                        n = step[1]
                        act.wait_ge(landed[n % MRAW].sem, landed[n % MRAW].at(l, 32 * (n // MRAW + 1)))
                        if n >= 2:
                            wait_chunk_used(act, l, n - 2)
                        floats, half = chunk_source(l, n)[1], step[2]
                        o = slice(half * floats // 2, (half + 1) * floats // 2)
                        A(ring_r[MRAW + n % 2][:, o], ring[n % MRAW][:, o], ACT.Copy).then_inc(hi_done.sem, 1)
                    elif kind == "yaS":
                        act.wait_ge(pv_done.sem, pv_done.at(l, PV_AT[("V", NH - 1)] + 1))
                        A(ya_hi_r, yaT, ACT.Copy).then_inc(ya_hi_done.sem, 1)
                    elif kind == "mS":
                        j = 2 * step[1]
                        act.wait_ge(sc_done.sem, sc_done.at(l, SC_AT[("wb", step[1])] + 1))
                        A(xT_r[:, j:j + 2, :], merged[:, j:j + 2, :], ACT.Copy).then_inc(m_hi_done.sem, 1)
                    elif kind == "CT":
                        i = TP_AT[step]
                        act.wait_ge(tp_ready.sem, tp_ready.at(l, i + 1))
                        A(pcT[:], tp[i % 2][:, 0:SEQ], ACT.Copy).then_inc(tp_done.sem, 1)
                    elif kind == "T":
                        for half, (o, n) in enumerate(((0, 512), (512, 256))):
                            i = TP_AT[step + (half,)]
                            act.wait_ge(tp_ready.sem, tp_ready.at(l, i + 1))
                            A(pT[:, o:o + n], tp[i % 2][:, 0:n], ACT.Copy).then_inc(tp_done.sem, 1)
                    elif kind == "CN":
                        act.wait_ge(soft_in.sem, soft_in.at(l, SOFT_AT[("CS",)] + 1))
                        A(scmp[:].rearrange("p n c -> p (n c)"), scmp[:].rearrange("p n c -> p (n c)"), ACT.Exp)\
                            .then_inc(exp_done.sem, 1)
                    elif kind == "N":
                        h = step[1]
                        act.wait_ge(soft_in.sem, soft_in.at(l, SOFT_AT[("S", h)] + 1))
                        s = scores[h % 2]
                        for j in range(4):
                            n = P if j < 2 else SEQ
                            o = (j % 2) * n + (0 if j < 2 else SEQ)
                            ins = A(s[:, o:o + n], s[:, o:o + n], ACT.Exp, bias=nmax[:, j:j + 1],
                                    accum_out=psum4[:, j:j + 1])
                        ins.then_inc(exp_done.sem, 1)
                    elif kind == "GN":
                        act.wait_ge(var_ready.sem, var_ready.at(l, 1))
                        A(sdev, vare, ACT.Sqrt).then_inc(sqrt_done.sem, 1)
                    elif kind == "LN1":
                        tile = step[1]
                        act.wait_ge(var_ready.sem, var_ready.at(l, 2 + tile))
                        A(sdev[:, tile:tile + 1], vare[:, tile:tile + 1], ACT.Sqrt).then_inc(sqrt_done.sem, 1)
                    elif kind == "route":
                        act.wait_ge(x_ready.sem, x_ready.at(l, 2))
                        A(acc.rearrange("p t d -> p (t d)"), x[:].rearrange("p t d -> p (t d)"), ACT.Copy, scale=ALPHA)
                        act.wait_ge(soft_in.sem, soft_in.at(l, SOFT_AT[("route",)] + 1))
                        A(rt[:, 0].rearrange("p t e -> p (t e)"), rt[:, 0].rearrange("p t e -> p (t e)"), ACT.Exp)\
                            .then_inc(exp_done.sem, 1)

                def take_gathered(c, x_no):
                    act.wait_ge(xg_ready.sem, xg_ready.after(x_no * 2 + 1 + c))
                    A(xg[:, 4 * c:4 * c + 4, :], pv[c][:].rearrange("p (k s) -> p k s", s=P), ACT.Copy).then_inc(xg_done.sem, 1)

                act.wait_ge(passes_ready.sem, passes_ready.at(l, 1))
                passes = act.value_load(passes_sb[0:1, 0:1], min_val=1, max_val=SEQ // SLOTS)
                with act.Fori(0, passes) as r:
                    x0 = act.snap(gathers_before + r * (PAIRS + 1))
                    g0 = act.snap(pairs_before + r * PAIRS)
                    take_gathered(0, x0)
                    take_gathered(1, x0)
                    with act.Fori(0, PAIRS) as pair:
                        g = act.snap(g0 + pair)
                        xn = act.snap(x0 + pair)
                        act.wait_ge(dt_ready.sem, dt_ready.after(g + 1))
                        A(dispwT, tp[1][:, 0:SEQ], ACT.Copy).then_inc(dt_done.sem, 1)
                        act.wait_ge(g_ready.sem, g_ready.after(g + 1))
                        A(hs, pj[0][:], ACT.Silu).then_inc(silu_done.sem, 1)
                        take_gathered(0, act.snap(xn + 1))
                        act.wait_ge(ht_ready.sem, ht_ready.after(g + 1))
                        A(hT.rearrange("p f s -> p (f s)"), tp[0][:], ACT.Copy).then_inc(ht_done.sem, 1)
                        take_gathered(1, act.snap(xn + 1))
                        for half in range(2):
                            act.wait_ge(y_ready.sem, y_ready.after(g * 2 + 1 + half))
                            A(ysb[:, half * 512:(half + 1) * 512], sc[half][:], ACT.Copy).then_inc(y_done.sem, 1)
                pairs_before = act.snap(pairs_before + passes * PAIRS)
                gathers_before = act.snap(gathers_before + passes * (PAIRS + 1))
                for tile in range(NT):
                    act.wait_ge(var_ready.sem, var_ready.at(l, 4 + tile))
                    A(sdev[:, tile:tile + 1], vare[:, tile:tile + 1], ACT.Sqrt).then_inc(sqrt_done.sem, 1)

        @block.vector
        def _(dve):
            v = dve
            steps_done = [0]
            dve.sem_inc(acc_done.sem, acc_done.credit)

            def then(ins):
                ins.then_inc(dve_step.sem, 1)
                steps_done[0] += 1
                dve.wait_ge(dve_step.sem, steps_done[0])

            def norm(l, which, src, tile):
                xt, st_, one = x[:, tile, :], src[:, tile, :], slice(tile, tile + 1)
                for c in range(2):
                    ins = v.bn_stats(lstats[:, tile, c, :], st_[:, c * 512:(c + 1) * 512])
                then(ins)
                then(v.bn_aggr(lmv[:, tile, :], lstats[:, tile].rearrange("p c n -> p (c n)")))
                v.tensor_scalar(vare[:, one], lmv[:, tile, 1:2], LN_EPS, None, ALU.add).then_inc(var_ready.sem, 1)
                v.wait_ge(lnw_in.sem, lnw_in.at(l, 32 * (which + 1)))
                v.scalar_tensor_tensor(out=xt, in0=st_, scalar=lmv[:, tile, 0:1], in1=lnw[:, 0, :], op0=ALU.subtract, op1=ALU.mult)
                v.wait_ge(sqrt_done.sem, sqrt_done.at(l, 2 * which + tile + 2))
                then(v.reciprocal(rstd[:, one], sdev[:, one]))
                v.scalar_tensor_tensor(out=xt, in0=xt, scalar=rstd[:, one], in1=lnw[:, 1, :], op0=ALU.mult, op1=ALU.add)\
                    .then_inc(x_ready.sem, 1)

            def route(l, b):
                lg, pr, sel, msk, o1, o2, tmp, both = (rt[:, i] for i in (0, 1, 2, 3, 4, 5, 11, 6))
                w = wpad[:, :, 0:NE]
                pair6 = rt[:, 7:10].rearrange("p a t e -> p (a t e)")[:, 0:48].rearrange("p (t g s) -> p t g s", t=NT, g=EG)
                g4 = rt[:, 10].rearrange("p t e -> p (t e)")
                gs, ge = (g4[:, i * 8:i * 8 + 8].rearrange("p (t g) -> p t g", t=NT) for i in range(2))
                s2 = g4[:, 16:18]
                s2b = g4[:, 18:20]
                wide = [P, NT, NE]

                def grp(a):
                    return a.rearrange("p t (g s) -> p t g s", g=EG)

                def b2(a):
                    return a.rearrange("p (t a) -> p t a", a=1).broadcast_to(wide)

                def b2g(a):
                    return a.rearrange("p (t a) -> p t a", a=1).broadcast_to([P, NT, EG])
                eidx = const[:, C_EIDX:C_EIDX + NE].rearrange("p (a e) -> p a e", a=1).broadcast_to(wide)
                gidx = const[:, C_GIDX:C_GIDX + EG].rearrange("p (a e) -> p a e", a=1).broadcast_to([P, NT, EG])
                rb = t["s_rb"].rearrange("p (a e) -> p a e", a=1).broadcast_to(wide)
                TT = v.tensor_tensor
                then(v.tensor_reduce(s2, b, AX.X, ALU.max))
                TT(lg, b, b2(s2), ALU.subtract).then_inc(soft_in.sem, 1)
                v.wait_ge(exp_done.sem, exp_done.at(l, len(EXP_AT)))
                then(v.tensor_reduce(s2, lg, AX.X, ALU.add))
                then(v.reciprocal(s2b, s2))
                then(TT(pr, lg, b2(s2b), ALU.mult))
                then(TT(sel, pr, rb, ALU.add))
                sg = grp(sel)
                TT(pair6[:, :, :, 0:3], sg[:, :, :, 0:3], sg[:, :, :, 1:4], ALU.add)
                TT(pair6[:, :, :, 3:5], sg[:, :, :, 0:2], sg[:, :, :, 2:4], ALU.add)
                then(TT(pair6[:, :, :, 5:6], sg[:, :, :, 0:1], sg[:, :, :, 3:4], ALU.add))
                then(v.tensor_reduce(gs, pair6, AX.X, ALU.max))
                then(v.tensor_reduce(s2, gs, AX.X, ALU.max))
                then(TT(ge, gs, b2g(s2), ALU.is_equal))
                then(TT(gs, ge, gidx, ALU.mult))
                then(v.tensor_reduce(s2, gs, AX.X, ALU.max))
                then(TT(ge, gs, b2g(s2), ALU.is_equal))
                ins = v.tensor_scalar(grp(msk), ge.rearrange("p t (g s) -> p t g s", s=1).broadcast_to([P, NT, EG, EG]),
                                      -MASKED, MASKED, ALU.mult, ALU.add)
                then(ins)
                then(TT(msk, msk, sel, ALU.add))
                for pick in (o1, o2):
                    then(v.tensor_reduce(s2, msk, AX.X, ALU.max))
                    then(TT(tmp, msk, b2(s2), ALU.is_equal))
                    then(TT(tmp, tmp, eidx, ALU.mult))
                    then(v.tensor_reduce(s2, tmp, AX.X, ALU.max))
                    then(TT(pick, tmp, b2(s2), ALU.is_equal))
                    if pick is o1:
                        then(v.scalar_tensor_tensor(out=msk, in0=o1, scalar=3 * MASKED, in1=msk, op0=ALU.mult, op1=ALU.add))
                TT(both, o1, o2, ALU.add).then_inc(oh_ready.sem, 1)
                v.wait_ge(oh_ready.sem, oh_ready.at(l, 1))
                then(TT(tmp, both, pr, ALU.mult))
                then(v.tensor_reduce(s2, tmp, AX.X, ALU.add))
                then(v.reciprocal(s2b, s2))
                then(TT(w, tmp, b2(s2b), ALU.mult))

            def bias_sums():
                dve.wait_ge(setup_mm.sem, 1)
                v.tensor_tensor(t["s_rows"], sc[0][0:NH, 0:REV], t["s_neg"], ALU.add).then_inc(setup_rows.sem, 1)
                dve.wait_ge(setup_mm.sem, 2)
                cadd = const[:, C_CADD:C_CADD + NT * CP].rearrange("p (t a c) -> p t a c", t=NT, a=1)
                v.tensor_tensor(bcmp[:], sc[1][:, 0:NT * NH * CP].rearrange("p (t c h) -> p t h c", t=NT, c=CP),
                                cadd.broadcast_to([P, NT, NH, CP]), ALU.add).then_inc(setup_bc.sem, 1)

            cmul = const[:, C_CMUL:C_CMUL + NT * CP].rearrange("p (t a c) -> p t a c", t=NT, a=1)
            pairs_before = gathers_before = passes_before = 0
            for l in range(DEPTH):
                for step in STEPS:
                    kind = step[0]
                    if step in SC_AT:
                        i = SC_AT[step]
                        b = sc[i % 2]
                        v.wait_ge(sc_ready.sem, sc_ready.at(l, i + 1))
                    if kind in ("xT", "ybT"):
                        _, tile, c = step
                        i = TP_AT[step]
                        part = (slice(None), slice(4 * c, 4 * c + 4), slice(tile * P, (tile + 1) * P))
                        v.wait_ge(tp_done.sem, tp_done.at(l, i + 1))
                        v.tensor_tensor((xT_r if kind == "xT" else ybT_r)[part], tp[i % 2][:].rearrange("p (b s) -> p b s", b=4),
                                        xhi_r[part].bitcast(F32), ALU.subtract).then_inc(lo_done.sem, 1)
                        if l == 0 and step == ("xT", NT - 1, 1):
                            bias_sums()
                    elif kind == "split":
                        n = step[1]
                        floats, half = chunk_source(l, n)[1], step[2]
                        o = slice(half * floats // 2, (half + 1) * floats // 2)
                        v.wait_ge(hi_done.sem, hi_done.at(l, 2 * n + half + 1))
                        raw = ring[n % MRAW][:, o]
                        v.tensor_tensor(ring_r[n % MRAW][:, o], raw, ring_r[MRAW + n % 2][:, o].bitcast(F32), ALU.subtract)\
                            .then_inc(split_done.sem, 1)
                    elif kind == "yaS":
                        v.wait_ge(ya_hi_done.sem, ya_hi_done.at(l, 1))
                        v.tensor_tensor(yaT_r, yaT, ya_hi_r.bitcast(F32), ALU.subtract).then_inc(ya_lo_done.sem, 1)
                    elif kind == "mS":
                        j = 2 * step[1]
                        v.wait_ge(m_hi_done.sem, m_hi_done.at(l, step[1] + 1))
                        m = merged[:, j:j + 2, :]
                        v.tensor_tensor(merged_r[:, j:j + 2, :], m, xT_r[:, j:j + 2, :].bitcast(F32), ALU.subtract).then_inc(m_lo_done.sem, 1)
                    elif kind == "win":
                        v.wait_ge(pj_done.sem, pj_done.at(l, PJ_AT[("kcvc",)] + 1))
                        v.wait_ge(cw_in.sem, cw_in.at(l, 96))
                        for a in range(2):
                            for g in range(GROUPS):
                                src = bass.AP(kv2.tensor, kv2[:, a, g, 0:1].offset,
                                              [list(kv2.ap[0]), [2, L2], [NSTRIDE, NC]])
                                ins = v.tensor_tensor(win[:, a, :, g, :], src,
                                                      pos[:, a, :].rearrange("p (l c) -> p l c", c=1).broadcast_to([P, L2, NC]), ALU.add)
                        ins.then_inc(win_ready.sem, 1)
                    elif kind == "VC":
                        blk = const[:, C_BLK:C_BLK + NH].rearrange("p (h d) -> p h d", d=1).broadcast_to([P, NH, HD])
                        v.tensor_tensor(vcz[:], b[:, 0:HD].rearrange("p (h d) -> p h d", h=1).broadcast_to([P, NH, HD]), blk,
                                        ALU.mult).then_inc(sc_done.sem, 1)
                    elif kind == "CS":
                        v.tensor_tensor(scmp[:].rearrange("p n c -> p (n c)"), b[:, 0:NT * NH * CP],
                                        bcmp[:].rearrange("p t h c -> p (t h c)"), ALU.add).then_inc(sc_done.sem, 1)
                        v.wait_ge(sc_done.sem, sc_done.at(l, i + 1))
                        then(v.tensor_reduce(cmax, scmp[:], AX.X, ALU.max))
                        v.tensor_tensor(scmp[:], scmp[:], cmax.rearrange("p (n c) -> p n c", c=1).broadcast_to([P, NT * NH, CP]),
                                        ALU.subtract).then_inc(soft_in.sem, 1)
                    elif kind == "CN":
                        v.wait_ge(exp_done.sem, exp_done.at(l, EXP_AT[("CN",)] + 1))
                        sview = scmp[:].rearrange("p (t h) c -> p t h c", t=NT)
                        then(v.tensor_tensor(sview, sview, cmul.broadcast_to([P, NT, NH, CP]), ALU.mult))
                        then(v.tensor_reduce(csum, scmp[:], AX.X, ALU.add))
                        then(v.tensor_scalar(csum, csum, 1e-30, None, ALU.max))
                        then(v.reciprocal(crec, csum))
                        v.wait_ge(pj_done.sem, pj_done.at(l, PJ_AT[("gate",)] + 1))
                        then(v.tensor_tensor(crec.rearrange("p (t h) -> p t h", t=NT), crec.rearrange("p (t h) -> p t h", t=NT),
                                             gates[:, :, 0:NG3:3], ALU.mult))
                        v.tensor_tensor(scmp[:], scmp[:], crec.rearrange("p (n c) -> p n c", c=1).broadcast_to([P, NT * NH, CP]),
                                        ALU.mult).then_inc(p_ready.sem, 1)
                    elif kind == "S":
                        h = step[1]
                        s = scores[h % 2]
                        if h == 0:
                            v.wait_ge(toep_in.sem, toep_in.at(l, 16))
                        for qt in range(NT):
                            i = SC_AT[step + (qt,)]
                            n = (qt + 1) * P
                            o = qt * SEQ
                            v.wait_ge(sc_ready.sem, sc_ready.at(l, i + 1))
                            v.tensor_tensor(s[:, o:o + 2 * n].rearrange("p (r k) -> p r k", r=2),
                                            sc[i % 2][:, 0:2 * n].rearrange("p (r k) -> p r k", r=2),
                                            bias[:, h:h + 1, SEQ - n:SEQ].broadcast_to([P, 2, n]), ALU.add).then_inc(sc_done.sem, 1)
                        v.wait_ge(sc_done.sem, sc_done.at(l, i))
                        v.tensor_reduce(nmax[:, 0:2], s[:, 0:SEQ].rearrange("p (r k) -> p r k", r=2), AX.X, ALU.max, negate=True)
                        v.wait_ge(sc_done.sem, sc_done.at(l, i + 1))
                        v.tensor_reduce(nmax[:, 2:4], s[:, SEQ:3 * SEQ].rearrange("p (r k) -> p r k", r=2), AX.X, ALU.max,
                                        negate=True).then_inc(soft_in.sem, 1)
                    elif kind == "N":
                        h = step[1]
                        v.wait_ge(exp_done.sem, exp_done.at(l, EXP_AT[step] + 1))
                        then(v.reciprocal(r4, psum4))
                        r22 = r4.rearrange("p (t r) -> p t r", t=NT)
                        then(v.tensor_tensor(r22, r22, gates[:, :, 3 * h + 1:3 * h + 3], ALU.mult))
                        for qt in range(NT):
                            n = (qt + 1) * P
                            s = scores[h % 2][:, qt * SEQ:qt * SEQ + 2 * n].rearrange("p (r k) -> p r k", r=2)
                            ins = v.tensor_tensor(s, s, r4[:, 2 * qt:2 * qt + 2].rearrange("p (r k) -> p r k", k=1).broadcast_to([P, 2, n]),
                                                  ALU.mult)
                        ins.then_inc(p_ready.sem, 1)
                    elif kind == "V" and step[1] % 2:
                        i = PV_AT[step]
                        v.wait_ge(pv_ready.sem, pv_ready.at(l, i + 1))
                        v.tensor_copy(yaT[:, step[1] // 2, :], pv[i % 2][:, 0:SEQ]).then_inc(pv_done.sem, 1)
                    elif kind == "rot":
                        r = step[1]
                        half = [P, 2, SEQ]
                        sinb = sinT.rearrange("p (b s) -> p b s", b=1).broadcast_to(half)
                        cosb = cosT.rearrange("p (b s) -> p b s", b=1).broadcast_to(half)
                        v.tensor_tensor(rtmp, b[:].rearrange("p (b s) -> p b s", b=2), sinb, ALU.mult)
                        then(v.tensor_tensor(rsum, rraw[:, r % 2], cosb, ALU.mult))
                        if r < 2:
                            v.wait_ge(zeroed.sem, zeroed.at(l, 4))
                            v.tensor_tensor(qrz[0:64, 4 * r:4 * r + 4:2, :], rtmp[0:64], rsum[0:64], ALU.add)
                            v.tensor_tensor(qrz[64:P, 4 * r + 1:4 * r + 4:2, :], rtmp[64:P], rsum[64:P], ALU.add)\
                                .then_inc(sc_done.sem, 1)
                        else:
                            v.tensor_tensor(krT[:, 2 * (r - 2):2 * (r - 2) + 2, :], rtmp, rsum, ALU.add).then_inc(sc_done.sem, 1)
                        v.wait_ge(sc_done.sem, sc_done.at(l, i + 1))
                    elif kind == "ST":
                        h = step[1]
                        if h >= 2:
                            v.wait_ge(pv_ready.sem, pv_ready.at(l, PV_AT[("Y", h - 2)] + 1))
                        if h == 0:
                            v.wait_ge(decay_in.sem, decay_in.at(l, 16))
                        s = st[:, h % 2, :]
                        v.tensor_tensor(s[:, 0:SEQ], b[:, 0:SEQ], decay[:, h, :], ALU.mult)
                        v.tensor_tensor(s[:, SEQ:SEQ + P], b[:, SEQ:SEQ + P], decay[:, h, 0:P], ALU.mult).then_inc(sc_done.sem, 1)
                    elif kind == "Y":
                        h = step[1]
                        i = PV_AT[step]
                        v.wait_ge(pv_ready.sem, pv_ready.at(l, i + 1))
                        v.tensor_copy(yraw[:, :, h * P:(h + 1) * P], pv[i % 2][:, 0:SEQ].rearrange("p (t d) -> p t d", t=NT))\
                            .then_inc(pv_done.sem, 1)
                        v.wait_ge(pv_done.sem, pv_done.at(l, i + 1))
                        for tile in range(NT):
                            ins = v.bn_stats(stats[:, tile, h, :], yraw[:, tile, h * P:(h + 1) * P])
                        if h == NH - 1:
                            then(ins)
                    elif kind == "GN":
                        for tile in range(NT):
                            for h in range(NH):
                                ins = v.bn_aggr(mv[:, tile, h, :], stats[:, tile, h, :])
                        then(ins)
                        v.tensor_scalar(vare.rearrange("p (t h) -> p t h", t=NT), mv[:, :, :, 1], LN_EPS, None, ALU.add)\
                            .then_inc(var_ready.sem, 1)
                        v.wait_ge(sqrt_done.sem, sqrt_done.at(l, 1))
                        then(v.reciprocal(rstd, sdev))
                        for tile in range(NT):
                            for h in range(NH):
                                y = yraw[:, tile, h * P:(h + 1) * P]
                                ins = v.tensor_scalar(y, y, mv[:, tile, h, 0:1], rstd[:, tile * NH + h:tile * NH + h + 1],
                                                      ALU.subtract, ALU.mult)
                        then(ins)
                        v.wait_ge(pj_done.sem, pj_done.at(l, PJ_AT[("gr", 1, 1)] + 1))
                        for tile in range(NT):
                            ins = v.tensor_tensor(yb[:, tile, :], yb[:, tile, :], yraw[:, tile, :], ALU.mult)
                        ins.then_inc(yb_ready.sem, 1)
                    elif kind in ("wa", "wb"):
                        j = step[1]
                        m = merged[:, 2 * j:2 * j + 2, :]
                        product = b[:].rearrange("p (b s) -> p b s", b=2)
                        if kind == "wa":
                            v.wait_ge(pj_done.sem, pj_done.at(l, PJ_AT[("ma", j)] + 1))
                            v.tensor_tensor(m, product, m, ALU.mult).then_inc(sc_done.sem, 1)
                        else:
                            v.wait_ge(pj_done.sem, pj_done.at(l, PJ_AT[("mb", j)] + 1))
                            g = gateb[:, 2 * j:2 * j + 2, :]
                            then(v.tensor_tensor(g, product, g, ALU.mult))
                            v.tensor_tensor(m, m, g, ALU.add).then_inc(sc_done.sem, 1)
                    elif kind == "wo":
                        _, c, tile = step
                        xs = x[:, tile, c * 512:(c + 1) * 512]
                        v.scalar_tensor_tensor(out=xs, in0=xs, scalar=ALPHA, in1=b[:], op0=ALU.mult, op1=ALU.add)\
                            .then_inc(sc_done.sem, 1)
                    elif kind == "LN1":
                        v.wait_ge(sc_done.sem, sc_done.at(l, SC_AT[("wo", 1, step[1])] + 1))
                        norm(l, 0, x, step[1])
                    elif kind == "R":
                        v.tensor_copy(rt[:, 6, step[1], :], b[:, 0:NE]).then_inc(sc_done.sem, 1)
                    elif kind == "route":
                        v.wait_ge(sc_done.sem, sc_done.at(l, SC_AT[("R", NT - 1)] + 1))
                        route(l, rt[:, 6])
                    elif kind == "K":
                        both = rt[:, 6]
                        rank = b[:, 0:NT * NE].rearrange("p (t e) -> p t e", t=NT)
                        if l == 0:
                            v.memset(key[:, :, NE:NE + 2], -1.0)
                            v.memset(wpad[:, :, NE:NE + 2], 0.0)
                        ks = key[:, :, 0:NE]
                        then(v.scalar_tensor_tensor(out=ks, in0=rank, scalar=1.0, in1=both, op0=ALU.add, op1=ALU.mult))
                        v.tensor_scalar(ks, ks, -1.0, None, ALU.add)
                        most, over = npf[:, 0:1], npf[:, 1:4]
                        then(v.tensor_reduce(most, b[:, 2 * NE:3 * NE], AX.X, ALU.max))
                        for i in range(3):
                            ins = v.tensor_scalar(over[:, i:i + 1], most, float(SLOTS * (i + 1)), None, ALU.is_gt)
                        then(ins)
                        then(v.tensor_reduce(most, over, AX.X, ALU.add))
                        then(v.tensor_scalar(passes_sb[:], most, 1.0, None, ALU.add))
                        v.sem_inc(passes_ready.sem, 1)
                        v.sem_inc(sc_done.sem, 1)

                def dispatch(pair, x_no, g):
                    wide = [P, NT, 2, SLOTS]
                    iota = const[:, C_IOTA:C_IOTA + SLOTS].rearrange("p (t e s) -> p t e s", t=1, e=1).broadcast_to(wide)
                    cols = bass.ds(pair * 2, 2)
                    v.wait_ge(xg_ready.sem, xg_ready.after(x_no * 2))
                    v.wait_ge(dt_ready.sem, dt_ready.after(g))
                    v.sem_inc(dve_paced.sem, 1)
                    v.tensor_tensor(disp, iota, key[:, :, cols].rearrange("p t (e s) -> p t e s", s=1).broadcast_to(wide), ALU.is_equal)\
                        .then_inc(disp_made.sem, 1)
                    v.wait_ge(disp_made.sem, disp_made.after(x_no + 1))
                    v.sem_inc(dve_paced.sem, 1)
                    v.tensor_tensor(dispw, disp, wpad[:, :, cols].rearrange("p t (e s) -> p t e s", s=1).broadcast_to(wide), ALU.mult)\
                        .then_inc(disp_ready.sem, 1)

                v.wait_ge(passes_ready.sem, passes_ready.at(l, 1))
                passes = v.value_load(passes_sb[0:1, 0:1], min_val=1, max_val=SEQ // SLOTS)
                with dve.Fori(0, passes) as r:
                    x0 = v.snap(gathers_before + r * (PAIRS + 1))
                    g0 = v.snap(pairs_before + r * PAIRS)
                    dispatch(0, x0, g0)
                    with dve.Fori(0, PAIRS) as pair:
                        g = v.snap(g0 + pair)
                        dispatch(v.snap(pair + 1), v.snap(x0 + pair + 1), v.snap(g + 1))
                        v.wait_ge(u_ready.sem, u_ready.after(g + 1))
                        v.wait_ge(silu_done.sem, silu_done.after(g + 1))
                        v.sem_inc(dve_paced.sem, 1)
                        v.tensor_tensor(hh, hs, pj[1][:], ALU.mult).then_inc(h_ready.sem, 1)
                        for half in range(2):
                            for tile in range(NT):
                                i = 2 * half + tile
                                v.wait_ge(c_ready.sem, c_ready.after(g * 4 + 1 + i))
                                v.wait_ge(acc_done.sem, acc_done.after(g * 4 - 3 + i))
                                v.sem_inc(dve_paced.sem, 1)
                                xs = acc[:, tile, half * 512:(half + 1) * 512]
                                v.tensor_tensor(xs, xs, (pj, pv)[half][tile][:], ALU.add).then_inc(acc_done.sem, 1)
                    v.wait_ge(disp_ready.sem, disp_ready.after(x0 + PAIRS + 1))
                    v.sem_inc(dve_paced.sem, 1)
                    v.tensor_scalar(key[:], key[:], -float(SLOTS), None, ALU.add).then_inc(key_moved.sem, 1)
                    v.wait_ge(key_moved.sem, key_moved.after(v.snap(passes_before + r) + 1))
                    v.sem_inc(dve_paced.sem, 1)
                passes_before = v.snap(passes_before + passes)
                pairs_before = v.snap(pairs_before + passes * PAIRS)
                gathers_before = v.snap(gathers_before + passes * (PAIRS + 1))
                v.wait_ge(acc_done.sem, acc_done.after(pairs_before * 4))
                v.sem_inc(dve_paced.sem, 1)
                for tile in range(NT):
                    norm(l, 1, acc, tile)


def _constants():
    import numpy as np
    f = np.float32

    def bucket(n):
        n = np.maximum(n, 0)
        nf = np.maximum(n, 1).astype(f)
        large = 16 + (np.log(nf / f(16)) / f(np.log(2048 / 16)) * f(16)).astype(np.int32)
        return np.where(n < 16, n, np.minimum(large, 31))

    def onehot(dist):
        return (bucket(dist)[None, :] == np.arange(32)[:, None]).astype(f)
    pack = np.zeros((P, NCONST), f)
    pack[:, C_ID:C_ID + P] = np.eye(P)
    swap = np.zeros((P, P), f)
    for d in range(P):
        if d % 64 < 32:
            swap[d + 32, d] = -1.0
        else:
            swap[d - 32, d] = 1.0
    pack[:, C_SWAP:C_SWAP + P] = swap
    inv = (f(10000.0) ** (-np.arange(32, dtype=f) * f(2.0) / f(64))).astype(f)
    ang = (np.arange(SEQ, dtype=f)[None, :] * inv[:, None]).astype(f)
    pack[:, C_COS:C_COS + SEQ] = np.tile(np.cos(ang), (4, 1))
    pack[:, C_SIN:C_SIN + SEQ] = np.tile(np.sin(ang), (4, 1))
    tok = (np.arange(NT)[None, :, None] * P + np.arange(P)[:, None, None])
    end = np.arange(CP)[None, None, :] * NSTRIDE + NLEN - 1
    ok = (end <= tok) & (np.arange(CP)[None, None, :] < NC)
    pack[:, C_CADD:C_CADD + 32] = np.where(ok, 0, MASKED).reshape(P, 32)
    pack[:, C_CMUL:C_CMUL + 32] = ok.astype(f).reshape(P, 32)
    pack[:, C_BLK:C_BLK + NH] = (np.arange(P)[:, None] // CP == np.arange(NH)[None, :])
    pack[:, C_EIDX:C_EIDX + NE] = NE - np.arange(NE)
    pack[:, C_GIDX:C_GIDX + EG] = EG - np.arange(EG)
    pack[:, C_TRI:C_TRI + P] = np.triu(np.ones((P, P)), 1)
    pack[:, C_ONES:C_ONES + P] = 1.0
    pack[:, C_IOTA:C_IOTA + SLOTS] = np.arange(SLOTS)
    lg = np.log(1.0 - 2.0 ** (-5.0 - np.arange(NH)))
    diff = np.arange(SEQ)[None, :] - np.arange(P)[:, None]
    decay = np.where(diff[:, None, :] >= 0, np.exp(np.maximum(diff, 0)[:, None, :] * lg[None, :, None]), 0.0) * HD ** -0.5
    neg = np.where(np.arange(REV) > SEQ - 1, MASKED, 0.0)
    return {
        "c_pack": pack, "c_decay": decay.astype(f), "c_neg": np.tile(neg, (NH, 1)).astype(f),
        "c_rev": onehot(SEQ - 1 - np.arange(REV)), "c_fwd": np.concatenate([onehot(np.arange(FWD) - FWD0 - NSTRIDE * j) for j in range(4)]),
    }


def launch_program(nc, t):
    build(nc, t)


_INS = ["x", "w_in", "cmp_pos", "cmp_w1", "cmp_w2", "w_br_a", "w_br_b", "w_o", "ln1_g", "ln1_b",
        "w_router", "router_bias", "moe_w_gate", "moe_w_up", "moe_w_down", "ln2_g", "ln2_b", "rel_bias"]


def kernel(**inputs):
    import numpy as np
    import concourse.bacc as bacc
    from concourse import mybir as mb
    from concourse.bass_utils import run_bass_kernel_spmd as run

    nc = bacc.Bacc("TRN2", target_bir_lowering=False, num_devices=1)
    arrays, t = {}, {}
    given = {name: np.ascontiguousarray(inputs[name]) for name in _INS}
    given.update(_constants())
    given["cmp_pos"] = np.ascontiguousarray(given["cmp_pos"].reshape(DEPTH, 2, L2, 2 * HD).transpose(0, 1, 3, 2))
    for name, a in given.items():
        arrays[f"in_{name}"] = a
        t[name] = nc.dram_tensor(f"in_{name}", a.shape, mb.dt.from_np(a.dtype), kind="ExternalInput").ap()
    t["out"] = nc.dram_tensor("out_0", (1, SEQ, D), mb.dt.float32, kind="ExternalOutput").ap()
    launch_program(nc, t)
    r = run(nc, [arrays], core_ids=[0])
    return r.results[0]["out_0"]
```
